# Optimizing a Trainium2 kernel written in Bass

```python
import jax, jax.numpy as jnp
from jax import lax
import numpy as np

D_MODEL = 1024
BATCH = 1
SEQ = 256
DEPTH = 2
DEC_BATCH = 8
DEC_SEQ = 1
PAST_LEN = 1024
PAGE_SIZE = 128

N_A_LAYERS = DEPTH // 2
N_B_LAYERS = DEPTH - N_A_LAYERS
D_PLE = 256
D_FF = 2816
EPS = 1e-6
SSM_EXPAND = 2
D_INNER = SSM_EXPAND * D_MODEL
SSM_HEAD_DIM = 64
SSM_HEADS = D_INNER // SSM_HEAD_DIM
SSM_GROUPS = 8
HEADS_PER_GROUP = SSM_HEADS // SSM_GROUPS
D_STATE = 128
CONV_W = 4
CONV_DIM = D_INNER + 2 * SSM_GROUPS * D_STATE
SSD_CHUNK = 128
ATT_HEAD_DIM = 64
ATT_HEADS = D_MODEL // ATT_HEAD_DIM
ATT_KV_HEADS = 4
ATT_GROUP = ATT_HEADS // ATT_KV_HEADS
WINDOW = 128
Q_BLOCK = 128
ROPE_THETA = 10000.0

kernel_name = "yoco_mamba2_swa_sink_macaron_decoder_step"

F32 = jnp.float32

def rmsnorm(x, g):
    xf = x.astype(F32)
    y = xf * lax.rsqrt(jnp.mean(xf * xf, axis=-1, keepdims=True) + EPS)
    return (y * g.astype(F32)).astype(x.dtype)

def swiglu(x, wi, wo):
    gt, up = jnp.split(x @ wi, 2, axis=-1)
    return (jax.nn.silu(gt) * up) @ wo

def rope(x, pos):
    half = x.shape[-1] // 2
    inv = ROPE_THETA ** (-jnp.arange(half, dtype=F32) / half)
    ang = pos.astype(F32)[:, None] * inv[None, :]
    cos = jnp.cos(ang)[None, :, None, :]
    sin = jnp.sin(ang)[None, :, None, :]
    xf = x.astype(F32)
    x1, x2 = xf[..., :half], xf[..., half:]
    return jnp.concatenate([x1 * cos - x2 * sin, x2 * cos + x1 * sin], axis=-1).astype(x.dtype)

def ssd_scan(x, dt, a, bm, cm, h0):
    bsz, t_len = x.shape[:2]
    L = min(SSD_CHUNK, t_len)
    t_pad = -(-t_len // L) * L
    pad = t_pad - t_len
    if pad:
        def pw(arr):
            return jnp.pad(arr, [(0, 0), (0, pad)] + [(0, 0)] * (arr.ndim - 2))
        x, dt, bm, cm = pw(x), pw(dt), pw(bm), pw(cm)
    nc = t_pad // L
    G, E, P, N = SSM_GROUPS, HEADS_PER_GROUP, SSM_HEAD_DIM, D_STATE
    xf = x.astype(F32).reshape(bsz, nc, L, G, E, P)
    dtc = dt.astype(F32).reshape(bsz, nc, L, G, E)
    bc = bm.astype(F32).reshape(bsz, nc, L, G, N)
    cc = cm.astype(F32).reshape(bsz, nc, L, G, N)
    xdt = xf * dtc[..., None]
    cum = jnp.cumsum(dtc * a.reshape(G, E), axis=2)
    cum_t = jnp.moveaxis(cum, 2, -1)
    causal = jnp.tril(jnp.ones((L, L), dtype=bool))
    seg = cum_t[..., :, None] - cum_t[..., None, :]
    decay = jnp.exp(jnp.where(causal, seg, -jnp.inf))
    cb = jnp.einsum('bclgn,bcsgn->bcgls', cc, bc)
    y_intra = jnp.einsum('bcgels,bcsgep->bclgep', cb[:, :, :, None] * decay, xdt)
    cum_last = cum[:, :, -1]
    to_end = jnp.exp(cum_last[:, :, None] - cum)
    s_chunk = jnp.einsum('bclgn,bclgep->bcgepn', bc, xdt * to_end[..., None])

    def step(h, inp):
        s_c, dec_c = inp
        return h * dec_c[..., None, None] + s_c, h

    h_init = h0.astype(F32).reshape(bsz, G, E, P, N)
    h_last, h_in = lax.scan(step, h_init, (jnp.moveaxis(s_chunk, 1, 0), jnp.moveaxis(jnp.exp(cum_last), 1, 0)))
    h_in = jnp.moveaxis(h_in, 0, 1)
    y_inter = jnp.einsum('bclgn,bcgepn->bclgep', cc, h_in) * jnp.exp(cum)[..., None]
    y = (y_intra + y_inter).reshape(bsz, t_pad, SSM_HEADS, P)[:, :t_len]
    return y, h_last.reshape(bsz, SSM_HEADS, P, N)

def mamba2_mixer(u, w_in, conv_w, conv_b, dt_bias, a_log, d_skip, norm_g, w_out, ssm0, conv0):
    bsz, t_len, _ = u.shape
    z, xbc, dt_raw = jnp.split(u @ w_in, [D_INNER, D_INNER + CONV_DIM], axis=-1)
    xbc_full = jnp.concatenate([conv0.astype(xbc.dtype), xbc], axis=1)
    conv = conv_b + sum(xbc_full[:, k:k + t_len] * conv_w[k] for k in range(CONV_W))
    xbc_act = jax.nn.silu(conv)
    xs, bm, cm = jnp.split(xbc_act, [D_INNER, D_INNER + SSM_GROUPS * D_STATE], axis=-1)
    xs = xs.reshape(bsz, t_len, SSM_HEADS, SSM_HEAD_DIM)
    bm = bm.reshape(bsz, t_len, SSM_GROUPS, D_STATE)
    cm = cm.reshape(bsz, t_len, SSM_GROUPS, D_STATE)
    dt = jax.nn.softplus(dt_raw.astype(F32) + dt_bias.astype(F32))
    a = -jnp.exp(a_log.astype(F32))
    y, h_last = ssd_scan(xs, dt, a, bm, cm, ssm0)
    y = y + d_skip.astype(F32)[:, None] * xs.astype(F32)
    gated = y.reshape(bsz, t_len, D_INNER) * jax.nn.silu(z.astype(F32))
    gg = gated.reshape(bsz, t_len, SSM_GROUPS, D_INNER // SSM_GROUPS)
    gg = gg * lax.rsqrt(jnp.mean(gg * gg, axis=-1, keepdims=True) + EPS)
    out = (gg.reshape(bsz, t_len, D_INNER) * norm_g.astype(F32)).astype(u.dtype) @ w_out
    return out, h_last.astype(ssm0.dtype), xbc_full[:, -(CONV_W - 1):].astype(conv0.dtype)

def shared_kv(x, kv_norm, w_kv, k_norm, pos):
    bsz, t_len, _ = x.shape
    k, v = jnp.split(rmsnorm(x, kv_norm) @ w_kv, 2, axis=-1)
    k = k.reshape(bsz, t_len, ATT_KV_HEADS, ATT_HEAD_DIM)
    v = v.reshape(bsz, t_len, ATT_KV_HEADS, ATT_HEAD_DIM)
    return rope(rmsnorm(k, k_norm), pos), v

def window_attention(q, k_all, v_all, hist_valid, sinks):
    bsz, t_len = q.shape[:2]
    qb = Q_BLOCK if t_len % Q_BLOCK == 0 else t_len
    nb = t_len // qb
    kspan = qb + WINDOW
    starts = jnp.arange(nb) * qb
    kidx = starts[:, None] + jnp.arange(kspan)[None, :]
    tq = starts[:, None] + jnp.arange(qb)[None, :]
    kb = jnp.take(k_all, kidx, axis=1)
    vb = jnp.take(v_all, kidx, axis=1)
    qg = q.reshape(bsz, nb, qb, ATT_KV_HEADS, ATT_GROUP, ATT_HEAD_DIM)
    s = jnp.einsum('bnqkgd,bnskd->bnkgqs', qg, kb).astype(F32) * (ATT_HEAD_DIM ** -0.5)
    rel = (WINDOW + tq)[:, :, None] - kidx[:, None, :]
    mask = (rel >= 0) & (rel <= WINDOW)
    if not hist_valid:
        mask = mask & (kidx[:, None, :] >= WINDOW)
    s = jnp.where(mask[None, :, None, None], s, -jnp.inf)
    sink = jnp.broadcast_to(sinks.astype(F32).reshape(ATT_KV_HEADS, ATT_GROUP)[None, None, :, :, None, None], s.shape[:-1] + (1,))
    prob = jax.nn.softmax(jnp.concatenate([s, sink], axis=-1), axis=-1)[..., :-1]
    o = jnp.einsum('bnkgqs,bnskd->bnqkgd', prob.astype(vb.dtype), vb)
    return o.reshape(bsz, t_len, ATT_HEADS * ATT_HEAD_DIM)

def trunk(x, p, ssm0, conv0, k_hist, v_hist, pos0, hist_valid, w):
    bsz, t_len, _ = x.shape
    pos = pos0 + jnp.arange(t_len)
    new_ssm, new_conv = [], []
    k_all = v_all = None
    for i in range(DEPTH):
        x = x + 0.5 * swiglu(rmsnorm(x, w['ffn1_norm'][i]), w['ffn1_wi'][i], w['ffn1_wo'][i])
        h = rmsnorm(x, w['mix_norm'][i])
        if i < N_A_LAYERS:
            out, h_last, c_last = mamba2_mixer(h, w['ssm_in'][i], w['ssm_conv_w'][i], w['ssm_conv_b'][i], w['ssm_dt_bias'][i], w['ssm_a_log'][i], w['ssm_d'][i], w['ssm_norm'][i], w['ssm_out'][i], ssm0[i], conv0[i])
            new_ssm.append(h_last)
            new_conv.append(c_last)
        else:
            j = i - N_A_LAYERS
            q = (h @ w['w_q'][j]).reshape(bsz, t_len, ATT_HEADS, ATT_HEAD_DIM)
            q = rope(rmsnorm(q, w['q_norm'][j]), pos)
            out = window_attention(q, k_all, v_all, hist_valid, w['attn_sinks'][j]) @ w['w_o'][j]
        x = x + out
        x = x + 0.5 * swiglu(rmsnorm(x, w['ffn2_norm'][i]), w['ffn2_wi'][i], w['ffn2_wo'][i])
        gate = jax.nn.sigmoid(rmsnorm(x, w['ple_norm'][i]) @ w['ple_gate'][i])
        x = x + gate * (p[i] @ w['ple_proj'][i])
        if i == N_A_LAYERS - 1:
            k_new, v_new = shared_kv(x, w['kv_norm'], w['w_kv'], w['k_norm'], pos)
            k_all = jnp.concatenate([k_hist.astype(k_new.dtype), k_new], axis=1)
            v_all = jnp.concatenate([v_hist.astype(v_new.dtype), v_new], axis=1)
    return x, jnp.stack(new_ssm), jnp.stack(new_conv), k_all[:, -WINDOW:], v_all[:, -WINDOW:]

def setup_inputs(seed: int = 0) -> dict:
    key = jax.random.key(seed)
    ks = list(jax.random.split(key, 48))
    cnt = [0]

    def nk():
        cnt[0] += 1
        return ks[cnt[0] - 1]

    def nrm(shape, scale):
        return scale * jax.random.normal(nk(), shape, F32)

    def gain(shape):
        return 1.0 + nrm(shape, 0.02)

    dt0 = jnp.exp(jax.random.uniform(nk(), (N_A_LAYERS, SSM_HEADS), F32, np.log(1e-3), np.log(1e-1)))
    d = {
        'x_prompt': nrm((BATCH, SEQ, D_MODEL), 1.0),
        'x_sample': nrm((DEC_BATCH, DEC_SEQ, D_MODEL), 1.0),
        'state_ssm': nrm((N_A_LAYERS, DEC_BATCH, SSM_HEADS, SSM_HEAD_DIM, D_STATE), 0.5),
        'state_conv': nrm((N_A_LAYERS, DEC_BATCH, CONV_W - 1, CONV_DIM), 1.0),
        'cache_k': nrm((DEC_BATCH, WINDOW, ATT_KV_HEADS, ATT_HEAD_DIM), 1.0),
        'cache_v': nrm((DEC_BATCH, WINDOW, ATT_KV_HEADS, ATT_HEAD_DIM), 1.0),
        'p_prompt': nrm((DEPTH, BATCH, SEQ, D_PLE), 1.0),
        'p_sample': nrm((DEPTH, DEC_BATCH, DEC_SEQ, D_PLE), 1.0),
        'ffn1_norm': gain((DEPTH, D_MODEL)),
        'ffn1_wi': nrm((DEPTH, D_MODEL, 2 * D_FF), D_MODEL ** -0.5),
        'ffn1_wo': nrm((DEPTH, D_FF, D_MODEL), D_FF ** -0.5),
        'mix_norm': gain((DEPTH, D_MODEL)),
        'ffn2_norm': gain((DEPTH, D_MODEL)),
        'ffn2_wi': nrm((DEPTH, D_MODEL, 2 * D_FF), D_MODEL ** -0.5),
        'ffn2_wo': nrm((DEPTH, D_FF, D_MODEL), D_FF ** -0.5),
        'ple_norm': gain((DEPTH, D_MODEL)),
        'ple_gate': nrm((DEPTH, D_MODEL, D_MODEL), D_MODEL ** -0.5),
        'ple_proj': nrm((DEPTH, D_PLE, D_MODEL), D_PLE ** -0.5),
        'ssm_in': nrm((N_A_LAYERS, D_MODEL, D_INNER + CONV_DIM + SSM_HEADS), D_MODEL ** -0.5),
        'ssm_conv_w': nrm((N_A_LAYERS, CONV_W, CONV_DIM), CONV_W ** -0.5),
        'ssm_conv_b': nrm((N_A_LAYERS, CONV_DIM), 0.01),
        'ssm_dt_bias': dt0 + jnp.log(-jnp.expm1(-dt0)),
        'ssm_a_log': jnp.log(jax.random.uniform(nk(), (N_A_LAYERS, SSM_HEADS), F32, 1.0, 16.0)),
        'ssm_d': gain((N_A_LAYERS, SSM_HEADS)),
        'ssm_norm': gain((N_A_LAYERS, D_INNER)),
        'ssm_out': nrm((N_A_LAYERS, D_INNER, D_MODEL), D_INNER ** -0.5),
        'kv_norm': gain((D_MODEL,)),
        'w_kv': nrm((D_MODEL, 2 * ATT_KV_HEADS * ATT_HEAD_DIM), D_MODEL ** -0.5),
        'k_norm': gain((ATT_HEAD_DIM,)),
        'w_q': nrm((N_B_LAYERS, D_MODEL, ATT_HEADS * ATT_HEAD_DIM), D_MODEL ** -0.5),
        'q_norm': gain((N_B_LAYERS, ATT_HEAD_DIM)),
        'attn_sinks': nrm((N_B_LAYERS, ATT_HEADS), 1.0),
        'w_o': nrm((N_B_LAYERS, ATT_HEADS * ATT_HEAD_DIM, D_MODEL), (ATT_HEADS * ATT_HEAD_DIM) ** -0.5),
    }
    return d

def reference(x_prompt, x_sample, state_ssm, state_conv, cache_k, cache_v, p_prompt, p_sample,
              ffn1_norm, ffn1_wi, ffn1_wo, mix_norm, ffn2_norm, ffn2_wi, ffn2_wo,
              ple_norm, ple_gate, ple_proj,
              ssm_in, ssm_conv_w, ssm_conv_b, ssm_dt_bias, ssm_a_log, ssm_d, ssm_norm, ssm_out,
              kv_norm, w_kv, k_norm, w_q, q_norm, attn_sinks, w_o):
    w = {'ffn1_norm': ffn1_norm, 'ffn1_wi': ffn1_wi, 'ffn1_wo': ffn1_wo, 'mix_norm': mix_norm,
         'ffn2_norm': ffn2_norm, 'ffn2_wi': ffn2_wi, 'ffn2_wo': ffn2_wo,
         'ple_norm': ple_norm, 'ple_gate': ple_gate, 'ple_proj': ple_proj,
         'ssm_in': ssm_in, 'ssm_conv_w': ssm_conv_w, 'ssm_conv_b': ssm_conv_b, 'ssm_dt_bias': ssm_dt_bias,
         'ssm_a_log': ssm_a_log, 'ssm_d': ssm_d, 'ssm_norm': ssm_norm, 'ssm_out': ssm_out,
         'kv_norm': kv_norm, 'w_kv': w_kv, 'k_norm': k_norm, 'w_q': w_q, 'q_norm': q_norm,
         'attn_sinks': attn_sinks, 'w_o': w_o}
    bp = x_prompt.shape[0]
    ssm0_p = jnp.zeros((N_A_LAYERS, bp, SSM_HEADS, SSM_HEAD_DIM, D_STATE), x_prompt.dtype)
    conv0_p = jnp.zeros((N_A_LAYERS, bp, CONV_W - 1, CONV_DIM), x_prompt.dtype)
    kv0_p = jnp.zeros((bp, WINDOW, ATT_KV_HEADS, ATT_HEAD_DIM), x_prompt.dtype)
    y_prompt, ssm_p, conv_p, k_p, v_p = trunk(x_prompt, p_prompt, ssm0_p, conv0_p, kv0_p, kv0_p, 0, False, w)
    y_sample, ssm_s, conv_s, k_s, v_s = trunk(x_sample, p_sample, state_ssm, state_conv, cache_k, cache_v, PAST_LEN, True, w)
    return (y_prompt, y_sample, ssm_p, conv_p, k_p, v_p, ssm_s, conv_s, k_s, v_s)


_drawn_inputs = setup_inputs


def setup_inputs(seed=0):
    import zlib

    import numpy as np

    out = dict(_drawn_inputs(seed))
    spreads = {}
    factors = {'ffn1_norm': 4.184,
     'ffn2_norm': 7.418,
     'ple_norm': 200.0,
     'ssm_conv_b': 3.54,
     'ssm_d': 32.261,
     'ssm_norm': 4.169,
     'kv_norm': 7.723,
     'k_norm': 7.262,
     'q_norm': 34.507,
     'attn_sinks': 200.0}
    for name, (base, spread) in spreads.items():
        noise = np.random.default_rng([zlib.crc32(name.encode()), seed]).standard_normal(out[name].shape)
        drawn = base * np.exp(spread * noise) if base else spread * noise
        out[name] = __import__('jax').numpy.asarray(drawn.astype(out[name].dtype))
    for name, factor in factors.items():
        out[name] = (out[name] * factor).astype(out[name].dtype)
    return out
```

```python
from contextlib import ExitStack

import numpy as np

import concourse.bass as bass
from concourse import mybir

F32 = mybir.dt.float32
F32R = mybir.dt.float32r
ACT = mybir.ActivationFunctionType
ALU = mybir.AluOpType
AX = mybir.AxisListType

P = 128
D = 1024
KT = D // P
T = 256
SEQS = 8
N = T + SEQS
FT = 2816 // P
EPS = 1e-6
HEADS = 32
XT = 16
G = 8
CT = 32
WINDOW = 128
AH = 16
RING = 4
UNIT = KT * P
SCALE = 64 ** -0.5

STAGES = [("f1i0", 2 * FT), ("f1o0", FT), ("sin", 49), ("sout", XT), ("f2i0", 2 * FT), ("f2o0", FT), ("pp0", 2), ("pg0", 8),
          ("kv", 4), ("f1i1", 2 * FT), ("f1o1", FT), ("q", 8), ("o", 8), ("f2i1", 2 * FT), ("f2o1", FT), ("pp1", 2), ("pg1", 8)]
NU = sum(n for _, n in STAGES)
U0 = {}
for _name, _n in STAGES:
    U0[_name] = sum(n for _, n in STAGES[:len(U0)])
A0, _a = {}, 0
for _name, _n in STAGES:
    A0[_name] = _a
    if not (_name[:3] in ("f1o", "f2o") or _name in ("sout", "o")):
        _a += 4 * _n if _name[:2] == "pp" else _n
A0["end"] = _a
BSTAGE = {"f1o0": 0, "sout": 1, "f2o0": 2, "f1o1": 3, "o": 4, "f2o1": 5}
NORM = {"f1i0": 0, "sin": 1, "f2i0": 2, "pg0": 3, "kv": 4, "q": 5, "f2i1": 6, "pg1": 7}
XREADY = {"f1i0": 0, "sin": 8, "f2i0": 16, "pg0": 24, "f1i1": 32, "q": 40, "f2i1": 48, "pg1": 56}
HREADY = {"f1o0": 0, "sout": FT, "f2o0": FT + XT, "f1o1": 2 * FT + XT, "o": 3 * FT + XT, "f2o1": 3 * FT + XT + 8}

C_ID, C_TRI, C_ONE, C_BLK, C_ROT, C_COS, C_SIN, C_MASK = 0, 128, 256, 384, 512, 640, 640 + N, 640 + 2 * N
NC_ = 640 + 2 * N + 384
G_F1, G_MIX, G_F2, G_PLE, G_KV = 0, 16, 32, 48, 64
V_CW, V_CB, V_D, V_NG, V_ALOG, V_DTB, V_KN, V_QN, V_SINKD, V_SINK = 72, 200, 232, 248, 264, 265, 266, 267, 268, 269
NV = 269 + AH


DT_STEPS = 18
PRE_D = 8


def gd_base(g, c):
    return 22 * g + 10 * c


def unit(base, i, j):
    return base + j + 4 * i, (base + j) // RING + i, (base + j) % RING


def trunk_kernel(nc, weights, xT, pT, cst, vec, convst, ssm0, kcT, vc_in, ck, cv,
                 y_out, ssm_p, conv_p, kv_p, ssm_s, conv_s, k_old, v_old, kv_new):
    dtx_rows = nc.dram_tensor("dtx_rows", (SEQS, XT * P), F32, kind="Internal").ap()
    with ExitStack() as ctx:
        def sb(name, shape, dt=F32):
            return ctx.enter_context(nc.sbuf_tensor(name, shape, dt))

        def sem(name):
            return ctx.enter_context(nc.semaphore(name))

        raw = sb("raw", [P, RING, UNIT])
        whi = sb("whi", [P, RING, UNIT], F32R)
        wlo = sb("wlo", [P, RING, UNIT], F32R)
        x = sb("x", [P, KT, N])
        xh = sb("xh", [P, KT, N], F32R)
        xl = sb("xl", [P, KT, N], F32R)
        sq = sb("sq", [P, KT * N])
        hh = sb("hh", [P, FT, N], F32R)
        hl = sb("hl", [P, FT, N], F32R)
        xact = sb("xact", [P, CT, N])
        zs = sb("zs", [P, XT, N])
        ph = sb("ph", [P, 2, N], F32R)
        pl = sb("pl", [P, 2, N], F32R)
        gu = sb("gu", [P, 4, N])
        rstd = sb("rstd", [P, N])
        cs = sb("cs", [P, NC_])
        vs = sb("vs", [P, NV])
        avec = sb("avec", [P, 1])
        gsq = sb("gsq", [P, 2, N])
        small = sb("small", [P, 1024])
        bank = [ctx.enter_context(nc.psum_tensor(f"bank{b}", [P, 512], F32)) for b in range(8)]

        ident, tri, ones = cs[:, C_ID:C_ID + P], cs[:, C_TRI:C_TRI + P], cs[:, C_ONE:C_ONE + P]
        blk, rot = cs[:, C_BLK:C_BLK + P], cs[:, C_ROT:C_ROT + P]
        cosT, sinT, mask = cs[:, C_COS:C_COS + N], cs[:, C_SIN:C_SIN + N], cs[:, C_MASK:C_MASK + 384]
        sq3 = sq[:, :].rearrange("p (k n) -> p k n", k=KT)

        raw_landed = [sem(f"raw_landed{s}") for s in range(RING)]
        hi_ready = sem("hi_ready")
        lo_ready = sem("lo_ready")
        unit_used = sem("unit_used")
        a_free = sem("a_free")
        b_done = sem("b_done")
        b_free = sem("b_free")
        xh_ready = sem("xh_ready")
        xl_ready = sem("xl_ready")
        sq_ready = sem("sq_ready")
        sums_done = sem("sums_done")
        var_ready = sem("var_ready")
        std_ready = sem("std_ready")
        silu_done = sem("silu_done")
        h_ready = sem("h_ready")
        hh_ready = sem("hh_ready")
        hl_ready = sem("hl_ready")
        init = sem("init")
        p_landed = sem("p_landed")
        ph_ready = sem("ph_ready")
        pl_ready = sem("pl_ready")
        pj_done = sem("pj_done")
        sig_done = sem("sig_done")
        dve_step = sem("dve_step")
        act_step = sem("act_step")
        pool_step = sem("pool_step")
        stored = sem("stored")
        x_final = sem("x_final")
        conv_raw = sem("conv_raw")
        conv_first = sem("conv_first")
        conv_sum = sem("conv_sum")
        conv_act = sem("conv_act")
        dt_d_step = sem("dt_d_step")
        dt_a_step = sem("dt_a_step")
        dec_sum = sem("dec_sum")
        dec_act = sem("dec_act")
        pre_p = sem("pre_p")
        pre_d = sem("pre_d")
        pre_a = sem("pre_a")
        dtx_out = sem("dtx_out")
        h0_landed = [sem("h0_landed0"), sem("h0_landed1")]
        h0_used = sem("h0_used")
        y_dec = sem("y_dec")
        gp = sem("gp")
        gd = sem("gd")
        ga = sem("ga")
        z_silu = sem("z_silu")
        gated = sem("gated")
        gated_sq = sem("gated_sq")
        gated_sum = sem("gated_sum")
        gated_var = sem("gated_var")
        gated_std = sem("gated_std")
        gn_ready = sem("gn_ready")
        st_out = [sem("st_out0"), sem("st_out1")]
        conv_out = sem("conv_out")
        late_in = [sem("late_in0"), sem("late_in1")]
        late_out = sem("late_out")
        kvh_ready = sem("kvh_ready")
        kvl_ready = sem("kvl_ready")
        head_sq = sem("head_sq")
        head_sum = sem("head_sum")
        head_var = sem("head_var")
        head_std = sem("head_std")
        head_n = sem("head_n")
        rot_done = sem("rot_done")
        roped = sem("roped")
        v_tr = sem("v_tr")
        v_tok = sem("v_tok")
        cache_in = sem("cache_in")
        old_out = sem("old_out")
        kv_out = sem("kv_out")
        dec_p = sem("dec_p")
        dec_d = sem("dec_d")
        dec_a = sem("dec_a")
        dec_a_go = sem("dec_a_go")
        s_done = sem("s_done")
        s_max = sem("s_max")
        s_exp = sem("s_exp")
        s_prob = sem("s_prob")
        p_tr = sem("p_tr")
        p_read = sem("p_read")
        pv_done = sem("pv_done")
        o_read = sem("o_read")

        block = ctx.enter_context(nc.Block())

        dd = small[0:64, 0:N]
        ddT = [small[:, N + 64 * c:N + 64 * c + 64] for c in range(2)]
        o_ = N + 128
        cumT = [small[0:32, o_ + 128 * c:o_ + 128 * c + 128] for c in range(2)]
        ncumT = [small[0:32, o_ + 256 + 128 * c:o_ + 256 + 128 * c + 128] for c in range(2)]
        o_ += 512
        tok = sb("tok", [P, 2, 3, HEADS])
        da_bc = sb("da_bc", [P, SEQS, HEADS])
        da_d = sb("da_d", [P, XT, SEQS])
        dt_d = sb("dt_d", [P, XT, SEQS])
        dtx_d = sb("dtx_d", [P, XT, SEQS])
        bc_d = sb("bc_d", [P, G, SEQS])
        b_d = sb("b_d", [P, G, SEQS])
        c_d = sb("c_d", [P, G, SEQS])
        t1d = sb("t1d", [P, XT, SEQS])
        state = sb("state", [P, 2, 256])
        decraw = sb("decraw", [P, CT, SEQS])
        tail = sb("tail", [P, CT, 3])
        zf = zs[:, :, :].rearrange("p k n -> p (k n)")
        convs = zf[:, 8 * N:8 * N + 768].rearrange("p (k w s) -> p k w s", k=CT, w=3)
        dgl = zf[0:64, 12 * N:12 * N + 256].rearrange("p (s h) -> p s h", s=SEQS)
        cwork = zf[:, 13 * N:13 * N + 256].rearrange("p (k s) -> p k s", k=CT)
        csum = xact[:, :, T:N]
        h0buf = [sq[:, 0:2048], zs[:, 8:16, :].rearrange("p k n -> p (k n)")[:, 0:2048]]
        dtxt = zs[0:SEQS, 8:16, :].rearrange("p k n -> p (k n)")[:, 0:2048]
        late = xact[:, 16:32, :].rearrange("p k n -> p (k n)")
        lateA, lateB = late[:, 0:2048], late[:, 2048:4096]
        Dm, Mm = sq[:, 0:512], sq[:, 512:1024]
        xdt, xte = sq[:, 1024:1280], sq[:, 1280:1536]
        h1, ytok = sq[:, 1536:1792], sq[:, 1792:2048]
        guf = gu[:, :, :].rearrange("p k n -> p (k n)")
        btok, cbm = guf[:, 0:128], guf[:, 128:256]
        xraw = guf[:, 0:4 * 260].rearrange("p (k n) -> p k n", k=4)
        pj = zs[:, 0:8, :]
        qf, kf, vf = xact[:, 0:8, :], xact[:, 8:10, :], xact[:, 10:12, :]
        xf = xact[:, :, :].rearrange("p k n -> p (k n)")
        vtok = xf[:, 12 * N:12 * N + 512].rearrange("p (c n) -> p c n", c=2)
        kc = xf[:, 14 * N:14 * N + 2048].rearrange("p (k s w) -> p k s w", k=2, s=SEQS)
        vc = xf[:, 22 * N:22 * N + 2048].rearrange("p (s n) -> p s n", s=SEQS)
        o32 = zs[:, 0:8, :]
        sm = zs[:, 8:11, :].rearrange("p k n -> p (k n)")[:, 0:768].rearrange("p (b n) -> p b n", b=2)
        pT_ = zs[:, 11:14, :].rearrange("p k n -> p (k n)")[:, 0:768].rearrange("p (b n) -> p b n", b=2)
        aw = sq[:, 0:4 * N].rearrange("p (k n) -> p k n", k=4)
        mx = small[:, 0:4]; nmx = small[:, 4:8]; rs = small[:, 8:12]; es = small[:, 12:16]; rr = small[:, 16:20]
        dS = small[:, 128:128 + 129]; dP = small[:, 260:260 + 129]; sTd = small[:, 400:528]
        prod = small[:, 528:656]; dgP = small[:, 656:784]; pTd = small[:, 784:912]; od = small[:, 912:976]
        dm = small[:, 976:984]

        def link(eng, step, count, ins):
            count[0] += 1
            ins.then_inc(step, 1)
            eng.wait_ge(step, count[0])

        @block.sync
        def _(sp):
            sp.dma_start(x[:, :, :], xT).then_inc(init, 16)
            sp.dma_start(cs[:, :], cst).then_inc(init, 16)
            sp.dma_start(vs[:, :], vec).then_inc(init, 16)
            sp.dma_start(convs, convst).then_inc(init, 16)
            for s in range(RING):
                sp.dma_start(raw[:, s, :], weights[s]).then_inc(raw_landed[s], 16)

            with sp.Fori(1, NU // RING) as i:
                for s in range(RING):
                    sp.wait_ge(lo_ready, i * RING + (s - RING + 1))
                    sp.dma_start(raw[:, s, :], weights[bass.ds(i * RING + s, 1)].rearrange("u p n -> p (u n)")).then_inc(raw_landed[s], 16)
            for u in range(NU // RING * RING, NU):
                sp.wait_ge(lo_ready, u - RING + 1)
                sp.dma_start(raw[:, u % RING, :], weights[u]).then_inc(raw_landed[u % RING], 16)
            for m in range(KT):
                sp.wait_ge(x_final, KT + m + 1)
                sp.dma_start(y_out[:, m, :], x[:, m, :]).then_inc(stored, 16)
            sp.wait_ge(stored, 16 * KT)

        @block.tensor
        def _(pe):
            pe.sem_inc(unit_used, RING)

            def split_products(out, w, tile, rh, rl, start, stop):
                c = slice(tile * P, tile * P + P)
                pe.matmul(out, whi[:, w, c], rh, start=start, stop=False)
                pe.matmul(out, whi[:, w, c], rl, start=False, stop=False)
                return pe.matmul(out, wlo[:, w, c], rh, start=False, stop=stop)

            def unit_a(stage, i, j, b_wait=None, x_wait=False, rh=xh, rl=xl, kv_wait=False):
                u, _, s = unit(U0[stage], i, j)
                out = bank[(A0[stage] + j) % 4]
                pe.wait_ge(lo_ready, u + 1)
                pe.wait_ge(a_free, A0[stage] + j + 4 * i + 1)
                if b_wait is not None:
                    pe.wait_ge(b_free, 8 * b_wait + (A0[stage] + j) % 4 + 1)
                for k in range(KT):
                    if x_wait:
                        pe.wait_ge(xl_ready, XREADY[stage] + k + 1)
                    if kv_wait:
                        pe.wait_ge(kvl_ready, k + 1)
                    mm = split_products(out[:, 0:N], s, k, rh[:, k, :], rl[:, k, :], k == 0, k == KT - 1)
                mm.then_inc(unit_used, 1)

            def sums(stage, b_wait=None):
                pe.wait_ge(sq_ready, NORM[stage] + 1)
                if b_wait is not None:
                    pe.wait_ge(b_free, 8 * b_wait + 5)
                for k in range(KT):
                    mm = pe.matmul(bank[4][:, 0:N], ones, sq3[:, k, :], start=k == 0, stop=k == KT - 1)
                mm.then_inc(sums_done, 1)

            def first_units(stage, n, b_wait, no_sums=False):
                for j in range(n):
                    unit_a(stage, 0, j, b_wait if j < 4 else None, x_wait=(j == 0))
                    if j == 1 and not no_sums:
                        sums(stage, b_wait)

            def first_units_p(stage, b_wait):
                for j in range(KT):
                    unit_a(stage, 0, j, x_wait=(j == 0))
                    if j == 1:
                        sums(stage, b_wait)

            def head_sum_(n_):
                pe.wait_ge(head_sq, n_ + 1)
                if n_ > 0:
                    pe.wait_ge(head_var, n_)
                pe.matmul(bank[5][:, 0:N], blk, aw[:, n_ % 2, :], start=True, stop=True).then_inc(head_sum, 1)

            def head_rot(n_, tile):
                pe.wait_ge(head_n, n_ + 1)
                if n_ > 0:
                    pe.wait_ge(roped, n_)
                pe.matmul(bank[6][:, 0:N], rot, tile, start=True, stop=True).then_inc(rot_done, 1)

            def head_norms(n0, n1):
                for n_ in range(n0, n1):
                    head_sum_(n_)
                for n_ in range(n0, n1):
                    head_rot(n_, kf[:, n_, :])

            def ffn_in(stage, b_wait):
                first_units(stage, 4, b_wait)
                with pe.Fori(1, 2 * FT // RING) as i:
                    for j in range(RING):
                        unit_a(stage, i, j)

            def unit_b(stage, u, s, kt, where, order, first, last, hready):
                pe.wait_ge(lo_ready, u + 1)
                pe.wait_ge(hl_ready, hready)
                rh, rl = (hh[:, kt, :], hl[:, kt, :]) if isinstance(kt, int) else (
                    hh[:, bass.ds(kt, 1), :].rearrange("p a n -> p (a n)"), hl[:, bass.ds(kt, 1), :].rearrange("p a n -> p (a n)"))
                for n_, m in enumerate(order):
                    if first and m == 0:
                        pe.wait_ge(a_free, A0[where] + 4)
                    mm = split_products(bank[m][:, 0:N], s, m, rh, rl, first, last)
                    if last and n_ < 7:
                        mm.then_inc(b_done, 1)
                mm.then_inc(unit_used, 1)

            def stage_b(stage, n, after):
                h0_ = HREADY[stage]
                u, _, s = unit(U0[stage], 0, 0)
                unit_b(stage, u, s, 0, after, (4, 5, 6, 7, 0, 1, 2, 3), True, False, h0_ + 1)
                loops = (n - 2) // RING
                with pe.Fori(0, loops) as i:
                    for j in range(1, RING + 1):
                        u, _, s = unit(U0[stage], i, j)
                        unit_b(stage, u, s, i * RING + j, after, range(8), False, False, i * RING + (h0_ + j + 1))
                for j in range(1 + loops * RING, n):
                    u, _, s = unit(U0[stage], 0, j)
                    unit_b(stage, u, s, j, after, range(8), False, j == n - 1, h0_ + j + 1)

            def embed(stage, b_wait, layer):
                pe.wait_ge(pl_ready, layer + 1)
                for j in range(2):
                    u, _, s = unit(U0[stage], 0, j)
                    pe.wait_ge(lo_ready, u + 1)
                    for m in range(4):
                        a = A0[stage] + 4 * j + m
                        pe.wait_ge(a_free, a + 1)
                        if j == 0:
                            pe.wait_ge(b_free, 8 * b_wait + a % 4 + 1)
                        for k in range(2):
                            mm = split_products(bank[a % 4][:, 0:N], s, 2 * m + k, ph[:, k, :], pl[:, k, :], k == 0, k == 1)
                        mm.then_inc(unit_used if m == 3 else pj_done, 1)

            def group_step(g, c):
                k_ = 2 * g + c
                r = slice(128 * c, 128 * c + 128)
                base = gd_base(g, c)
                if k_ == 0:
                    pe.wait_ge(y_dec, 1)
                else:
                    pe.wait_ge(gd, base - (12 if c == 0 else 10) + 3)
                pe.matmul(bank[4][:, 0:128], xact[:, 16 + g, r], xact[:, 24 + g, r], start=True, stop=True)
                pe.transpose(bank[4][:, 128:256], xact[:, 2 * g, r], ident)
                pe.transpose(bank[4][:, 256:384], xact[:, 2 * g + 1, r], ident)
                pe.transpose(bank[4][:, 384:512], xact[:, 16 + g, r], ident).then_inc(gp, 1)
                if k_ > 0:
                    pe.wait_ge(gd, base - (12 if c == 0 else 10) + 5)
                if g > 5 or (g == 5 and c == 1):
                    pe.wait_ge(gated_var, g - 5)
                for h in range(4):
                    pe.matmul(bank[5][:, 128 * h:128 * h + 128], ident[0:32, 4 * g + h:4 * g + h + 1].to_broadcast([32, 128]),
                              cumT[c], start=(h == 0), stop=False, skip_group_check=True)
                pe.matmul(bank[5][:, 0:512], ncumT[c], ident[0:32, 4 * g:4 * g + 4].unsqueeze(2).to_broadcast([32, 4, 128]),
                          start=False, stop=True, skip_group_check=True).then_inc(gp, 1)
                pe.wait_ge(gd, base + 6)
                for h in range(4):
                    pe.matmul(bank[6][:, 64 * h:64 * h + 64], Mm[:, 128 * h:128 * h + 128], xdt[:, 64 * h:64 * h + 64], start=True, stop=True)
                if c == 1:
                    pe.matmul(bank[6][:, 256:512], xact[:, 24 + g, r], h1, start=True, stop=True)
                pe.matmul(bank[7][:, 0:256], btok, xte, start=True, stop=True).then_inc(gp, 1)
                pe.wait_ge(gd, base + (8 if c == 0 else 10))
                pe.transpose(bank[7][:, 256:384], ytok[:, 0:128], ident)
                pe.transpose(bank[7][:, 384:512], ytok[:, 128:256], ident).then_inc(gp, 1)

            def norm_sums(g):
                pe.wait_ge(gated_sq, g + 1)
                if g > 0:
                    pe.wait_ge(gated_var, g)
                pe.matmul(bank[5][:, 0:N], ones, gsq[:, 0, :], start=True, stop=False)
                pe.matmul(bank[5][:, 0:N], ones, gsq[:, 1, :], start=False, stop=True).then_inc(gated_sum, 1)

            pe.wait_ge(init, 64)
            ffn_in("f1i0", None)
            stage_b("f1o0", FT, "sin")
            first_units("sin", 5, 0)
            with pe.Fori(0, 7) as i:
                for j in range(5, 9):
                    unit_a("sin", i, j)
            pe.wait_ge(dt_d_step, DT_STEPS)
            pe.transpose(bank[5][:, 0:64], dd[:, 0:128], ident[0:64, 0:64])
            pe.transpose(bank[5][:, 64:128], dd[:, 128:256], ident[0:64, 0:64]).then_inc(pre_p, 1)
            pe.wait_ge(pre_d, 1)
            for c in range(2):
                dta = ddT[c][:, 0:HEADS]
                pe.matmul(bank[6][:, 64 * c:64 * c + 32], tri, dta, start=True, stop=True)
                pe.matmul(bank[6][:, 64 * c + 32:64 * c + 64], ones, dta, start=True, stop=True)
                pe.matmul(bank[7][0:32, 128 * c:128 * c + 128], dta, tri, start=True, stop=True)
            pe.wait_ge(pre_d, 3)
            pe.matmul(bank[4][:, 0:256], ones[32:64, :], dgl[32:64], start=True, stop=True)
            pe.matmul(bank[6][:, 128:384], ones[0:32, :], dgl[0:32], start=True, stop=True)
            pe.matmul(bank[5][:, 128:192], ones, bc_d[:, :, :], start=True, stop=True).then_inc(pre_p, 1)
            pe.wait_ge(pre_d, PRE_D)
            for j in range(XT):
                mm = pe.transpose(bank[4 + j // 4][0:SEQS, 128 * (j % 4):128 * (j % 4) + 128], dtx_d[:, j, :], ident)
            mm.then_inc(pre_p, 1)
            for s_ in range(XT + 1):
                if s_ < XT:
                    unit_a("sin", 0, 33 + s_)
                if s_ < 4:
                    for q in (2 * s_, 2 * s_ + 1):
                        if q == 0:
                            pe.wait_ge(pre_d, PRE_D + 1)
                        pe.wait_ge(h0_landed[q % 2], 16 * (q // 2 + 1))
                        for j in range(XT):
                            mm = pe.matmul(bank[4][:, 8 * j + q:8 * j + q + 1], h0buf[q % 2][:, 128 * j:128 * j + 128],
                                           c_d[:, j // 2, q:q + 1], start=True, stop=True)
                        mm.then_inc(h0_used, 1)
                if 4 <= s_ < 12:
                    group_step(s_ - 4, 0)
                    group_step(s_ - 4, 1)
                if s_ >= 9:
                    norm_sums(s_ - 9)
            pe.wait_ge(gated_var, 8)
            stage_b("sout", XT, "f2i0")
            ffn_in("f2i0", 1)
            stage_b("f2o0", FT, "pp0")
            embed("pp0", 2, 0)
            first_units_p("pg0", 2)
            for j in range(4):
                unit_a("kv", 0, j, rh=hh, rl=hl, kv_wait=(j == 0))
                if j == 1:
                    sums("kv", None)
            head_norms(0, 2)
            pe.wait_ge(a_free, A0["kv"] + 4 + 4)
            pe.wait_ge(roped, 2)
            for c in range(2):
                for n_ in range(2):
                    mm = pe.transpose(bank[7][:, 256 * c + 128 * n_:256 * c + 128 * n_ + 128], vf[:, n_, 128 * c:128 * c + 128], ident)
            mm.then_inc(v_tr, 1)
            first_units("f1i1", 4, None, no_sums=True)
            with pe.Fori(1, 2 * FT // RING) as i:
                for j in range(RING):
                    unit_a("f1i1", i, j)
            stage_b("f1o1", FT, "q")
            for t in range(KT + 2):
                if t < KT:
                    unit_a("q", 0, t, 3 if t < 4 else None, x_wait=(t == 0))
                if t == 1:
                    sums("q", 3)
                if 1 <= t <= KT:
                    head_sum_(2 + t - 1)
                if t >= 2:
                    head_rot(2 + t - 2, qf[:, t - 2, :])
            pe.wait_ge(roped, 10)
            pe.wait_ge(cache_in, 32)
            for b in range(2):
                hs = slice(64 * b, 64 * b + 64)
                for q in range(SEQS):
                    for kp in range(2):
                        c_ = 8 * q + 4 * kp
                        mm = pe.matmul(bank[4 + b][:, c_:c_ + 4], kc[hs, kp, q, :], qf[hs, 4 * kp:4 * kp + 4, T + q],
                                       start=True, stop=True)
            mm.then_inc(dec_p, 1)
            pe.wait_ge(dec_d, 2)
            pe.transpose(bank[6][:, 0:128], sTd, ident)
            pe.matmul(bank[6][0:64, 128:129], prod[0:64, 0:64], ones[0:64, 0:1], start=True, stop=True)
            pe.matmul(bank[7][64:128, 0:1], prod[64:128, 0:64], ones[64:128, 0:1], start=True, stop=True).then_inc(dec_p, 1)
            pe.wait_ge(dec_d, 3)
            pe.transpose(bank[6][:, 0:128], dP[:, 0:128], ident)
            pe.matmul(bank[5][:, 0:128], ones, dgP, start=True, stop=True).then_inc(dec_p, 1)
            pe.wait_ge(dec_d, 4)
            for q in range(SEQS):
                for kp in range(2):
                    for b in range(2):
                        c_ = 8 * q + 4 * kp
                        mm = pe.matmul(bank[4][64 * b:64 * b + 64, c_:c_ + 4], vc[:, q, 64 * (2 * kp + b):64 * (2 * kp + b) + 64],
                                       pTd[:, 64 * b + c_:64 * b + c_ + 4], start=True, stop=True)
            mm.then_inc(dec_p, 1)
            def scores(e):
                t, b = e // 2, e % 2
                hs = slice(64 * b, 64 * b + 64)
                if e < 2:
                    pe.wait_ge(dec_d, 5)
                else:
                    pe.wait_ge(s_max, e - 1)
                k = kf[hs, t // 4, :]
                pe.matmul(bank[4 + b][:, 0:128], qf[hs, t, 0:128], k[:, 0:128], start=True, stop=True)
                pe.matmul(bank[4 + b][:, 128:384], qf[hs, t, 128:256], k[:, 0:256], start=True, stop=True).then_inc(s_done, 1)

            scores(0)
            scores(1)
            pe.wait_ge(v_tok, 1)
            for e in range(AH):
                t, b = e // 2, e % 2
                pe.wait_ge(s_prob, e + 1)
                if e > 0:
                    pe.wait_ge(p_read, e)
                for n_ in range(3):
                    mm = pe.transpose(bank[6][:, 128 * n_:128 * n_ + 128], sm[:, b, 128 * n_:128 * n_ + 128], ident)
                mm.then_inc(p_tr, 1)
                if e + 2 < AH:
                    scores(e + 2)
                pe.wait_ge(p_read, e + 1)
                if e > 0:
                    pe.wait_ge(o_read, e)
                ob = bank[7][64 * b:64 * b + 64, :]
                v_ = slice(64 * (2 * (t // 4) + b), 64 * (2 * (t // 4) + b) + 64)
                pe.matmul(ob[:, 0:128], vtok[:, 0, v_], pT_[:, b, 0:128], start=True, stop=True)
                pe.matmul(ob[:, 128:256], vtok[:, 0, v_], pT_[:, b, 128:256], start=True, stop=False)
                pe.matmul(ob[:, 128:256], vtok[:, 1, v_], pT_[:, b, 256:384], start=False, stop=True).then_inc(pv_done, 1)
            stage_b("o", 8, "f2i1")
            ffn_in("f2i1", 4)
            stage_b("f2o1", FT, "pp1")
            embed("pp1", 5, 1)
            first_units_p("pg1", 5)

        @block.scalar
        def _(act):
            steps = [0]

            def round_unit(u, q, s):
                act.wait_ge(raw_landed[s], q * 16 + 16)
                act.wait_ge(unit_used, u + 1)
                act.activation(whi[:, s, :], raw[:, s, :], ACT.Copy).then_inc(hi_ready, 1)

            def ahead(stage, i, j):
                if U0[stage] + RING + j < NU:
                    round_unit(*unit(U0[stage] + RING, i, j))

            def ahead_all(stage, n):
                if n >= 8:
                    with act.Fori(0, n // RING) as i:
                        for j in range(RING):
                            ahead(stage, i, j)
                for j in range(n // RING * RING if n >= 8 else 0, n):
                    ahead(stage, 0, j)

            def split_x(gain, b_stage):
                for m in range(KT):
                    if b_stage is not None:
                        act.wait_ge(b_free, 8 * b_stage + m + 1)
                    act.activation(xh[:, m, :], x[:, m, :], ACT.Copy, scale=vs[:, gain + m:gain + m + 1]).then_inc(xh_ready, 1)
                act.activation(sq[:, :], x[:, :, :].rearrange("p k n -> p (k n)"), ACT.Square).then_inc(sq_ready, 1)

            def root(stage):
                act.wait_ge(var_ready, NORM[stage] + 1)
                act.activation(rstd[:, :], rstd[:, :], ACT.Sqrt).then_inc(std_ready, 1)

            def ffn_in(stage, out, ffn):
                def silu(i, p):
                    act.wait_ge(a_free, A0[stage] + 4 * i + 2 * p + 1 + 4)
                    act.activation(gu[:, 2 * p, :], gu[:, 2 * p, :], ACT.Silu).then_inc(silu_done, 1)

                def round_h(i, p):
                    act.wait_ge(h_ready, FT * ffn + 2 * i + p + 1)
                    dst = hh[:, p, :] if isinstance(i, int) else hh[:, bass.ds(2 * i + p, 1), :].rearrange("p a n -> p (a n)")
                    act.activation(dst, gu[:, 2 * p + 1, :], ACT.Copy).then_inc(hh_ready, 1)

                ahead(stage, 0, 0)
                ahead(stage, 0, 1)
                if stage in NORM:
                    root(stage)
                act.preload_act_table(ACT.Silu)
                silu(0, 0)
                ahead(stage, 0, 2)
                round_h(0, 0)
                silu(0, 1)
                ahead(stage, 0, 3)
                round_h(0, 1)
                with act.Fori(1, 2 * FT // RING) as i:
                    ahead(stage, i, 0)
                    silu(i, 0)
                    ahead(stage, i, 1)
                    round_h(i, 0)
                    ahead(stage, i, 2)
                    silu(i, 1)
                    ahead(stage, i, 3)
                    round_h(i, 1)

            def embed(stage, gate, layer):
                ahead(stage, 0, 0)
                ahead(stage, 0, 1)
                ahead(gate, 0, 0)
                ahead(gate, 0, 1)
                root(gate)
                for j in range(KT):
                    act.wait_ge(a_free, A0[gate] + j + 1 + 4)
                    act.activation(gu[:, j % 4, :], gu[:, j % 4, :], ACT.Sigmoid).then_inc(sig_done, 1)
                    if j >= 2:
                        ahead(gate, 0, j)

            def split_p(layer):
                act.wait_ge(p_landed, 16 * (layer + 1))
                act.activation(ph[:, :, :], gsq[:, :, :], ACT.Copy).then_inc(ph_ready, 1)

            def head_square(n_, tile, a):
                act.wait_ge(a_free, a + 1 + 4)
                if n_ > 1:
                    act.wait_ge(head_n, n_ - 1)
                act.activation(aw[:, n_ % 2, :], tile, ACT.Square).then_inc(head_sq, 1)

            def head_root(n_):
                act.wait_ge(head_var, n_ + 1)
                act.activation(aw[:, n_ % 2, :], aw[:, n_ % 2, :], ACT.Sqrt).then_inc(head_std, 1)

            for u in range(RING):
                round_unit(*unit(0, 0, u))
            act.wait_ge(init, 64)
            split_x(G_F1, None)
            ffn_in("f1i0", "f1o0", 0)
            ahead_all("f1o0", FT)
            split_x(G_MIX, 0)
            ahead("sin", 0, 0)
            root("sin")
            act.activation(avec[0:32, :], vs[0:32, V_ALOG:V_ALOG + 1], ACT.Exp).then_inc(dt_a_step, 1)
            act.wait_ge(dt_d_step, 2)
            act.activation(zs[0:64, 1, :], zs[0:64, 1, :], ACT.Exp).then_inc(dt_a_step, 1)
            act.preload_act_table(ACT.Silu)

            def tap_last(i, p, tile):
                act.wait_ge(conv_raw, tile + 1)
                one = (lambda a: a[:, p, :]) if isinstance(i, int) else (lambda a: a[:, bass.ds(tile, 1), :].rearrange("p a n -> p (a n)"))
                act.activation(one(xact)[:, 0:T], xraw[:, p, 3:259], ACT.Identity, scale=cw3(i, p, tile), bias=cb(i, p, tile)).then_inc(conv_first, 1)

            def cw3(i, p, tile):
                c = V_CW + 3 * CT
                return vs[:, c + p:c + p + 1] if isinstance(i, int) else vs[:, bass.ds(tile + c, 1)]

            def cb(i, p, tile):
                return vs[:, V_CB + p:V_CB + p + 1] if isinstance(i, int) else vs[:, bass.ds(tile + V_CB, 1)]

            def conv_silu(i, p, tile):
                t_ = xact[:, p, 0:T] if isinstance(i, int) else xact[:, bass.ds(tile, 1), 0:T].rearrange("p a n -> p (a n)")
                act.activation(t_, t_, ACT.Silu).then_inc(conv_act, 1)

            def conv_body(i, j0):
                for p in range(4):
                    tap_last(i, p, i * 4 + p)
                    if p > 0:
                        act.wait_ge(conv_sum, 3 * (i * 4) + (3 * p if p < 3 else 12))
                    ahead("sin", *((0, j0 + p) if isinstance(i, int) else (i - 1, j0 + p)))
                    if p > 0:
                        conv_silu(i, p - 1, i * 4 + (p - 1))
                conv_silu(i, 3, i * 4 + 3)

            conv_body(0, 1)
            with act.Fori(1, CT // 4) as i:
                conv_body(i, 5)
            act.wait_ge(dec_sum, 1)
            act.activation(csum, csum, ACT.Silu).then_inc(dec_act, 1)
            act.wait_ge(pre_d, 6)
            act.activation(tok[:, :, :, :], tok[:, :, :, :], ACT.Exp).then_inc(pre_a, 1)
            act.wait_ge(pre_d, 7)
            act.activation(da_d[:, :, :], da_d[:, :, :], ACT.Exp).then_inc(pre_a, 1)
            act.wait_ge(pre_d, 8)
            act.activation(da_bc[:, :, :], da_bc[:, :, :], ACT.Exp).then_inc(pre_a, 1)

            def zsilu(t0, t1):
                act.wait_ge(a_free, A0["sin"] + 33 + t1 + 4)
                act.activation(zs[:, t0:t1, :], zs[:, t0:t1, :], ACT.Silu).then_inc(z_silu, 1)

            for s_ in range(XT + 1):
                if s_ < XT:
                    ahead("sin", 0, 33 + s_)
                if s_ == 9:
                    zsilu(0, 8)
                if 4 <= s_ < 12:
                    for c in range(2):
                        act.wait_ge(gd, gd_base(s_ - 4, c) + 5)
                        act.activation(Dm, Dm, ACT.Exp).then_inc(ga, 1)
                if s_ >= 9:
                    g = s_ - 9
                    if g >= 4:
                        zsilu(2 * g, 2 * g + 2)
                    act.wait_ge(gated, g + 1)
                    act.activation(gsq[:, :, :], zs[:, 2 * g:2 * g + 2, :], ACT.Square).then_inc(gated_sq, 1)
                    if g % 4 == 3:
                        act.wait_ge(gated_var, g + 1)
                        v_ = xact[:, 2 * g - 6:2 * g + 1:2, :]
                        act.activation(v_, v_, ACT.Sqrt).then_inc(gated_std, 1)
                        for t in range(2 * g - 6, 2 * g + 2):
                            act.wait_ge(gn_ready, t + 1)
                            act.activation(hh[:, t, :], zs[:, t, :], ACT.Copy).then_inc(hh_ready, 1)
            ahead_all("sout", XT)
            split_x(G_F2, 1)
            act.wait_ge(gated_sum, 8)
            act.dma_start(gsq[:, :, :], pT[0]).then_inc(p_landed, 16)
            ffn_in("f2i0", "f2o0", 1)
            split_p(0)
            ahead_all("f2o0", FT)
            split_x(G_PLE, 2)
            embed("pp0", "pg0", 0)
            for m in range(KT):
                act.wait_ge(x_final, m + 1)
                act.activation(hh[:, m, :], x[:, m, :], ACT.Copy, scale=vs[:, G_KV + m:G_KV + m + 1]).then_inc(kvh_ready, 1)
            act.activation(sq[:, :], x[:, :, :].rearrange("p k n -> p (k n)"), ACT.Square).then_inc(sq_ready, 1)
            for m in range(KT):
                act.activation(xh[:, m, :], x[:, m, :], ACT.Copy, scale=vs[:, G_F1 + 8 + m:G_F1 + 8 + m + 1]).then_inc(xh_ready, 1)
            for j in range(4):
                ahead("kv", 0, j)
                if j == 1:
                    root("kv")
                    head_square(0, kf[:, 0, :], A0["kv"])
                    head_square(1, kf[:, 1, :], A0["kv"] + 1)
            head_root(0)
            head_root(1)
            ffn_in("f1i1", "f1o1", 2)
            ahead_all("f1o1", FT)
            split_x(G_MIX + 8, 3)
            ahead("q", 0, 0)
            ahead("q", 0, 1)
            root("q")
            for t in range(KT + 1):
                if t < KT:
                    head_square(2 + t, qf[:, t, :], A0["q"] + t)
                if t >= 1:
                    head_root(2 + t - 1)
                if 2 <= t < KT:
                    ahead("q", 0, t)
            act.wait_ge(dec_a_go, 1)
            act.activation(dP, dS, ACT.Exp, bias=dm[:, 1:2], accum_out=dm[:, 2:3])
            act.activation(dm[:, 3:4], dm[:, 1:2], ACT.Exp, bias=vs[:, V_SINKD:V_SINKD + 1]).then_inc(dec_a, 1)
            for e in range(AH):
                b = e % 2
                act.wait_ge(s_max, e + 1)
                act.activation(sm[:, b, 0:128], sm[:, b, 0:128], ACT.Exp, bias=nmx[:, 2 * b:2 * b + 1], accum_out=rs[:, 2 * b:2 * b + 1])
                act.activation(sm[:, b, 128:384], sm[:, b, 128:384], ACT.Exp, bias=nmx[:, 2 * b + 1:2 * b + 2], accum_out=rs[:, 2 * b + 1:2 * b + 2])
                act.activation(es[:, 2 * b:2 * b + 2], nmx[:, 2 * b:2 * b + 2], ACT.Exp, bias=vs[:, V_SINK + e:V_SINK + e + 1]).then_inc(s_exp, 1)
            for t in range(KT):
                act.wait_ge(o_read, 2 * t + 2)
                act.activation(hh[:, t, :], o32[:, t, :], ACT.Copy).then_inc(hh_ready, 1)
            ahead_all("o", 8)
            split_x(G_F2 + 8, 4)
            act.wait_ge(pl_ready, 1)
            act.dma_start(gsq[:, :, :], pT[1]).then_inc(p_landed, 16)
            ffn_in("f2i1", "f2o1", 3)
            split_p(1)
            ahead_all("f2o1", FT)
            split_x(G_PLE + 8, 5)
            embed("pp1", "pg1", 1)

        @block.vector
        def _(dve):
            steps = [0]

            def low_unit(u, q, s):
                dve.wait_ge(hi_ready, u + 1)
                dve.tensor_tensor(wlo[:, s, :], raw[:, s, :], whi[:, s, :].bitcast(F32), ALU.subtract).then_inc(lo_ready, 1)

            def ahead(stage, i, j):
                if U0[stage] + RING + j < NU:
                    low_unit(*unit(U0[stage] + RING, i, j))

            def ahead_all(stage, n):
                if n >= 8:
                    with dve.Fori(0, n // RING) as i:
                        for j in range(RING):
                            ahead(stage, i, j)
                for j in range(n // RING * RING if n >= 8 else 0, n):
                    ahead(stage, 0, j)

            def low_x(m, gain, n_):
                dve.wait_ge(xh_ready, n_ + m + 1)
                dve.scalar_tensor_tensor(out=xl[:, m, :], in0=x[:, m, :], scalar=vs[:, gain + m:gain + m + 1],
                                         in1=xh[:, m, :].bitcast(F32), op0=ALU.mult, op1=ALU.subtract).then_inc(xl_ready, 1)

            def add_b(stage, n, scale, gain, after):
                b = BSTAGE[stage]
                for m in range(KT):
                    if m < 7:
                        dve.wait_ge(b_done, 7 * b + m + 1)
                    else:
                        dve.wait_ge(unit_used, U0[stage] + n + RING)
                    dve.scalar_tensor_tensor(out=x[:, m, :], in0=bank[m][:, 0:N], scalar=scale, in1=x[:, m, :],
                                             op0=ALU.mult, op1=ALU.add).then_inc(b_free, 1)
                    if m > 0:
                        low_x(m - 1, gain, XREADY[after])
                low_x(7, gain, XREADY[after])

            def row_factor(stage):
                dve.wait_ge(sums_done, NORM[stage] + 1)
                dve.tensor_scalar(rstd[:, :], bank[4][:, 0:N], 1.0 / D, EPS, ALU.mult, ALU.add).then_inc(var_ready, 1)
                dve.wait_ge(std_ready, NORM[stage] + 1)
                link(dve, dve_step, steps, dve.reciprocal(rstd[:, :], rstd[:, :]))

            def take(dst, stage, j, i=0, cols=slice(0, N), scale=True, signal=True):
                dve.wait_ge(unit_used, U0[stage] + j + 4 * i + 1 + RING)
                ins = dve.tensor_tensor(dst, bank[(A0[stage] + j) % 4][:, cols], rstd[:, cols], ALU.mult)
                return ins.then_inc(a_free, 1) if signal else ins

            def ffn_in(stage, out, ffn):
                def gate(i, p):
                    take(gu[:, 2 * p, :], stage, 2 * p, i)

                def up(i, p):
                    take(gu[:, 2 * p + 1, :], stage, 2 * p + 1, i)

                def hidden(i, p):
                    dve.wait_ge(silu_done, FT * ffn + 2 * i + p + 1)
                    dve.wait_ge(a_free, A0[stage] + 4 * i + 2 * p + 2 + 4)
                    dve.tensor_tensor(gu[:, 2 * p + 1, :], gu[:, 2 * p, :], gu[:, 2 * p + 1, :], ALU.mult).then_inc(h_ready, 1)

                def low_h(i, p):
                    dve.wait_ge(hh_ready, HREADY[out] + 2 * i + p + 1)
                    one = (lambda a: a[:, p, :]) if isinstance(i, int) else (lambda a: a[:, bass.ds(2 * i + p, 1), :].rearrange("p a n -> p (a n)"))
                    dve.tensor_tensor(one(hl), gu[:, 2 * p + 1, :], one(hh).bitcast(F32), ALU.subtract).then_inc(hl_ready, 1)

                ahead(stage, 0, 0)
                ahead(stage, 0, 1)
                if stage in NORM:
                    row_factor(stage)
                gate(0, 0)
                up(0, 0)
                hidden(0, 0)
                gate(0, 1)
                ahead(stage, 0, 2)
                low_h(0, 0)
                up(0, 1)
                ahead(stage, 0, 3)
                hidden(0, 1)
                low_h(0, 1)
                with dve.Fori(1, 2 * FT // RING) as i:
                    gate(i, 0)
                    ahead(stage, i, 0)
                    up(i, 0)
                    ahead(stage, i, 1)
                    hidden(i, 0)
                    gate(i, 1)
                    ahead(stage, i, 2)
                    low_h(i, 0)
                    up(i, 1)
                    ahead(stage, i, 3)
                    hidden(i, 1)
                    low_h(i, 1)

            def embed(stage, gate, layer, kv):
                def gated_add(j):
                    t_ = gu[:, j % 4, :]
                    dve.wait_ge(sig_done, KT * layer + j + 1)
                    link(dve, dve_step, steps, dve.tensor_tensor(t_, t_, pj[:, j, :], ALU.mult))
                    dve.tensor_tensor(x[:, j, :], x[:, j, :], t_, ALU.add).then_inc(x_final, 1)

                for j in range(2):
                    ahead(stage, 0, j)
                    for m in range(4):
                        if m < 3:
                            dve.wait_ge(pj_done, 3 * (2 * layer + j) + m + 1)
                        else:
                            dve.wait_ge(unit_used, U0[stage] + j + 1 + RING)
                        dve.tensor_copy(pj[:, 4 * j + m, :], bank[(A0[stage] + 4 * j + m) % 4][:, 0:N]).then_inc(a_free, 1)
                ahead(gate, 0, 0)
                ahead(gate, 0, 1)
                row_factor(gate)
                for j in range(KT):
                    take(gu[:, j % 4, :], gate, j)
                    if j >= 2:
                        ahead(gate, 0, j)
                    if j > 0:
                        gated_add(j - 1)
                gated_add(KT - 1)
                if kv:
                    for m in range(KT):
                        low_kv(m)

            def low_kv(m):
                dve.wait_ge(kvh_ready, m + 1)
                dve.scalar_tensor_tensor(out=hl[:, m, :], in0=x[:, m, :], scalar=vs[:, G_KV + m:G_KV + m + 1],
                                         in1=hh[:, m, :].bitcast(F32), op0=ALU.mult, op1=ALU.subtract).then_inc(kvl_ready, 1)

            def low_p(layer):
                dve.wait_ge(ph_ready, layer + 1)
                dve.tensor_tensor(pl[:, :, :], gsq[:, :, :], ph[:, :, :].bitcast(F32), ALU.subtract).then_inc(pl_ready, 1)

            def head_norm(n_, tile, gain):
                w = aw[:, n_ % 2, :]
                dve.wait_ge(head_sum, n_ + 1)
                dve.tensor_scalar(w, bank[5][:, 0:N], 1.0 / 64, EPS, ALU.mult, ALU.add).then_inc(head_var, 1)
                dve.wait_ge(head_std, n_ + 1)
                link(dve, dve_step, steps, dve.reciprocal(w, w))
                dve.scalar_tensor_tensor(out=tile, in0=tile, scalar=vs[:, gain:gain + 1], in1=w, op0=ALU.mult, op1=ALU.mult).then_inc(head_n, 1)

            def rope(n_, tile):
                dve.wait_ge(rot_done, n_ + 1)
                dve.tensor_tensor(aw[:, 2, :], bank[6][:, 0:N], sinT, ALU.mult)
                link(dve, dve_step, steps, dve.tensor_tensor(tile, tile, cosT, ALU.mult))
                dve.tensor_tensor(tile, tile, aw[:, 2, :], ALU.add).then_inc(roped, 1)

            dve.sem_inc(a_free, 4)
            for u in range(RING):
                low_unit(*unit(0, 0, u))
            dve.wait_ge(init, 64)
            for m in range(KT):
                low_x(m, G_F1, 0)
            ffn_in("f1i0", "f1o0", 0)
            ahead_all("f1o0", FT)
            add_b("f1o0", FT, 0.5, G_MIX, "sin")
            dve.memset(xraw[:, :, 0:3], 0.0)
            dve.memset(avec[32:64, :], 1.0)
            ahead("sin", 0, 0)
            row_factor("sin")
            t_, e_, m_, r_, s_, s2_, a_ = (zs[0:64, k, :] for k in range(7))
            n_dt = [0]

            def dt_step(ins):
                link(dve, dt_d_step, n_dt, ins)

            dve.wait_ge(unit_used, U0["sin"] + 1 + RING)
            dve.tensor_tensor(t_, bank[A0["sin"] % 4][0:64, 0:N], rstd[0:64, :], ALU.mult).then_inc(a_free, 1)
            dve.wait_ge(a_free, A0["sin"] + 1 + 4)
            dt_step(dve.tensor_scalar(t_, t_, vs[0:64, V_DTB:V_DTB + 1], None, ALU.add))
            dt_step(dve.scalar_tensor_tensor(out=e_, in0=t_, scalar=-1.0, in1=t_, op0=ALU.mult, op1=ALU.min))
            dt_step(dve.tensor_scalar(m_, t_, 0.0, None, ALU.max))
            dve.wait_ge(dt_a_step, 2)
            dt_step(dve.tensor_scalar(r_, e_, 2.0, None, ALU.add))
            dt_step(dve.reciprocal(r_, r_))
            dt_step(dve.tensor_tensor(s_, e_, r_, ALU.mult))
            dt_step(dve.tensor_tensor(s2_, s_, s_, ALU.mult))
            dt_step(dve.tensor_scalar(a_, s2_, 1.0 / 17, None, ALU.mult))
            for k in (15, 13, 11, 9, 7, 5, 3):
                dt_step(dve.scalar_tensor_tensor(out=a_, in0=a_, scalar=1.0 / k, in1=s2_, op0=ALU.add, op1=ALU.mult))
            dt_step(dve.scalar_tensor_tensor(out=a_, in0=a_, scalar=1.0, in1=s_, op0=ALU.add, op1=ALU.mult))
            dt_step(dve.scalar_tensor_tensor(out=a_, in0=a_, scalar=2.0, in1=m_, op0=ALU.mult, op1=ALU.add))
            link(dve, dve_step, steps, dve.tensor_scalar(avec[0:32, :], avec[0:32, :], -1.0, None, ALU.mult))
            dt_step(dve.tensor_scalar(dd, a_, avec[0:64, :], None, ALU.mult))
            assert n_dt[0] == DT_STEPS

            def conv_in(i, p, j):
                tile = i * 4 + p
                if not isinstance(i, int):
                    i_ = i - 1
                    dst = decraw[:, bass.ds(tile, 1), :].rearrange("p a n -> p (a n)")
                else:
                    i_ = 0
                    dst = decraw[:, tile, :]
                take(xraw[:, p, 3:259], "sin", j, i_, slice(0, T), signal=False).then_inc(conv_raw, 1)
                take(dst, "sin", j, i_, slice(T, N))

            def conv_taps(i, p):
                tile = i * 4 + p
                fixed = isinstance(i, int)
                out = xact[:, p, 0:T] if fixed else xact[:, bass.ds(tile, 1), 0:T].rearrange("p a n -> p (a n)")
                tl = tail[:, p, :] if fixed else tail[:, bass.ds(tile, 1), :].rearrange("p a n -> p (a n)")
                dve.wait_ge(conv_first, tile + 1)
                dve.tensor_copy(tl, xraw[:, p, T:T + 3])
                for k in range(3):
                    w = vs[:, V_CW + CT * k + p:V_CW + CT * k + p + 1] if fixed else vs[:, bass.ds(tile + (V_CW + CT * k), 1)]
                    if k > 0:
                        dve.wait_ge(conv_sum, tile * 3 + k)
                    dve.scalar_tensor_tensor(out=out, in0=xraw[:, p, k:k + T], scalar=w, in1=out, op0=ALU.mult, op1=ALU.add).then_inc(conv_sum, 1)

            def conv_body(i, j0):
                for p in range(4):
                    conv_in(i, p, j0 + p)
                    if p == 3:
                        conv_taps(i, p)
                    ahead("sin", *((0, j0 + p) if isinstance(i, int) else (i - 1, j0 + p)))
                    if p < 3:
                        conv_taps(i, p)

            conv_body(0, 1)
            with dve.Fori(1, CT // 4) as i:
                conv_body(i, 5)
            cw_ = lambda k: vs[:, V_CW + CT * k:V_CW + CT * k + CT].unsqueeze(2).to_broadcast([P, CT, SEQS])
            link(dve, dve_step, steps, dve.tensor_tensor(csum, decraw[:, :, :], cw_(3), ALU.mult))
            link(dve, dve_step, steps, dve.tensor_tensor(csum, csum, vs[:, V_CB:V_CB + CT].unsqueeze(2).to_broadcast([P, CT, SEQS]), ALU.add))
            for k in range(3):
                link(dve, dve_step, steps, dve.tensor_tensor(cwork, convs[:, :, k, :], cw_(k), ALU.mult))
                ins = dve.tensor_tensor(csum, csum, cwork, ALU.add)
                if k < 2:
                    link(dve, dve_step, steps, ins)
            ins.then_inc(dec_sum, 1)
            dve.wait_ge(pre_p, 1)
            dve.tensor_copy(small[:, N:N + 128], bank[5][:, 0:128]).then_inc(pre_d, 1)
            for k in (0, 32):
                ins = dve.tensor_tensor(dgl[k:k + 32], ident[k:k + 32, k:k + 32].unsqueeze(1).to_broadcast([32, SEQS, HEADS]),
                                        dd[k:k + 32, T:N].unsqueeze(2).to_broadcast([32, SEQS, HEADS]), ALU.mult)
            ins.then_inc(pre_d, 1)
            dve.wait_ge(dec_act, 1)
            dve.tensor_copy(b_d[:, :, :], xact[:, 16:24, T:N])
            link(dve, dve_step, steps, dve.tensor_copy(c_d[:, :, :], xact[:, 24:32, T:N]))
            dve.tensor_tensor(bc_d[:, :, :], b_d[:, :, :], c_d[:, :, :], ALU.mult).then_inc(pre_d, 1)
            dve.wait_ge(pre_p, 2)
            for c in range(2):
                link(dve, dve_step, steps, dve.tensor_copy(cumT[c], bank[7][0:32, 128 * c:128 * c + 128]))
                ins = dve.tensor_scalar(ncumT[c], cumT[c], -1.0, None, ALU.mult).then_inc(pre_d, 1)
            cum_ps = bank[6][:, 0:128].rearrange("p (c k h) -> p c k h", c=2, k=2)
            dve.tensor_copy(tok[:, :, 0, :], cum_ps[:, :, 0, :])
            link(dve, dve_step, steps, dve.tensor_copy(tok[:, :, 2, :], cum_ps[:, :, 1, :]))
            dve.tensor_tensor(tok[:, :, 1, :], tok[:, :, 2, :], tok[:, :, 0, :], ALU.subtract).then_inc(pre_d, 1)
            for b in range(2):
                hs = slice(64 * b, 64 * b + 64)
                spread = lambda ps: ps[hs].rearrange("p (s k b) -> p b k s", s=SEQS, b=2)[:, b]
                dve.tensor_copy(da_d[hs, :, :], spread(bank[6][:, 128:384]))
                ins = dve.tensor_copy(dt_d[hs, :, :], spread(bank[4][:, 0:256]))
            link(dve, dve_step, steps, ins)
            dve.tensor_tensor(dtx_d[:, :, :], xact[:, 0:16, T:N], dt_d[:, :, :], ALU.mult).then_inc(pre_d, 1)
            dve.tensor_copy(bc_d[:, :, :], bank[5][:, 128:192])
            dve.tensor_copy(da_bc[:, :, :], bank[6][:, 128:384]).then_inc(pre_d, 1)
            dve.wait_ge(pre_p, 3)
            dve.wait_ge(conv_out, 48)
            for k in range(4):
                ins = dve.tensor_copy(dtxt[:, 512 * k:512 * k + 512], bank[4 + k][0:SEQS, :])
            ins.then_inc(pre_d, 1)

            def decode_y():
                dve.wait_ge(h0_used, 8)
                dve.wait_ge(pre_a, 2)
                link(dve, dve_step, steps, dve.tensor_tensor(t1d[:, :, :], bank[4][:, 0:128].rearrange("p (k s) -> p k s", k=XT), da_d[:, :, :], ALU.mult))
                link(dve, dve_step, steps, dve.tensor_tensor(dt_d[:, :, :].rearrange("p (g t) s -> p g t s", g=G), bc_d[:, :, :].unsqueeze(2).to_broadcast([P, G, 2, SEQS]),
                                                             dtx_d[:, :, :].rearrange("p (g t) s -> p g t s", g=G), ALU.mult))
                link(dve, dve_step, steps, dve.tensor_tensor(t1d[:, :, :], t1d[:, :, :], dt_d[:, :, :], ALU.add))
                xd = xact[:, 0:XT, T:N]
                link(dve, dve_step, steps, dve.tensor_tensor(xd, xd, vs[:, V_D:V_D + XT].unsqueeze(2).to_broadcast([P, XT, SEQS]), ALU.mult))
                dve.tensor_tensor(xd, xd, t1d[:, :, :], ALU.add).then_inc(y_dec, 1)

            def group_step(g, c):
                k_ = 2 * g + c
                r = slice(128 * c, 128 * c + 128)
                base = gd_base(g, c)
                n_ = [0]

                def step(ins):
                    ins.then_inc(gd, 1)
                    n_[0] += 1

                def by_head(a):
                    return a.rearrange("p (h w) -> p h w", h=4)

                def heads(a):
                    return a.unsqueeze(2).to_broadcast([P, 4, 64])

                dve.wait_ge(gp, 4 * k_ + 1)
                step(dve.tensor_tensor(cbm, bank[4][:, 0:128], tri, ALU.mult))
                step(dve.tensor_tensor(by_head(xdt), by_head(bank[4][:, 128:384]), heads(ddT[c][:, 32 + 4 * g:36 + 4 * g]), ALU.mult))
                step(dve.tensor_copy(btok, bank[4][:, 384:512]))
                dve.wait_ge(gd, base + 2)
                dve.wait_ge(pre_a, 1)
                step(dve.tensor_tensor(by_head(xte), by_head(xdt), heads(tok[:, c, 1, 4 * g:4 * g + 4]), ALU.mult))
                dve.wait_ge(gp, 4 * k_ + 2)
                step(dve.tensor_scalar(Dm, bank[5][:, 0:512], 0.0, None, ALU.min))
                dve.wait_ge(ga, k_ + 1)
                step(dve.tensor_tensor(by_head(Mm), by_head(Dm), cbm.unsqueeze(1).to_broadcast([P, 4, 128]), ALU.mult))
                dve.wait_ge(gp, 4 * k_ + 3)
                if c == 0:
                    step(dve.tensor_copy(ytok, bank[6][:, 0:256]))
                    step(dve.tensor_copy(h1, bank[7][:, 0:256]))
                else:
                    step(dve.tensor_tensor(by_head(ytok), by_head(bank[6][:, 256:512]), heads(tok[:, 1, 0, 4 * g:4 * g + 4]), ALU.mult))
                    dve.wait_ge(gd, base + 7)
                    step(dve.tensor_tensor(ytok, ytok, bank[6][:, 0:256], ALU.add))
                    step(dve.tensor_tensor(by_head(h1), by_head(h1), heads(tok[:, 1, 2, 4 * g:4 * g + 4]), ALU.mult))
                    dve.wait_ge(gd, base + 9)
                    if g >= 2:
                        dve.wait_ge(st_out[g % 2], 16 * (g // 2))
                    step(dve.tensor_tensor(state[:, g % 2, :], h1, bank[7][:, 0:256], ALU.add))
                dve.wait_ge(gp, 4 * k_ + 4)
                for n2 in range(2):
                    xt_ = xact[:, 2 * g + n2, r]
                    step(dve.scalar_tensor_tensor(out=xt_, in0=xt_, scalar=vs[:, V_D + 2 * g + n2:V_D + 2 * g + n2 + 1],
                                                  in1=bank[7][:, 256 + 128 * n2:384 + 128 * n2], op0=ALU.mult, op1=ALU.add))
                assert n_[0] == gd_base(g, c + 1) - base if c == 0 else n_[0] == 12

            for s_ in range(XT + 1):
                if s_ == 8:
                    dve.wait_ge(dtx_out, 16)
                if s_ < XT:
                    take(zs[:, s_, :], "sin", 33 + s_)
                if s_ < XT:
                    ahead("sin", 0, 33 + s_)
                if s_ == 4:
                    decode_y()
                if 4 <= s_ < 12:
                    group_step(s_ - 4, 0)
                    group_step(s_ - 4, 1)
                if s_ >= 9:
                    g = s_ - 9
                    dve.wait_ge(z_silu, 1 if g < 4 else g - 2)
                    dve.wait_ge(gd, 22 * (g + 1))
                    dve.tensor_tensor(zs[:, 2 * g:2 * g + 2, :], zs[:, 2 * g:2 * g + 2, :], xact[:, 2 * g:2 * g + 2, :], ALU.mult).then_inc(gated, 1)
                    dve.wait_ge(gated_sum, g + 1)
                    dve.tensor_scalar(xact[:, 2 * g, :], bank[5][:, 0:N], 1.0 / 256, EPS, ALU.mult, ALU.add).then_inc(gated_var, 1)
                    if g % 4 == 3:
                        dve.wait_ge(gated_std, g // 4 + 1)
                        v_ = xact[:, 2 * g - 6:2 * g + 1:2, :]
                        link(dve, dve_step, steps, dve.reciprocal(v_, v_))

                        def low_z(t):
                            dve.wait_ge(hh_ready, HREADY["sout"] + t + 1)
                            dve.tensor_tensor(hl[:, t, :], zs[:, t, :], hh[:, t, :].bitcast(F32), ALU.subtract).then_inc(hl_ready, 1)

                        for t in range(2 * g - 6, 2 * g + 2):
                            dve.scalar_tensor_tensor(out=zs[:, t, :], in0=zs[:, t, :], scalar=vs[:, V_NG + t:V_NG + t + 1],
                                                     in1=xact[:, t // 2 * 2, :], op0=ALU.mult, op1=ALU.mult).then_inc(gn_ready, 1)
                            if t > 2 * g - 6:
                                low_z(t - 1)
                        low_z(2 * g + 1)
            ahead_all("sout", XT)
            add_b("sout", XT, 1.0, G_F2, "f2i0")
            ffn_in("f2i0", "f2o0", 1)
            low_p(0)
            ahead_all("f2o0", FT)
            add_b("f2o0", FT, 0.5, G_PLE, "pg0")
            embed("pp0", "pg0", 0, True)
            for m in range(KT):
                low_x(m, G_F1 + 8, XREADY["f1i1"])
            ahead("kv", 0, 0)
            ahead("kv", 0, 1)
            row_factor("kv")
            take(kf[:, 0, :], "kv", 0)
            take(kf[:, 1, :], "kv", 1)
            ahead("kv", 0, 2)
            ahead("kv", 0, 3)
            take(vf[:, 0, :], "kv", 2)
            take(vf[:, 1, :], "kv", 3)
            for n_ in range(2):
                head_norm(n_, kf[:, n_, :], V_KN)
            for n_ in range(2):
                rope(n_, kf[:, n_, :])
            dve.wait_ge(v_tr, 1)
            dve.tensor_copy(vtok, bank[7][:, :].rearrange("p (c n) -> p c n", c=2)).then_inc(v_tok, 1)
            ffn_in("f1i1", "f1o1", 2)
            ahead_all("f1o1", FT)
            add_b("f1o1", FT, 0.5, G_MIX + 8, "q")
            ahead("q", 0, 0)
            ahead("q", 0, 1)
            row_factor("q")
            for t in range(KT + 2):
                if t < KT:
                    take(qf[:, t, :], "q", t)
                if 1 <= t <= KT:
                    head_norm(2 + t - 1, qf[:, t - 1, :], V_QN)
                if t >= 2:
                    rope(2 + t - 2, qf[:, t - 2, :])
                if 2 <= t < KT:
                    ahead("q", 0, t)
            dve.wait_ge(dec_p, 1)
            dve.wait_ge(roped, 10)
            dve.tensor_copy(sTd[:, 0:64], bank[4][:, 0:64])
            dve.tensor_copy(sTd[:, 64:128], bank[5][:, 0:64]).then_inc(dec_d, 1)
            dve.tensor_tensor(prod.rearrange("p (a b) -> p a b", a=2)[:, 0, :].rearrange("p (s k i) -> p s k i", s=SEQS, k=2),
                              qf[:, :, T:N].rearrange("p (k i) s -> p s k i", k=2),
                              kf[:, :, T:N].rearrange("p k s -> p s k").unsqueeze(3).to_broadcast([P, SEQS, 2, 4]), ALU.mult).then_inc(dec_d, 1)
            dve.wait_ge(dec_p, 2)
            dve.tensor_scalar(dS[:, 0:128], bank[6][:, 0:128], SCALE, None, ALU.mult)
            dve.tensor_scalar(dS[0:64, 128:129], bank[6][0:64, 128:129], SCALE, None, ALU.mult)
            link(dve, dve_step, steps, dve.tensor_scalar(dS[64:128, 128:129], bank[7][64:128, 0:1], SCALE, None, ALU.mult))
            link(dve, dve_step, steps, dve.tensor_reduce(dm[:, 0:1], dS, AX.X, ALU.max))
            link(dve, dve_step, steps, dve.tensor_scalar(dm[:, 0:1], dm[:, 0:1], vs[:, V_SINKD:V_SINKD + 1], None, ALU.max))
            dve.tensor_scalar(dm[:, 1:2], dm[:, 0:1], -1.0, None, ALU.mult).then_inc(dec_a_go, 1)
            dve.wait_ge(dec_a, 1)
            link(dve, dve_step, steps, dve.tensor_tensor(dm[:, 4:5], dm[:, 2:3], dm[:, 3:4], ALU.add))
            link(dve, dve_step, steps, dve.reciprocal(dm[:, 4:5], dm[:, 4:5]))
            link(dve, dve_step, steps, dve.tensor_scalar(dP, dP, dm[:, 4:5], None, ALU.mult))
            dve.tensor_scalar(dgP, ident, dP[:, 128:129], None, ALU.mult).then_inc(dec_d, 1)
            dve.wait_ge(dec_p, 3)
            dve.tensor_copy(pTd, bank[6][:, 0:128]).then_inc(dec_d, 1)
            dve.wait_ge(dec_p, 4)
            for b in range(2):
                hs = slice(64 * b, 64 * b + 64)
                od3 = od[hs, :].rearrange("p (s k i) -> p s k i", s=SEQS, k=2)
                link(dve, dve_step, steps, dve.tensor_tensor(od3, bank[5][hs, 64 * b:64 * b + 64].rearrange("p (s k i) -> p s k i", s=SEQS, k=2),
                                                             vf[hs, :, T:N].rearrange("p k s -> p s k").unsqueeze(3).to_broadcast([64, SEQS, 2, 4]), ALU.mult))
                ins = dve.tensor_tensor(o32[hs, :, T:N].rearrange("p (k i) s -> p s k i", k=2), od3,
                                        bank[4][hs, 0:64].rearrange("p (s k i) -> p s k i", s=SEQS, k=2), ALU.add)
            ins.then_inc(dec_d, 1)

            def maxima(e):
                b = e % 2
                dve.wait_ge(s_done, e + 1)
                link(dve, dve_step, steps, dve.scalar_tensor_tensor(out=sm[:, b, :], in0=bank[4 + b][:, 0:384], scalar=SCALE, in1=mask, op0=ALU.mult, op1=ALU.add))
                dve.tensor_reduce(mx[:, 2 * b:2 * b + 1], sm[:, b, 0:128], AX.X, ALU.max)
                link(dve, dve_step, steps, dve.tensor_reduce(mx[:, 2 * b + 1:2 * b + 2], sm[:, b, 128:384], AX.X, ALU.max))
                link(dve, dve_step, steps, dve.tensor_scalar(mx[:, 2 * b:2 * b + 2], mx[:, 2 * b:2 * b + 2], vs[:, V_SINK + e:V_SINK + e + 1], None, ALU.max))
                dve.tensor_scalar(nmx[:, 2 * b:2 * b + 2], mx[:, 2 * b:2 * b + 2], -1.0, None, ALU.mult).then_inc(s_max, 1)

            maxima(0)
            for e in range(AH):
                t, b = e // 2, e % 2
                hs = slice(64 * b, 64 * b + 64)
                if e + 1 < AH:
                    maxima(e + 1)
                dve.wait_ge(s_exp, e + 1)
                link(dve, dve_step, steps, dve.tensor_tensor(rr[:, 2 * b:2 * b + 2], rs[:, 2 * b:2 * b + 2], es[:, 2 * b:2 * b + 2], ALU.add))
                link(dve, dve_step, steps, dve.reciprocal(rr[:, 2 * b:2 * b + 2], rr[:, 2 * b:2 * b + 2]))
                dve.tensor_scalar(sm[:, b, 0:128], sm[:, b, 0:128], rr[:, 2 * b:2 * b + 1], None, ALU.mult)
                dve.tensor_scalar(sm[:, b, 128:384], sm[:, b, 128:384], rr[:, 2 * b + 1:2 * b + 2], None, ALU.mult).then_inc(s_prob, 1)
                dve.wait_ge(p_tr, e + 1)
                dve.tensor_copy(pT_[:, b, :], bank[6][:, 0:384]).then_inc(p_read, 1)
                dve.wait_ge(pv_done, e + 1)
                dve.tensor_copy(o32[hs, t, 0:T], bank[7][hs, 0:T]).then_inc(o_read, 1)
            for t in range(KT):
                dve.wait_ge(hh_ready, HREADY["o"] + t + 1)
                dve.tensor_tensor(hl[:, t, :], o32[:, t, :], hh[:, t, :].bitcast(F32), ALU.subtract).then_inc(hl_ready, 1)
            ahead_all("o", 8)
            add_b("o", 8, 1.0, G_F2 + 8, "f2i1")
            ffn_in("f2i1", "f2o1", 3)
            low_p(1)
            ahead_all("f2o1", FT)
            add_b("f2o1", FT, 0.5, G_PLE + 8, "pg1")
            embed("pp1", "pg1", 1, False)

        @block.gpsimd
        def _(pool):
            steps = [0]
            pool.dma_start(k_old, ck).then_inc(old_out, 16)
            pool.dma_start(v_old, cv).then_inc(old_out, 16)
            pool.wait_ge(dec_sum, 1)
            pool.wait_ge(conv_sum, 3 * CT)
            pool.dma_start(conv_p, tail[:, :, :]).then_inc(conv_out, 16)
            pool.dma_start(conv_s[:, :, 0:2, :], convs[:, :, 1:3, :]).then_inc(conv_out, 16)
            pool.dma_start(conv_s[:, :, 2, :], decraw[:, :, :]).then_inc(conv_out, 16)
            pool.wait_ge(conv_out, 48)
            pool.wait_ge(sums_done, 2)
            pool.dma_start(h0buf[0], ssm0[0]).then_inc(h0_landed[0], 16)
            pool.wait_ge(pre_d, PRE_D + 1)
            pool.dma_start(dtx_rows, dtxt).then_inc(dtx_out, 16)
            pool.wait_ge(dtx_out, 16)
            for q in range(1, SEQS):
                if q >= 2:
                    pool.wait_ge(h0_used, q - 1)
                pool.dma_start(h0buf[q % 2], ssm0[q]).then_inc(h0_landed[q % 2], 16)
            for g in range(G):
                pool.wait_ge(gd, gd_base(g, 1) + 10)
                pool.dma_start(ssm_p[:, 256 * g:256 * g + 256], state[:, g % 2, :]).then_inc(st_out[g % 2], 16)
            pool.wait_ge(pre_a, 3)
            pool.wait_ge(gd, 22 * G)
            for q in range(SEQS):
                if q > 0:
                    pool.wait_ge(late_out, 16 * q)
                pool.dma_start(lateA, ssm0[q]).then_inc(late_in[0], 16)
                pool.dma_start(lateB, dtx_rows[q:q + 1, :].to_broadcast([P, XT * P])).then_inc(late_in[1], 16)
                pool.wait_ge(late_in[0], 16 * (q + 1))
                pool.tensor_tensor(lateA.rearrange("p (h w) -> p h w", h=HEADS), lateA.rearrange("p (h w) -> p h w", h=HEADS),
                                   da_bc[:, q, :].unsqueeze(2).to_broadcast([P, HEADS, 64]), ALU.mult)
                pool.wait_ge(late_in[1], 16 * (q + 1))
                link(pool, pool_step, steps, pool.tensor_tensor(lateB.rearrange("p (g w) -> p g w", g=G), lateB.rearrange("p (g w) -> p g w", g=G),
                                                                b_d[:, :, q].unsqueeze(2).to_broadcast([P, G, 256]), ALU.mult))
                link(pool, pool_step, steps, pool.tensor_tensor(lateA, lateA, lateB, ALU.add))
                pool.dma_start(ssm_s[q], lateA).then_inc(late_out, 16)
            pool.wait_ge(late_out, 16 * SEQS)
            pool.wait_ge(gn_ready, XT)
            pool.dma_start(kc, kcT).then_inc(cache_in, 16)
            pool.dma_start(vc, vc_in).then_inc(cache_in, 16)
            pool.wait_ge(roped, 2)
            pool.wait_ge(v_tok, 1)
            pool.dma_start(kv_p[0], kf[:, :, 128:256]).then_inc(kv_out, 16)
            pool.dma_start(kv_p[1], vf[:, :, 128:256]).then_inc(kv_out, 16)
            pool.dma_start(kv_new[0], kf[:, :, T:N]).then_inc(kv_out, 16)
            pool.dma_start(kv_new[1], vf[:, :, T:N]).then_inc(kv_out, 16)
            pool.wait_ge(kv_out, 64)
            pool.wait_ge(old_out, 32)
            for b in range(2):
                pool.wait_ge(st_out[b], 16 * G // 2)


def in_a(w):
    m = w.shape[1] // P
    return w.reshape(KT, P, m, P).transpose(2, 1, 0, 3).reshape(m, P, UNIT)


def ffn_units(wi):
    return in_a(wi).reshape(2, FT, P, UNIT).transpose(1, 0, 2, 3).reshape(2 * FT, P, UNIT)


def in_b(w):
    return w.reshape(-1, P, UNIT)


def proj_units(w):
    return w.reshape(2, P, 2, 4, P).transpose(2, 1, 3, 0, 4).reshape(2, P, UNIT)


def columns(v):
    return v.reshape(-1, P).T


def constants():
    c = np.zeros((P, NC_), np.float32)
    k, m = np.arange(P)[:, None], np.arange(P)[None, :]
    c[:, C_ID:C_ID + P] = k == m
    c[:, C_TRI:C_TRI + P] = k <= m
    c[:, C_ONE:C_ONE + P] = 1
    c[:, C_BLK:C_BLK + P] = k // 64 == m // 64
    c[:, C_ROT:C_ROT + P] = 1.0 * ((k == m - 32) & (m % 64 >= 32)) - 1.0 * ((k == m + 32) & (m % 64 < 32))
    pos = np.concatenate([np.arange(T), np.full(SEQS, 1024)]).astype(np.float32)
    inv = np.float32(10000.0) ** (-np.arange(32, dtype=np.float32) / np.float32(32))
    ang = (pos[None, :] * inv[:, None]).astype(np.float32)[np.arange(P) % 32]
    c[:, C_COS:C_COS + N] = np.cos(ang)
    c[:, C_SIN:C_SIN + N] = np.sin(ang)
    far = np.float32(-1e30)
    c[:, C_MASK:C_MASK + 128] = np.where(m <= k, 0, far)
    c[:, C_MASK + 128:C_MASK + 256] = np.where(m >= k, 0, far)
    c[:, C_MASK + 256:C_MASK + 384] = np.where(m <= k, 0, far)
    return c


def kernel(**inputs):
    import concourse.bacc as bacc
    from concourse.bass_utils import run_bass_kernel_spmd

    a = {k: np.asarray(v) for k, v in inputs.items()}
    perm = [(2 * (t // 4) + b) * 4 + t % 4 for t in range(KT) for b in range(2)]
    ssm_in = a["ssm_in"][0]
    weights = np.concatenate([
        ffn_units(a["ffn1_wi"][0]), in_b(a["ffn1_wo"][0]),
        in_a(np.tile(ssm_in[:, 6144:6176], (1, 4))), in_a(ssm_in[:, 2048:6144]), in_a(ssm_in[:, 0:2048]),
        in_b(a["ssm_out"][0]),
        ffn_units(a["ffn2_wi"][0]), in_b(a["ffn2_wo"][0]), proj_units(a["ple_proj"][0]), in_a(a["ple_gate"][0]),
        in_a(a["w_kv"]),
        ffn_units(a["ffn1_wi"][1]), in_b(a["ffn1_wo"][1]),
        in_a(a["w_q"][0].reshape(D, AH, 64)[:, perm].reshape(D, D)), in_b(a["w_o"][0].reshape(AH, 64, D)[perm].reshape(D, D)),
        ffn_units(a["ffn2_wi"][1]), in_b(a["ffn2_wo"][1]), proj_units(a["ple_proj"][1]), in_a(a["ple_gate"][1]),
    ])
    assert weights.shape == (NU, P, UNIT)
    rows = lambda p, s: np.concatenate([p, s])
    fm = lambda r: r.T.reshape(-1, P, r.shape[0]).transpose(1, 0, 2)
    xT = fm(rows(a["x_prompt"][0], a["x_sample"][:, 0]))
    pT = np.stack([fm(rows(a["p_prompt"][l, 0], a["p_sample"][l, :, 0])) for l in range(2)])
    v = [columns(a[n][l]) for n in ("ffn1_norm", "mix_norm", "ffn2_norm", "ple_norm") for l in range(2)] + [columns(a["kv_norm"])]
    v += [columns(a["ssm_conv_w"][0, k]) for k in range(4)] + [columns(a["ssm_conv_b"][0])]
    v += [columns(np.repeat(a["ssm_d"][0], 64)), columns(a["ssm_norm"][0])]
    v += [np.tile(a["ssm_a_log"][0], 4)[:, None], np.tile(a["ssm_dt_bias"][0], 4)[:, None]]
    v += [np.tile(a["k_norm"], 2)[:, None], np.tile(a["q_norm"][0], 2)[:, None]]
    sinks = a["attn_sinks"][0]
    v += [sinks[[(2 * kp + b) * 4 + i for b in range(2) for _ in range(SEQS) for kp in range(2) for i in range(4)]][:, None]]
    v += [np.broadcast_to(sinks[perm][None, :], (P, AH))]
    vec = np.concatenate(v, axis=1)
    assert vec.shape == (P, NV)
    convst = a["state_conv"][0].reshape(SEQS, 3, CT, P).transpose(3, 2, 1, 0)
    ssm0 = a["state_ssm"][0].transpose(0, 3, 1, 2).reshape(SEQS, P, XT * P)
    ck = a["cache_k"].reshape(SEQS, WINDOW, 256)
    cv = a["cache_v"].reshape(SEQS, WINDOW, 256)
    kcT = a["cache_k"].reshape(SEQS, WINDOW, 2, 2, 64).transpose(3, 4, 2, 0, 1).reshape(P, 2, SEQS, WINDOW)
    vcT = cv.transpose(1, 0, 2)

    nc = bacc.Bacc("TRN2", target_bir_lowering=False, num_devices=1)
    arrays = {"weights": weights, "xT": xT, "pT": pT, "cst": constants(), "vec": vec, "convst": convst, "ssm0": ssm0,
              "kcT": kcT, "vcT": vcT, "ck": ck, "cv": cv}
    arrays = {k: np.ascontiguousarray(v_) for k, v_ in arrays.items()}
    ins = {k: nc.dram_tensor(k, v_.shape, mybir.dt.from_np(v_.dtype), kind="ExternalInput").ap() for k, v_ in arrays.items()}
    shapes = {"y": (P, KT, N), "ssm_p": (P, 2048), "conv_p": (P, CT, 3), "kv_p": (2, P, 2, 128), "ssm_s": (SEQS, P, 2048),
              "conv_s": (P, CT, 3, SEQS), "k_old": (SEQS, WINDOW - 1, 256), "v_old": (SEQS, WINDOW - 1, 256), "kv_new": (2, P, 2, SEQS)}
    outs = {k: nc.dram_tensor("out_" + k, s, F32, kind="ExternalOutput").ap() for k, s in shapes.items()}
    i = ins
    trunk_kernel(nc, i["weights"], i["xT"], i["pT"], i["cst"], i["vec"], i["convst"], i["ssm0"], i["kcT"], i["vcT"],
                 i["ck"][:, 1:, :], i["cv"][:, 1:, :], *outs.values())
    r = run_bass_kernel_spmd(nc, [arrays], core_ids=[0]).results[0]
    o = {k: np.asarray(r["out_" + k]) for k in shapes}

    y = o["y"].transpose(2, 1, 0).reshape(N, D)
    ssm_p = o["ssm_p"].reshape(P, HEADS, 64).transpose(1, 2, 0)[None, None]
    conv_p = o["conv_p"].transpose(2, 1, 0).reshape(1, 1, 3, CT * P)
    heads = lambda t: t.reshape(2, 64, 2, -1).transpose(3, 2, 0, 1).reshape(-1, 4, 64)
    k_p, v_p = heads(o["kv_p"][0])[None], heads(o["kv_p"][1])[None]
    ssm_s = o["ssm_s"].reshape(SEQS, P, HEADS, 64).transpose(0, 2, 3, 1)[None]
    conv_s = o["conv_s"].transpose(3, 2, 1, 0).reshape(1, SEQS, 3, CT * P)
    k_s, v_s = (np.concatenate([o[n].reshape(SEQS, WINDOW - 1, 4, 64), heads(o["kv_new"][j])[:, None]], axis=1)
                for j, n in enumerate(("k_old", "v_old")))
    return (y[None, :T], y[T:][:, None], ssm_p, conv_p, k_p, v_p, ssm_s, conv_s, k_s, v_s)
```

```python
from contextlib import ExitStack

import numpy as np

import concourse.bass as bass
from concourse import mybir

F32 = mybir.dt.float32
F32R = mybir.dt.float32r
ACT = mybir.ActivationFunctionType
ALU = mybir.AluOpType
AX = mybir.AxisListType

P = 128
D = 1024
KT = D // P
T = 256
SEQS = 8
N = T + SEQS
FT = 2816 // P
EPS = 1e-6
HEADS = 32
XT = 16
G = 8
CT = 32
WINDOW = 128
AH = 16
RING = 4
UNIT = KT * P
SCALE = 64 ** -0.5

STAGES = [("f1i0", 2 * FT), ("f1o0", FT), ("sin", 49), ("sout", XT), ("f2i0", 2 * FT), ("f2o0", FT), ("pp0", 2), ("pg0", 8),
          ("kv", 4), ("f1i1", 2 * FT), ("f1o1", FT), ("q", 8), ("o", 8), ("f2i1", 2 * FT), ("f2o1", FT), ("pp1", 2), ("pg1", 8)]
NU = sum(n for _, n in STAGES)
U0 = {}
for _name, _n in STAGES:
    U0[_name] = sum(n for _, n in STAGES[:len(U0)])
A0, _a = {}, 0
for _name, _n in STAGES:
    A0[_name] = _a
    if not (_name[:3] in ("f1o", "f2o") or _name in ("sout", "o")):
        _a += 4 * _n if _name[:2] == "pp" else _n
A0["end"] = _a
BSTAGE = {"f1o0": 0, "sout": 1, "f2o0": 2, "f1o1": 3, "o": 4, "f2o1": 5}
NORM = {"f1i0": 0, "sin": 1, "f2i0": 2, "pg0": 3, "kv": 4, "q": 5, "f2i1": 6, "pg1": 7}
XREADY = {"f1i0": 0, "sin": 8, "f2i0": 16, "pg0": 24, "f1i1": 32, "q": 40, "f2i1": 48, "pg1": 56}
HREADY = {"f1o0": 0, "sout": FT, "f2o0": FT + XT, "f1o1": 2 * FT + XT, "o": 3 * FT + XT, "f2o1": 3 * FT + XT + 8}

C_ID, C_TRI, C_ONE, C_BLK, C_ROT, C_COS, C_SIN, C_MASK = 0, 128, 256, 384, 512, 640, 640 + N, 640 + 2 * N
C_IND, C_SEL = C_MASK + 384, C_MASK + 388
NC_ = C_SEL + G
G_F1, G_MIX, G_F2, G_PLE, G_KV = 0, 16, 32, 48, 64
V_CW, V_CB, V_D, V_NG, V_ALOG, V_DTB, V_KN, V_QN, V_SINKD, V_SINK = 72, 200, 232, 248, 264, 265, 266, 267, 268, 269
NV = 269 + AH


DT_STEPS = 18
CHUNK0 = 3
H0_AT = 2
NORM_AT = [11, 12, 13, 14, 16, 17, 19, 21]
SLOTS = NORM_AT[-1] + 1


def unit(base, i, j):
    return base + j + 4 * i, (base + j) // RING + i, (base + j) % RING


def trunk_kernel(nc, weights, xT, pT, cst, vec, convst, ssm0, kcT, vc_in, ck, cv,
                 y_out, ssm_p, conv_p, kv_p, ssm_s, conv_s, k_old, v_old, kv_new):
    dtx_rows = nc.dram_tensor("dtx_rows", (SEQS, XT * P), F32, kind="Internal").ap()
    with ExitStack() as ctx:
        def sb(name, shape, dt=F32):
            return ctx.enter_context(nc.sbuf_tensor(name, shape, dt))

        def sem(name):
            return ctx.enter_context(nc.semaphore(name))

        raw = sb("raw", [P, RING, UNIT])
        whi = sb("whi", [P, RING, UNIT], F32R)
        wlo = sb("wlo", [P, RING, UNIT], F32R)
        x = sb("x", [P, KT, N])
        xh = sb("xh", [P, KT, N], F32R)
        xl = sb("xl", [P, KT, N], F32R)
        sq = sb("sq", [P, KT * N])
        with nc.sbuf_tensor("h0", [P, 4, XT * P], F32) as h0buf_:
            h0buf = [h0buf_[:, b, :] for b in range(4)]
        hh = sb("hh", [P, FT, N], F32R)
        hl = sb("hl", [P, FT, N], F32R)
        xact = sb("xact", [P, CT, N])
        zs = sb("zs", [P, XT, N])
        ph = sb("ph", [P, 2, N], F32R)
        pl = sb("pl", [P, 2, N], F32R)
        gu = sb("gu", [P, 4, N])
        rstd = sb("rstd", [P, N])
        cs = sb("cs", [P, NC_])
        vs = sb("vs", [P, NV])
        avec = sb("avec", [P, 1])
        gsq = sb("gsq", [P, 2, N])
        small = sb("small", [P, 1024])
        bank = [ctx.enter_context(nc.psum_tensor(f"bank{b}", [P, 512], F32)) for b in range(8)]

        ident, tri, ones = cs[:, C_ID:C_ID + P], cs[:, C_TRI:C_TRI + P], cs[:, C_ONE:C_ONE + P]
        blk, rot = cs[:, C_BLK:C_BLK + P], cs[:, C_ROT:C_ROT + P]
        cosT, sinT, mask = cs[:, C_COS:C_COS + N], cs[:, C_SIN:C_SIN + N], cs[:, C_MASK:C_MASK + 384]
        sq3 = sq[:, :].rearrange("p (k n) -> p k n", k=KT)

        raw_landed = [sem(f"raw_landed{s}") for s in range(RING)]
        hi_ready = sem("hi_ready")
        lo_ready = sem("lo_ready")
        unit_used = sem("unit_used")
        a_free = sem("a_free")
        b_done = sem("b_done")
        b_free = sem("b_free")
        xh_ready = sem("xh_ready")
        xl_ready = sem("xl_ready")
        sq_ready = sem("sq_ready")
        sums_done = sem("sums_done")
        var_ready = sem("var_ready")
        std_ready = sem("std_ready")
        silu_done = sem("silu_done")
        h_ready = sem("h_ready")
        hh_ready = sem("hh_ready")
        hl_ready = sem("hl_ready")
        init = sem("init")
        p_landed = sem("p_landed")
        ph_ready = sem("ph_ready")
        pl_ready = sem("pl_ready")
        pj_done = sem("pj_done")
        sig_done = sem("sig_done")
        dve_step = sem("dve_step")
        act_step = sem("act_step")
        pool_step = sem("pool_step")
        stored = sem("stored")
        x_final = sem("x_final")
        conv_raw = sem("conv_raw")
        conv_first = sem("conv_first")
        conv_sum = sem("conv_sum")
        conv_act = sem("conv_act")
        dt_d_step = sem("dt_d_step")
        dt_a_step = sem("dt_a_step")
        dec_sum = sem("dec_sum")
        dec_act = sem("dec_act")
        pre_p = sem("pre_p")
        pre_d = sem("pre_d")
        pre_a = sem("pre_a")
        dtx_tr = sem("dtx_tr")
        dtx_row = sem("dtx_row")
        dtx_out = sem("dtx_out")
        h0_landed = [sem(f"h0_landed{b}") for b in range(4)]
        h0_used = sem("h0_used")
        y_dec = sem("y_dec")
        ssd_in = sem("ssd_in")
        ssd_diff = sem("ssd_diff")
        ssd_sel = sem("ssd_sel")
        ssd_read = sem("ssd_read")
        ssd_exp = sem("ssd_exp")
        ssd_mm = sem("ssd_mm")
        ssd_part = sem("ssd_part")
        ssd_carry = sem("ssd_carry")
        ssd_isc = sem("ssd_isc")
        ssd_tr = sem("ssd_tr")
        ssd_y = sem("ssd_y")
        tok_ready = sem("tok_ready")
        z_silu = sem("z_silu")
        gated = sem("gated")
        gated_sq = sem("gated_sq")
        gated_sum = sem("gated_sum")
        gated_var = sem("gated_var")
        gated_std = sem("gated_std")
        gn_ready = sem("gn_ready")
        st_out = [sem("st_out0"), sem("st_out1")]
        conv_out = sem("conv_out")
        late_in = [sem("late_in0"), sem("late_in1")]
        late_out = sem("late_out")
        kvh_ready = sem("kvh_ready")
        kvl_ready = sem("kvl_ready")
        head_sq = sem("head_sq")
        head_sum = sem("head_sum")
        head_var = sem("head_var")
        head_std = sem("head_std")
        head_n = sem("head_n")
        rot_done = sem("rot_done")
        roped = sem("roped")
        v_tr = sem("v_tr")
        v_tok = sem("v_tok")
        cache_in = sem("cache_in")
        old_out = sem("old_out")
        kv_out = sem("kv_out")
        dec_p = sem("dec_p")
        dec_d = sem("dec_d")
        dec_a = sem("dec_a")
        dec_a_go = sem("dec_a_go")
        s_done = sem("s_done")
        s_max = sem("s_max")
        s_exp = sem("s_exp")
        s_prob = sem("s_prob")
        p_tr = sem("p_tr")
        p_read = sem("p_read")
        pv_done = sem("pv_done")
        o_read = sem("o_read")

        block = ctx.enter_context(nc.Block())

        dd = small[0:64, 0:N]
        o_ = N
        dtT = [small[:, o_ + 32 * c:o_ + 32 * c + 32] for c in range(2)]
        o_ += 64
        da4 = [small[:, o_ + P * c:o_ + P * c + P] for c in range(2)]
        tok = sb("tok", [P, 2, 3, HEADS])
        da_bc = sb("da_bc", [P, SEQS, HEADS])
        da_d = sb("da_d", [P, XT, SEQS])
        dt_d = sb("dt_d", [P, XT, SEQS])
        dtx_d = sb("dtx_d", [P, XT, SEQS])
        bc_d = sb("bc_d", [P, G, SEQS])
        b_d = sb("b_d", [P, G, SEQS])
        c_d = sb("c_d", [P, G, SEQS])
        t1d = sb("t1d", [P, XT, SEQS])
        state = sb("state", [P, 2, 256])
        decraw = sb("decraw", [P, CT, SEQS])
        tail = sb("tail", [P, CT, 3])
        zf = zs[:, :, :].rearrange("p k n -> p (k n)")
        convs = zf[:, 8 * N:8 * N + 768].rearrange("p (k w s) -> p k w s", k=CT, w=3)
        dgl = zf[0:64, 12 * N:12 * N + 256].rearrange("p (s h) -> p s h", s=SEQS)
        cwork = zf[:, 13 * N:13 * N + 256].rearrange("p (k s) -> p k s", k=CT)
        csum = xact[:, :, T:N]
        hl_mid = hl[:, 10:16, :].rearrange("p k n -> p (k n)")
        diffR = [hl_mid[:, 512 * c:512 * c + 512] for c in range(2)]
        diffL = [hl_mid[:, 1024 + P * c:1024 + P * c + P] for c in range(2)]
        diffLg = [hl_mid[:, 1280 + P * b:1280 + P * b + P] for b in range(2)]
        ident_r, mask_r = hl[:, 16, 0:P], hl[:, 16, P:2 * P]
        cum4 = hl[:, 17, 0:2 * P]
        dtxt = sq[0:SEQS, 0:2048]
        late = xact[:, 16:32, :].rearrange("p k n -> p (k n)")
        lateA, lateB = late[:, 0:2048], late[:, 2048:4096]
        Dm = [sq[:, 512 * b:512 * b + 512] for b in range(2)]
        xdt = [sq[:, 1024 + 256 * b:1280 + 256 * b] for b in range(2)]
        xte = [sq[:, 1536 + 256 * b:1792 + 256 * b] for b in range(2)]
        guf = gu[:, :, :].rearrange("p k n -> p (k n)")
        cbb = [guf[:, 256 * b:256 * b + 256] for b in range(2)]
        isc, h1 = guf[:, 512:768], guf[:, 768:1024]
        xraw = guf[:, 0:4 * 260].rearrange("p (k n) -> p k n", k=4)
        pj = zs[:, 0:8, :]
        qf, kf, vf = xact[:, 0:8, :], xact[:, 8:10, :], xact[:, 10:12, :]
        xf = xact[:, :, :].rearrange("p k n -> p (k n)")
        vtok = xf[:, 12 * N:12 * N + 512].rearrange("p (c n) -> p c n", c=2)
        kc = xf[:, 14 * N:14 * N + 2048].rearrange("p (k s w) -> p k s w", k=2, s=SEQS)
        vc = xf[:, 22 * N:22 * N + 2048].rearrange("p (s n) -> p s n", s=SEQS)
        o32 = zs[:, 0:8, :]
        sm = zs[:, 8:11, :].rearrange("p k n -> p (k n)")[:, 0:768].rearrange("p (b n) -> p b n", b=2)
        pT_ = zs[:, 11:14, :].rearrange("p k n -> p (k n)")[:, 0:768].rearrange("p (b n) -> p b n", b=2)
        aw = sq[:, 0:4 * N].rearrange("p (k n) -> p k n", k=4)
        mx = small[:, 0:4]; nmx = small[:, 4:8]; rs = small[:, 8:12]; es = small[:, 12:16]; rr = small[:, 16:20]
        dS = small[:, 128:128 + 129]; dP = small[:, 260:260 + 129]; sTd = small[:, 400:528]
        prod = small[:, 528:656]; dgP = small[:, 656:784]; pTd = small[:, 784:912]; od = small[:, 912:976]
        dm = small[:, 976:984]

        def link(eng, step, count, ins):
            count[0] += 1
            ins.then_inc(step, 1)
            eng.wait_ge(step, count[0])

        @block.sync
        def _(sp):
            sp.dma_start(x[:, :, :], xT).then_inc(init, 16)
            sp.dma_start(cs[:, :], cst).then_inc(init, 16)
            sp.dma_start(vs[:, :], vec).then_inc(init, 16)
            sp.dma_start(convs, convst).then_inc(init, 16)
            for s in range(RING):
                sp.dma_start(raw[:, s, :], weights[s]).then_inc(raw_landed[s], 16)

            with sp.Fori(1, NU // RING) as i:
                for s in range(RING):
                    sp.wait_ge(lo_ready, i * RING + (s - RING + 1))
                    sp.dma_start(raw[:, s, :], weights[bass.ds(i * RING + s, 1)].rearrange("u p n -> p (u n)")).then_inc(raw_landed[s], 16)
            for u in range(NU // RING * RING, NU):
                sp.wait_ge(lo_ready, u - RING + 1)
                sp.dma_start(raw[:, u % RING, :], weights[u]).then_inc(raw_landed[u % RING], 16)
            for m in range(KT):
                sp.wait_ge(x_final, KT + m + 1)
                sp.dma_start(y_out[:, m, :], x[:, m, :]).then_inc(stored, 16)
            sp.wait_ge(stored, 16 * KT)

        @block.tensor
        def _(pe):
            pe.sem_inc(unit_used, RING)

            def split_products(out, w, tile, rh, rl, start, stop):
                c = slice(tile * P, tile * P + P)
                pe.matmul(out, whi[:, w, c], rh, start=start, stop=False)
                pe.matmul(out, whi[:, w, c], rl, start=False, stop=False)
                return pe.matmul(out, wlo[:, w, c], rh, start=False, stop=stop)

            def unit_a(stage, i, j, b_wait=None, x_wait=False, rh=xh, rl=xl, kv_wait=False, banks=4):
                u, _, s = unit(U0[stage], i, j)
                out = bank[(A0[stage] + j) % banks]
                pe.wait_ge(lo_ready, u + 1)
                pe.wait_ge(a_free, A0[stage] + j + 4 * i + 5 - banks)
                if b_wait is not None:
                    pe.wait_ge(b_free, 8 * b_wait + (A0[stage] + j) % 4 + 1)
                for k in range(KT):
                    if x_wait:
                        pe.wait_ge(xl_ready, XREADY[stage] + k + 1)
                    if kv_wait:
                        pe.wait_ge(kvl_ready, k + 1)
                    mm = split_products(out[:, 0:N], s, k, rh[:, k, :], rl[:, k, :], k == 0, k == KT - 1)
                mm.then_inc(unit_used, 1)

            def sums(stage, b_wait=None):
                pe.wait_ge(sq_ready, NORM[stage] + 1)
                if b_wait is not None:
                    pe.wait_ge(b_free, 8 * b_wait + 5)
                for k in range(KT):
                    mm = pe.matmul(bank[4][:, 0:N], ones, sq3[:, k, :], start=k == 0, stop=k == KT - 1)
                mm.then_inc(sums_done, 1)

            def first_units(stage, n, b_wait, no_sums=False):
                for j in range(n):
                    unit_a(stage, 0, j, b_wait if j < 4 else None, x_wait=(j == 0))
                    if j == 1 and not no_sums:
                        sums(stage, b_wait)

            def first_units_p(stage, b_wait):
                for j in range(KT):
                    unit_a(stage, 0, j, x_wait=(j == 0))
                    if j == 1:
                        sums(stage, b_wait)

            def head_sum_(n_):
                pe.wait_ge(head_sq, n_ + 1)
                if n_ > 0:
                    pe.wait_ge(head_var, n_)
                pe.matmul(bank[5][:, 0:N], blk, aw[:, n_ % 2, :], start=True, stop=True).then_inc(head_sum, 1)

            def head_rot(n_, tile):
                pe.wait_ge(head_n, n_ + 1)
                if n_ > 0:
                    pe.wait_ge(roped, n_)
                pe.matmul(bank[6][:, 0:N], rot, tile, start=True, stop=True).then_inc(rot_done, 1)

            def head_norms(n0, n1):
                for n_ in range(n0, n1):
                    head_sum_(n_)
                for n_ in range(n0, n1):
                    head_rot(n_, kf[:, n_, :])

            def ffn_in(stage, b_wait):
                first_units(stage, 4, b_wait)
                with pe.Fori(1, 2 * FT // RING) as i:
                    for j in range(RING):
                        unit_a(stage, i, j)

            def unit_b(stage, u, s, kt, where, order, first, last, hready):
                pe.wait_ge(lo_ready, u + 1)
                pe.wait_ge(hl_ready, hready)
                rh, rl = (hh[:, kt, :], hl[:, kt, :]) if isinstance(kt, int) else (
                    hh[:, bass.ds(kt, 1), :].rearrange("p a n -> p (a n)"), hl[:, bass.ds(kt, 1), :].rearrange("p a n -> p (a n)"))
                for n_, m in enumerate(order):
                    if first and m == 0:
                        pe.wait_ge(a_free, A0[where] + 4)
                    mm = split_products(bank[m][:, 0:N], s, m, rh, rl, first, last)
                    if last and n_ < 7:
                        mm.then_inc(b_done, 1)
                mm.then_inc(unit_used, 1)

            def stage_b(stage, n, after):
                h0_ = HREADY[stage]
                u, _, s = unit(U0[stage], 0, 0)
                unit_b(stage, u, s, 0, after, (4, 5, 6, 7, 0, 1, 2, 3), True, False, h0_ + 1)
                loops = (n - 2) // RING
                with pe.Fori(0, loops) as i:
                    for j in range(1, RING + 1):
                        u, _, s = unit(U0[stage], i, j)
                        unit_b(stage, u, s, i * RING + j, after, range(8), False, False, i * RING + (h0_ + j + 1))
                for j in range(1 + loops * RING, n):
                    u, _, s = unit(U0[stage], 0, j)
                    unit_b(stage, u, s, j, after, range(8), False, j == n - 1, h0_ + j + 1)

            def embed(stage, b_wait, layer):
                pe.wait_ge(pl_ready, layer + 1)
                for j in range(2):
                    u, _, s = unit(U0[stage], 0, j)
                    pe.wait_ge(lo_ready, u + 1)
                    for m in range(4):
                        a = A0[stage] + 4 * j + m
                        pe.wait_ge(a_free, a + 1)
                        if j == 0:
                            pe.wait_ge(b_free, 8 * b_wait + a % 4 + 1)
                        for k in range(2):
                            mm = split_products(bank[a % 4][:, 0:N], s, 2 * m + k, ph[:, k, :], pl[:, k, :], k == 0, k == 1)
                        mm.then_inc(unit_used if m == 3 else pj_done, 1)

            def chunk_in(k):
                g, c = k // 2, k % 2
                r = slice(128 * c, 128 * c + 128)
                if k > 0:
                    pe.wait_ge(ssd_read, k)
                pe.matmul(bank[4][:, 0:128], xact[:, 16 + g, r], xact[:, 24 + g, r], start=True, stop=True)
                pe.transpose(bank[4][:, 128:256], xact[:, 16 + g, r], ident)
                pe.transpose(bank[4][:, 256:384], xact[:, 2 * g, r], ident)
                pe.transpose(bank[4][:, 384:512], xact[:, 2 * g + 1, r], ident).then_inc(ssd_in, 1)
                pe.wait_ge(ssd_sel, k + 1)
                if k > 0:
                    pe.wait_ge(ssd_exp, k)
                pe.matmul(bank[5][:, 0:512], diffLg[k % 2], diffR[c], start=True, stop=False)
                pe.matmul(bank[5][:, 0:512], ident_r, mask_r.unsqueeze(1).to_broadcast([P, 4, P]), start=False, stop=True).then_inc(ssd_diff, 1)

            def chunk_out(k):
                g, c = k // 2, k % 2
                yb = bank[6 + g % 2]
                pe.wait_ge(ssd_mm, k + 1)
                if k == 0:
                    pe.wait_ge(pre_d, 6)
                if g >= 2 and c == 0:
                    pe.wait_ge(ssd_y, g - 1)
                for h in range(4):
                    pe.matmul(yb[64 * (h % 2):64 * (h % 2) + 64, 256 * (h // 2) + 128 * c:256 * (h // 2) + 128 * c + 128],
                              xdt[k % 2][:, 64 * h:64 * h + 64], Dm[k % 2][:, 128 * h:128 * h + 128],
                              start=h < 2, stop=c == 0, skip_group_check=True)
                if k > 0:
                    pe.wait_ge(ssd_carry, k)
                mm = pe.matmul(bank[3][:, 0:256], cbb[k % 2][:, 128:256], xte[k % 2], start=True, stop=True)
                if c == 1:
                    mm = pe.matmul(bank[3][:, 256:512], xact[:, 24 + g, 128:256], h1, start=True, stop=True)
                mm.then_inc(ssd_part, 1)

            def add_inter(g):
                pe.wait_ge(ssd_isc, g + 1)
                for n_ in range(2):
                    mm = pe.matmul(bank[6 + g % 2][:, 256 * n_ + 128:256 * n_ + 256], isc[:, 128 * n_:128 * n_ + 128], ident,
                                   start=False, stop=True, skip_group_check=True)
                mm.then_inc(ssd_tr, 1)

            def decode_state(q):
                pe.wait_ge(h0_landed[q % 4], 16 * (q // 4 + 1))
                for j in range(XT):
                    mm = pe.matmul(bank[2][:, 8 * j + q:8 * j + q + 1], h0buf[q % 4][:, 128 * j:128 * j + 128],
                                   c_d[:, j // 2, q:q + 1], start=True, stop=True)
                mm.then_inc(h0_used, 1)

            def norm_sums(g):
                pe.wait_ge(gated_sq, g + 1)
                if g > 0:
                    pe.wait_ge(gated_var, g)
                pe.matmul(bank[2][:, 0:N], ones, gsq[:, 0, :], start=True, stop=False)
                pe.matmul(bank[2][:, 0:N], ones, gsq[:, 1, :], start=False, stop=True).then_inc(gated_sum, 1)

            pe.wait_ge(init, 64)
            ffn_in("f1i0", None)
            stage_b("f1o0", FT, "sin")
            first_units("sin", 5, 0)
            with pe.Fori(0, 7) as i:
                for j in range(5, 9):
                    unit_a("sin", i, j)
            def z_unit(s_):
                if s_ < XT:
                    unit_a("sin", 0, 33 + s_, banks=2)

            pe.transpose(bank[4][:, 0:64], dd[:, 0:128], ident[0:64, 0:64])
            pe.transpose(bank[4][:, 64:128], dd[:, 128:256], ident[0:64, 0:64]).then_inc(pre_p, 1)
            z_unit(0)
            pe.wait_ge(pre_d, 1)
            for c in range(2):
                dta = da4[c][:, 0:HEADS]
                pe.matmul(bank[5][:, 64 * c:64 * c + 32], tri, dta, start=True, stop=True)
                pe.matmul(bank[5][:, 64 * c + 32:64 * c + 64], ones, dta, start=True, stop=True)
                mm = pe.matmul(bank[2][:, 128 * c:128 * c + 128], da4[c], tri, start=True, stop=True)
            mm.then_inc(pre_p, 1)
            z_unit(1)
            pe.wait_ge(pre_d, 3)
            pe.wait_ge(a_free, A0["sin"] + 33 + 4)
            pe.matmul(bank[7][:, 0:256], ones[32:64, :], dgl[32:64], start=True, stop=True)
            pe.matmul(bank[6][:, 0:256], ones[0:32, :], dgl[0:32], start=True, stop=True)
            pe.matmul(bank[3][:, 0:64], ones, bc_d[:, :, :], start=True, stop=True).then_inc(pre_p, 1)
            pe.wait_ge(pre_d, 5)
            for s_ in range(2, SLOTS):
                z_unit(s_)
                if 0 <= s_ - H0_AT < SEQS:
                    decode_state(s_ - H0_AT)
                k = s_ - CHUNK0
                if 0 <= k < 2 * G:
                    chunk_in(k)
                if 0 <= k - 3 < 2 * G and k % 2 == 1:
                    add_inter((k - 3) // 2)
                if 0 <= k - 1 < 2 * G:
                    chunk_out(k - 1)
                if s_ in NORM_AT:
                    norm_sums(NORM_AT.index(s_))
                if s_ == SLOTS - 2:
                    pe.wait_ge(ssd_y, G)
                    for j in range(XT):
                        mm = pe.transpose(bank[3 + j // 4][0:SEQS, 128 * (j % 4):128 * (j % 4) + 128], dtx_d[:, j, :], ident)
                    mm.then_inc(dtx_tr, 1)
            pe.wait_ge(gated_var, G)
            pe.wait_ge(dtx_row, 1)
            stage_b("sout", XT, "f2i0")
            ffn_in("f2i0", 1)
            stage_b("f2o0", FT, "pp0")
            embed("pp0", 2, 0)
            first_units_p("pg0", 2)
            for j in range(4):
                unit_a("kv", 0, j, rh=hh, rl=hl, kv_wait=(j == 0))
                if j == 1:
                    sums("kv", None)
            head_norms(0, 2)
            pe.wait_ge(a_free, A0["kv"] + 4 + 4)
            pe.wait_ge(roped, 2)
            for c in range(2):
                for n_ in range(2):
                    mm = pe.transpose(bank[7][:, 256 * c + 128 * n_:256 * c + 128 * n_ + 128], vf[:, n_, 128 * c:128 * c + 128], ident)
            mm.then_inc(v_tr, 1)
            first_units("f1i1", 4, None, no_sums=True)
            with pe.Fori(1, 2 * FT // RING) as i:
                for j in range(RING):
                    unit_a("f1i1", i, j)
            stage_b("f1o1", FT, "q")
            for t in range(KT + 2):
                if t < KT:
                    unit_a("q", 0, t, 3 if t < 4 else None, x_wait=(t == 0))
                if t == 1:
                    sums("q", 3)
                if 1 <= t <= KT:
                    head_sum_(2 + t - 1)
                if t >= 2:
                    head_rot(2 + t - 2, qf[:, t - 2, :])
            pe.wait_ge(roped, 10)
            pe.wait_ge(cache_in, 32)
            for b in range(2):
                hs = slice(64 * b, 64 * b + 64)
                for q in range(SEQS):
                    for kp in range(2):
                        c_ = 8 * q + 4 * kp
                        mm = pe.matmul(bank[4 + b][:, c_:c_ + 4], kc[hs, kp, q, :], qf[hs, 4 * kp:4 * kp + 4, T + q],
                                       start=True, stop=True)
            mm.then_inc(dec_p, 1)
            pe.wait_ge(dec_d, 2)
            pe.transpose(bank[6][:, 0:128], sTd, ident)
            pe.matmul(bank[6][0:64, 128:129], prod[0:64, 0:64], ones[0:64, 0:1], start=True, stop=True)
            pe.matmul(bank[7][64:128, 0:1], prod[64:128, 0:64], ones[64:128, 0:1], start=True, stop=True).then_inc(dec_p, 1)
            pe.wait_ge(dec_d, 3)
            pe.transpose(bank[6][:, 0:128], dP[:, 0:128], ident)
            pe.matmul(bank[5][:, 0:128], ones, dgP, start=True, stop=True).then_inc(dec_p, 1)
            pe.wait_ge(dec_d, 4)
            for q in range(SEQS):
                for kp in range(2):
                    for b in range(2):
                        c_ = 8 * q + 4 * kp
                        mm = pe.matmul(bank[4][64 * b:64 * b + 64, c_:c_ + 4], vc[:, q, 64 * (2 * kp + b):64 * (2 * kp + b) + 64],
                                       pTd[:, 64 * b + c_:64 * b + c_ + 4], start=True, stop=True)
            mm.then_inc(dec_p, 1)
            def scores(e):
                t, b = e // 2, e % 2
                hs = slice(64 * b, 64 * b + 64)
                if e < 2:
                    pe.wait_ge(dec_d, 5)
                else:
                    pe.wait_ge(s_max, e - 1)
                k = kf[hs, t // 4, :]
                pe.matmul(bank[4 + b][:, 0:128], qf[hs, t, 0:128], k[:, 0:128], start=True, stop=True)
                pe.matmul(bank[4 + b][:, 128:384], qf[hs, t, 128:256], k[:, 0:256], start=True, stop=True).then_inc(s_done, 1)

            scores(0)
            scores(1)
            pe.wait_ge(v_tok, 1)
            for e in range(AH):
                t, b = e // 2, e % 2
                pe.wait_ge(s_prob, e + 1)
                if e > 0:
                    pe.wait_ge(p_read, e)
                for n_ in range(3):
                    mm = pe.transpose(bank[6][:, 128 * n_:128 * n_ + 128], sm[:, b, 128 * n_:128 * n_ + 128], ident)
                mm.then_inc(p_tr, 1)
                if e + 2 < AH:
                    scores(e + 2)
                pe.wait_ge(p_read, e + 1)
                if e > 0:
                    pe.wait_ge(o_read, e)
                ob = bank[7][64 * b:64 * b + 64, :]
                v_ = slice(64 * (2 * (t // 4) + b), 64 * (2 * (t // 4) + b) + 64)
                pe.matmul(ob[:, 0:128], vtok[:, 0, v_], pT_[:, b, 0:128], start=True, stop=True)
                pe.matmul(ob[:, 128:256], vtok[:, 0, v_], pT_[:, b, 128:256], start=True, stop=False)
                pe.matmul(ob[:, 128:256], vtok[:, 1, v_], pT_[:, b, 256:384], start=False, stop=True).then_inc(pv_done, 1)
            stage_b("o", 8, "f2i1")
            ffn_in("f2i1", 4)
            stage_b("f2o1", FT, "pp1")
            embed("pp1", 5, 1)
            first_units_p("pg1", 5)

        @block.scalar
        def _(act):
            steps = [0]

            def round_unit(u, q, s):
                act.wait_ge(raw_landed[s], q * 16 + 16)
                act.wait_ge(unit_used, u + 1)
                act.activation(whi[:, s, :], raw[:, s, :], ACT.Copy).then_inc(hi_ready, 1)

            def ahead(stage, i, j):
                if U0[stage] + RING + j < NU:
                    round_unit(*unit(U0[stage] + RING, i, j))

            def ahead_all(stage, n):
                if n >= 8:
                    with act.Fori(0, n // RING) as i:
                        for j in range(RING):
                            ahead(stage, i, j)
                for j in range(n // RING * RING if n >= 8 else 0, n):
                    ahead(stage, 0, j)

            def split_x(gain, b_stage):
                for m in range(KT):
                    if b_stage is not None:
                        act.wait_ge(b_free, 8 * b_stage + m + 1)
                    act.activation(xh[:, m, :], x[:, m, :], ACT.Copy, scale=vs[:, gain + m:gain + m + 1]).then_inc(xh_ready, 1)
                act.activation(sq[:, :], x[:, :, :].rearrange("p k n -> p (k n)"), ACT.Square).then_inc(sq_ready, 1)

            def root(stage):
                act.wait_ge(var_ready, NORM[stage] + 1)
                act.activation(rstd[:, :], rstd[:, :], ACT.Sqrt).then_inc(std_ready, 1)

            def ffn_in(stage, out, ffn):
                def silu(i, p):
                    act.wait_ge(a_free, A0[stage] + 4 * i + 2 * p + 1 + 4)
                    act.activation(gu[:, 2 * p, :], gu[:, 2 * p, :], ACT.Silu).then_inc(silu_done, 1)

                def round_h(i, p):
                    act.wait_ge(h_ready, FT * ffn + 2 * i + p + 1)
                    dst = hh[:, p, :] if isinstance(i, int) else hh[:, bass.ds(2 * i + p, 1), :].rearrange("p a n -> p (a n)")
                    act.activation(dst, gu[:, 2 * p + 1, :], ACT.Copy).then_inc(hh_ready, 1)

                ahead(stage, 0, 0)
                ahead(stage, 0, 1)
                if stage in NORM:
                    root(stage)
                act.preload_act_table(ACT.Silu)
                silu(0, 0)
                ahead(stage, 0, 2)
                round_h(0, 0)
                silu(0, 1)
                ahead(stage, 0, 3)
                round_h(0, 1)
                with act.Fori(1, 2 * FT // RING) as i:
                    ahead(stage, i, 0)
                    silu(i, 0)
                    ahead(stage, i, 1)
                    round_h(i, 0)
                    ahead(stage, i, 2)
                    silu(i, 1)
                    ahead(stage, i, 3)
                    round_h(i, 1)

            def embed(stage, gate, layer):
                ahead(stage, 0, 0)
                ahead(stage, 0, 1)
                ahead(gate, 0, 0)
                ahead(gate, 0, 1)
                root(gate)
                for j in range(KT):
                    act.wait_ge(a_free, A0[gate] + j + 1 + 4)
                    act.activation(gu[:, j % 4, :], gu[:, j % 4, :], ACT.Sigmoid).then_inc(sig_done, 1)
                    if j >= 2:
                        ahead(gate, 0, j)

            def split_p(layer):
                act.wait_ge(p_landed, 16 * (layer + 1))
                act.activation(ph[:, :, :], gsq[:, :, :], ACT.Copy).then_inc(ph_ready, 1)

            def head_square(n_, tile, a):
                act.wait_ge(a_free, a + 1 + 4)
                if n_ > 1:
                    act.wait_ge(head_n, n_ - 1)
                act.activation(aw[:, n_ % 2, :], tile, ACT.Square).then_inc(head_sq, 1)

            def head_root(n_):
                act.wait_ge(head_var, n_ + 1)
                act.activation(aw[:, n_ % 2, :], aw[:, n_ % 2, :], ACT.Sqrt).then_inc(head_std, 1)

            for u in range(RING):
                round_unit(*unit(0, 0, u))
            act.wait_ge(init, 64)
            split_x(G_F1, None)
            ffn_in("f1i0", "f1o0", 0)
            ahead_all("f1o0", FT)
            split_x(G_MIX, 0)
            ahead("sin", 0, 0)
            root("sin")
            act.activation(avec[0:32, :], vs[0:32, V_ALOG:V_ALOG + 1], ACT.Exp).then_inc(dt_a_step, 1)
            act.wait_ge(dt_d_step, 2)
            act.activation(zs[0:64, 1, :], zs[0:64, 1, :], ACT.Exp).then_inc(dt_a_step, 1)
            act.preload_act_table(ACT.Silu)

            def tap_last(i, p, tile):
                act.wait_ge(conv_raw, tile + 1)
                one = (lambda a: a[:, p, :]) if isinstance(i, int) else (lambda a: a[:, bass.ds(tile, 1), :].rearrange("p a n -> p (a n)"))
                act.activation(one(xact)[:, 0:T], xraw[:, p, 3:259], ACT.Identity, scale=cw3(i, p, tile), bias=cb(i, p, tile)).then_inc(conv_first, 1)

            def cw3(i, p, tile):
                c = V_CW + 3 * CT
                return vs[:, c + p:c + p + 1] if isinstance(i, int) else vs[:, bass.ds(tile + c, 1)]

            def cb(i, p, tile):
                return vs[:, V_CB + p:V_CB + p + 1] if isinstance(i, int) else vs[:, bass.ds(tile + V_CB, 1)]

            def conv_silu(i, p, tile):
                t_ = xact[:, p, 0:T] if isinstance(i, int) else xact[:, bass.ds(tile, 1), 0:T].rearrange("p a n -> p (a n)")
                act.activation(t_, t_, ACT.Silu).then_inc(conv_act, 1)

            def conv_body(i, j0):
                for p in range(4):
                    ahead("sin", *((0, j0 + p) if isinstance(i, int) else (i - 1, j0 + p)))
                    first = isinstance(i, int) and p == 0
                    if not first:
                        act.wait_ge(conv_sum, 3 * (i * 4) + 3 * p)
                    tap_last(i, p, i * 4 + p)
                    if not first:
                        conv_silu(i, p - 1, i * 4 + (p - 1))

            conv_body(0, 1)
            with act.Fori(1, CT // 4) as i:
                conv_body(i, 5)
            act.wait_ge(conv_sum, 3 * CT)
            act.activation(xact[:, CT - 1, 0:T], xact[:, CT - 1, 0:T], ACT.Silu).then_inc(conv_act, 1)
            act.wait_ge(dec_sum, 1)
            act.activation(csum, csum, ACT.Silu).then_inc(dec_act, 1)
            ahead("sin", 0, 33)
            act.wait_ge(pre_p, 2)
            act.activation(cum4, bank[2][:, 0:256], ACT.Copy).then_inc(pre_a, 1)
            act.wait_ge(pre_d, 4)
            act.activation(tok[:, :, :, :], tok[:, :, :, :], ACT.Exp).then_inc(pre_a, 1)
            ahead("sin", 0, 34)

            def select(k):
                g, c = k // 2, k % 2
                if k >= 2:
                    act.wait_ge(ssd_diff, k - 1)
                act.activation(diffLg[k % 2], diffL[c].bitcast(F32), ACT.Copy, scale=cs[:, C_SEL + g:C_SEL + g + 1]).then_inc(ssd_sel, 1)

            act.wait_ge(pre_d, 5)
            select(0)
            act.wait_ge(pre_d, 6)
            act.activation(da_d[:, :, :], da_d[:, :, :], ACT.Exp)
            act.activation(da_bc[:, :, :], da_bc[:, :, :], ACT.Exp).then_inc(pre_a, 1)

            def zsilu(t0):
                act.wait_ge(a_free, A0["sin"] + 33 + t0 + 8 + 4)
                act.activation(zs[:, t0:t0 + 8, :], zs[:, t0:t0 + 8, :], ACT.Silu).then_inc(z_silu, 1)

            for s_ in range(2, SLOTS):
                if s_ < XT:
                    ahead("sin", 0, 33 + s_)
                if s_ == NORM_AT[0] - 2:
                    zsilu(0)
                if s_ == NORM_AT[4]:
                    zsilu(8)
                k = s_ - CHUNK0
                if 0 <= k < 2 * G:
                    if k + 1 < 2 * G:
                        select(k + 1)
                    act.wait_ge(ssd_diff, k + 1)
                    if k >= 2:
                        act.wait_ge(ssd_part, k - 1)
                    act.activation(Dm[k % 2], bank[5][:, 0:512], ACT.Exp).then_inc(ssd_exp, 1)
                if s_ in NORM_AT:
                    g = NORM_AT.index(s_)
                    act.wait_ge(gated, g + 1)
                    if g > 0:
                        act.wait_ge(gated_sum, g)
                    act.activation(gsq[:, :, :], zs[:, 2 * g:2 * g + 2, :], ACT.Square).then_inc(gated_sq, 1)
                    if g % 4 == 3:
                        act.wait_ge(gated_var, g + 1)
                        v_ = xact[:, 2 * g - 6:2 * g + 1:2, :]
                        act.activation(v_, v_, ACT.Sqrt).then_inc(gated_std, 1)
                        for t in range(2 * g - 6, 2 * g + 2):
                            act.wait_ge(gn_ready, t + 1)
                            act.activation(hh[:, t, :], zs[:, t, :], ACT.Copy).then_inc(hh_ready, 1)
            ahead_all("sout", XT)
            act.wait_ge(dtx_out, 16)
            split_x(G_F2, 1)
            act.wait_ge(gated_sum, 8)
            act.dma_start(gsq[:, :, :], pT[0]).then_inc(p_landed, 16)
            ffn_in("f2i0", "f2o0", 1)
            split_p(0)
            ahead_all("f2o0", FT)
            split_x(G_PLE, 2)
            embed("pp0", "pg0", 0)
            for m in range(KT):
                act.wait_ge(x_final, m + 1)
                act.activation(hh[:, m, :], x[:, m, :], ACT.Copy, scale=vs[:, G_KV + m:G_KV + m + 1]).then_inc(kvh_ready, 1)
            act.activation(sq[:, :], x[:, :, :].rearrange("p k n -> p (k n)"), ACT.Square).then_inc(sq_ready, 1)
            for m in range(KT):
                act.activation(xh[:, m, :], x[:, m, :], ACT.Copy, scale=vs[:, G_F1 + 8 + m:G_F1 + 8 + m + 1]).then_inc(xh_ready, 1)
            for j in range(4):
                ahead("kv", 0, j)
                if j == 1:
                    root("kv")
                    head_square(0, kf[:, 0, :], A0["kv"])
                    head_square(1, kf[:, 1, :], A0["kv"] + 1)
            head_root(0)
            head_root(1)
            ffn_in("f1i1", "f1o1", 2)
            ahead_all("f1o1", FT)
            split_x(G_MIX + 8, 3)
            ahead("q", 0, 0)
            ahead("q", 0, 1)
            root("q")
            for t in range(KT + 1):
                if t < KT:
                    head_square(2 + t, qf[:, t, :], A0["q"] + t)
                if t >= 1:
                    head_root(2 + t - 1)
                if 2 <= t < KT:
                    ahead("q", 0, t)
            act.wait_ge(dec_a_go, 1)
            act.activation(dP, dS, ACT.Exp, bias=dm[:, 1:2], accum_out=dm[:, 2:3])
            act.activation(dm[:, 3:4], dm[:, 1:2], ACT.Exp, bias=vs[:, V_SINKD:V_SINKD + 1]).then_inc(dec_a, 1)
            for e in range(AH):
                b = e % 2
                act.wait_ge(s_max, e + 1)
                act.activation(sm[:, b, 0:128], sm[:, b, 0:128], ACT.Exp, bias=nmx[:, 2 * b:2 * b + 1], accum_out=rs[:, 2 * b:2 * b + 1])
                act.activation(sm[:, b, 128:384], sm[:, b, 128:384], ACT.Exp, bias=nmx[:, 2 * b + 1:2 * b + 2], accum_out=rs[:, 2 * b + 1:2 * b + 2])
                act.activation(es[:, 2 * b:2 * b + 2], nmx[:, 2 * b:2 * b + 2], ACT.Exp, bias=vs[:, V_SINK + e:V_SINK + e + 1]).then_inc(s_exp, 1)
            for t in range(KT):
                act.wait_ge(o_read, 2 * t + 2)
                act.activation(hh[:, t, :], o32[:, t, :], ACT.Copy).then_inc(hh_ready, 1)
            ahead_all("o", 8)
            split_x(G_F2 + 8, 4)
            act.wait_ge(pl_ready, 1)
            act.dma_start(gsq[:, :, :], pT[1]).then_inc(p_landed, 16)
            ffn_in("f2i1", "f2o1", 3)
            split_p(1)
            ahead_all("f2o1", FT)
            split_x(G_PLE + 8, 5)
            embed("pp1", "pg1", 1)

        @block.vector
        def _(dve):
            steps = [0]

            def low_unit(u, q, s):
                dve.wait_ge(hi_ready, u + 1)
                dve.tensor_tensor(wlo[:, s, :], raw[:, s, :], whi[:, s, :].bitcast(F32), ALU.subtract).then_inc(lo_ready, 1)

            def ahead(stage, i, j):
                if U0[stage] + RING + j < NU:
                    low_unit(*unit(U0[stage] + RING, i, j))

            def ahead_all(stage, n):
                if n >= 8:
                    with dve.Fori(0, n // RING) as i:
                        for j in range(RING):
                            ahead(stage, i, j)
                for j in range(n // RING * RING if n >= 8 else 0, n):
                    ahead(stage, 0, j)

            def low_x(m, gain, n_):
                dve.wait_ge(xh_ready, n_ + m + 1)
                dve.scalar_tensor_tensor(out=xl[:, m, :], in0=x[:, m, :], scalar=vs[:, gain + m:gain + m + 1],
                                         in1=xh[:, m, :].bitcast(F32), op0=ALU.mult, op1=ALU.subtract).then_inc(xl_ready, 1)

            def add_b(stage, n, scale, gain, after):
                b = BSTAGE[stage]
                for m in range(KT):
                    if m < 7:
                        dve.wait_ge(b_done, 7 * b + m + 1)
                    else:
                        dve.wait_ge(unit_used, U0[stage] + n + RING)
                    dve.scalar_tensor_tensor(out=x[:, m, :], in0=bank[m][:, 0:N], scalar=scale, in1=x[:, m, :],
                                             op0=ALU.mult, op1=ALU.add).then_inc(b_free, 1)
                    if m > 0:
                        low_x(m - 1, gain, XREADY[after])
                low_x(7, gain, XREADY[after])

            def row_factor(stage):
                dve.wait_ge(sums_done, NORM[stage] + 1)
                dve.tensor_scalar(rstd[:, :], bank[4][:, 0:N], 1.0 / D, EPS, ALU.mult, ALU.add).then_inc(var_ready, 1)
                dve.wait_ge(std_ready, NORM[stage] + 1)
                link(dve, dve_step, steps, dve.reciprocal(rstd[:, :], rstd[:, :]))

            def take(dst, stage, j, i=0, cols=slice(0, N), signal=True, banks=4):
                dve.wait_ge(unit_used, U0[stage] + j + 4 * i + 1 + RING)
                ins = dve.tensor_tensor(dst, bank[(A0[stage] + j) % banks][:, cols], rstd[:, cols], ALU.mult)
                return ins.then_inc(a_free, 1) if signal else ins

            def ffn_in(stage, out, ffn):
                def gate(i, p):
                    take(gu[:, 2 * p, :], stage, 2 * p, i)

                def up(i, p):
                    take(gu[:, 2 * p + 1, :], stage, 2 * p + 1, i)

                def hidden(i, p):
                    dve.wait_ge(silu_done, FT * ffn + 2 * i + p + 1)
                    dve.wait_ge(a_free, A0[stage] + 4 * i + 2 * p + 2 + 4)
                    dve.tensor_tensor(gu[:, 2 * p + 1, :], gu[:, 2 * p, :], gu[:, 2 * p + 1, :], ALU.mult).then_inc(h_ready, 1)

                def low_h(i, p):
                    dve.wait_ge(hh_ready, HREADY[out] + 2 * i + p + 1)
                    one = (lambda a: a[:, p, :]) if isinstance(i, int) else (lambda a: a[:, bass.ds(2 * i + p, 1), :].rearrange("p a n -> p (a n)"))
                    dve.tensor_tensor(one(hl), gu[:, 2 * p + 1, :], one(hh).bitcast(F32), ALU.subtract).then_inc(hl_ready, 1)

                ahead(stage, 0, 0)
                ahead(stage, 0, 1)
                if stage in NORM:
                    row_factor(stage)
                gate(0, 0)
                up(0, 0)
                hidden(0, 0)
                gate(0, 1)
                ahead(stage, 0, 2)
                low_h(0, 0)
                up(0, 1)
                ahead(stage, 0, 3)
                hidden(0, 1)
                low_h(0, 1)
                with dve.Fori(1, 2 * FT // RING) as i:
                    gate(i, 0)
                    ahead(stage, i, 0)
                    up(i, 0)
                    ahead(stage, i, 1)
                    hidden(i, 0)
                    gate(i, 1)
                    ahead(stage, i, 2)
                    low_h(i, 0)
                    up(i, 1)
                    ahead(stage, i, 3)
                    hidden(i, 1)
                    low_h(i, 1)

            def embed(stage, gate, layer, kv):
                def gated_add(j):
                    t_ = gu[:, j % 4, :]
                    dve.wait_ge(sig_done, KT * layer + j + 1)
                    link(dve, dve_step, steps, dve.tensor_tensor(t_, t_, pj[:, j, :], ALU.mult))
                    dve.tensor_tensor(x[:, j, :], x[:, j, :], t_, ALU.add).then_inc(x_final, 1)

                for j in range(2):
                    ahead(stage, 0, j)
                    for m in range(4):
                        if m < 3:
                            dve.wait_ge(pj_done, 3 * (2 * layer + j) + m + 1)
                        else:
                            dve.wait_ge(unit_used, U0[stage] + j + 1 + RING)
                        dve.tensor_copy(pj[:, 4 * j + m, :], bank[(A0[stage] + 4 * j + m) % 4][:, 0:N]).then_inc(a_free, 1)
                ahead(gate, 0, 0)
                ahead(gate, 0, 1)
                row_factor(gate)
                for j in range(KT):
                    take(gu[:, j % 4, :], gate, j)
                    if j >= 2:
                        ahead(gate, 0, j)
                    if j > 0:
                        gated_add(j - 1)
                gated_add(KT - 1)
                if kv:
                    for m in range(KT):
                        low_kv(m)

            def low_kv(m):
                dve.wait_ge(kvh_ready, m + 1)
                dve.scalar_tensor_tensor(out=hl[:, m, :], in0=x[:, m, :], scalar=vs[:, G_KV + m:G_KV + m + 1],
                                         in1=hh[:, m, :].bitcast(F32), op0=ALU.mult, op1=ALU.subtract).then_inc(kvl_ready, 1)

            def low_p(layer):
                dve.wait_ge(ph_ready, layer + 1)
                dve.tensor_tensor(pl[:, :, :], gsq[:, :, :], ph[:, :, :].bitcast(F32), ALU.subtract).then_inc(pl_ready, 1)

            def head_norm(n_, tile, gain):
                w = aw[:, n_ % 2, :]
                dve.wait_ge(head_sum, n_ + 1)
                dve.tensor_scalar(w, bank[5][:, 0:N], 1.0 / 64, EPS, ALU.mult, ALU.add).then_inc(head_var, 1)
                dve.wait_ge(head_std, n_ + 1)
                link(dve, dve_step, steps, dve.reciprocal(w, w))
                dve.scalar_tensor_tensor(out=tile, in0=tile, scalar=vs[:, gain:gain + 1], in1=w, op0=ALU.mult, op1=ALU.mult).then_inc(head_n, 1)

            def rope(n_, tile):
                dve.wait_ge(rot_done, n_ + 1)
                dve.tensor_tensor(aw[:, 2, :], bank[6][:, 0:N], sinT, ALU.mult)
                link(dve, dve_step, steps, dve.tensor_tensor(tile, tile, cosT, ALU.mult))
                dve.tensor_tensor(tile, tile, aw[:, 2, :], ALU.add).then_inc(roped, 1)

            dve.sem_inc(a_free, 4)
            for u in range(RING):
                low_unit(*unit(0, 0, u))
            dve.wait_ge(init, 64)
            for m in range(KT):
                low_x(m, G_F1, 0)
            ffn_in("f1i0", "f1o0", 0)
            ahead_all("f1o0", FT)
            add_b("f1o0", FT, 0.5, G_MIX, "sin")
            dve.memset(xraw[:, :, 0:3], 0.0)
            dve.memset(avec[32:64, :], 1.0)
            ahead("sin", 0, 0)
            row_factor("sin")
            t_, e_, m_, r_, s_, s2_, a_ = (zs[0:64, k, :] for k in range(7))
            n_dt = [0]

            def dt_step(ins):
                link(dve, dt_d_step, n_dt, ins)

            dve.wait_ge(unit_used, U0["sin"] + 1 + RING)
            dve.tensor_tensor(t_, bank[A0["sin"] % 4][0:64, 0:N], rstd[0:64, :], ALU.mult).then_inc(a_free, 1)
            dve.wait_ge(a_free, A0["sin"] + 1 + 4)
            dt_step(dve.tensor_scalar(t_, t_, vs[0:64, V_DTB:V_DTB + 1], None, ALU.add))
            dt_step(dve.scalar_tensor_tensor(out=e_, in0=t_, scalar=-1.0, in1=t_, op0=ALU.mult, op1=ALU.min))
            dt_step(dve.tensor_scalar(m_, t_, 0.0, None, ALU.max))
            dve.wait_ge(dt_a_step, 2)
            dt_step(dve.tensor_scalar(r_, e_, 2.0, None, ALU.add))
            dt_step(dve.reciprocal(r_, r_))
            dt_step(dve.tensor_tensor(s_, e_, r_, ALU.mult))
            dt_step(dve.tensor_tensor(s2_, s_, s_, ALU.mult))
            dt_step(dve.tensor_scalar(a_, s2_, 1.0 / 17, None, ALU.mult))
            for k in (15, 13, 11, 9, 7, 5, 3):
                dt_step(dve.scalar_tensor_tensor(out=a_, in0=a_, scalar=1.0 / k, in1=s2_, op0=ALU.add, op1=ALU.mult))
            dt_step(dve.scalar_tensor_tensor(out=a_, in0=a_, scalar=1.0, in1=s_, op0=ALU.add, op1=ALU.mult))
            dt_step(dve.scalar_tensor_tensor(out=a_, in0=a_, scalar=2.0, in1=m_, op0=ALU.mult, op1=ALU.add))
            link(dve, dve_step, steps, dve.tensor_scalar(avec[0:32, :], avec[0:32, :], -1.0, None, ALU.mult))
            dt_step(dve.tensor_scalar(dd, a_, avec[0:64, :], None, ALU.mult))
            assert n_dt[0] == DT_STEPS

            def conv_in(i, p, j):
                tile = i * 4 + p
                if not isinstance(i, int):
                    i_ = i - 1
                    dst = decraw[:, bass.ds(tile, 1), :].rearrange("p a n -> p (a n)")
                else:
                    i_ = 0
                    dst = decraw[:, tile, :]
                take(xraw[:, p, 3:259], "sin", j, i_, slice(0, T), signal=False).then_inc(conv_raw, 1)
                take(dst, "sin", j, i_, slice(T, N))

            def conv_taps(i, p):
                tile = p if i is None else i * 4 + p
                fixed = i is None or isinstance(i, int)
                xr = xraw[:, p % 4, :]
                out = xact[:, tile, 0:T] if fixed else xact[:, bass.ds(tile, 1), 0:T].rearrange("p a n -> p (a n)")
                tl = tail[:, tile, :] if fixed else tail[:, bass.ds(tile, 1), :].rearrange("p a n -> p (a n)")
                dve.wait_ge(conv_first, tile + 1)
                dve.tensor_copy(tl, xr[:, T:T + 3])
                for k in range(3):
                    w = vs[:, V_CW + CT * k + tile:V_CW + CT * k + tile + 1] if fixed else vs[:, bass.ds(tile + (V_CW + CT * k), 1)]
                    if k > 0:
                        dve.wait_ge(conv_sum, tile * 3 + k)
                    dve.scalar_tensor_tensor(out=out, in0=xr[:, k:k + T], scalar=w, in1=out, op0=ALU.mult, op1=ALU.add).then_inc(conv_sum, 1)

            def conv_body(i, j0):
                for p in range(4):
                    conv_in(i, p, j0 + p)
                    if p > 0 or not isinstance(i, int):
                        conv_taps(i, p - 1)
                    ahead("sin", *((0, j0 + p) if isinstance(i, int) else (i - 1, j0 + p)))

            conv_body(0, 1)
            with dve.Fori(1, CT // 4) as i:
                conv_body(i, 5)
            conv_taps(None, CT - 1)
            dve.wait_ge(pre_p, 1)
            for c in range(2):
                dve.tensor_copy(dtT[c], bank[4][:, 64 * c + 32:64 * c + 64])
                ins = dve.tensor_copy(da4[c].rearrange("p (k h) -> p k h", k=4), bank[4][:, 64 * c:64 * c + 32].unsqueeze(1).to_broadcast([P, 4, HEADS]))
            ins.then_inc(pre_d, 1)
            for k in (0, 32):
                ins = dve.tensor_tensor(dgl[k:k + 32], ident[k:k + 32, k:k + 32].unsqueeze(1).to_broadcast([32, SEQS, HEADS]),
                                        dd[k:k + 32, T:N].unsqueeze(2).to_broadcast([32, SEQS, HEADS]), ALU.mult)
            ins.then_inc(pre_d, 1)
            cw_ = lambda k: vs[:, V_CW + CT * k:V_CW + CT * k + CT].unsqueeze(2).to_broadcast([P, CT, SEQS])
            link(dve, dve_step, steps, dve.tensor_tensor(csum, decraw[:, :, :], cw_(3), ALU.mult))
            link(dve, dve_step, steps, dve.tensor_tensor(csum, csum, vs[:, V_CB:V_CB + CT].unsqueeze(2).to_broadcast([P, CT, SEQS]), ALU.add))
            for k in range(3):
                link(dve, dve_step, steps, dve.tensor_tensor(cwork, convs[:, :, k, :], cw_(k), ALU.mult))
                ins = dve.tensor_tensor(csum, csum, cwork, ALU.add)
                if k < 2:
                    link(dve, dve_step, steps, ins)
            ins.then_inc(dec_sum, 1)
            def z_take(s_):
                if s_ == 8:
                    dve.wait_ge(conv_out, 48)
                if s_ < XT:
                    take(zs[:, s_, :], "sin", 33 + s_, banks=2)
                    ahead("sin", 0, 33 + s_)

            z_take(0)
            dve.wait_ge(dec_act, 1)
            dve.tensor_copy(b_d[:, :, :], xact[:, 16:24, T:N])
            link(dve, dve_step, steps, dve.tensor_copy(c_d[:, :, :], xact[:, 24:32, T:N]))
            dve.tensor_tensor(bc_d[:, :, :], b_d[:, :, :], c_d[:, :, :], ALU.mult).then_inc(pre_d, 1)
            dve.wait_ge(pre_p, 2)
            cum_ps = bank[5][:, 0:128].rearrange("p (c k h) -> p c k h", c=2, k=2)
            dve.tensor_copy(tok[:, :, 0, :], cum_ps[:, :, 0, :])
            link(dve, dve_step, steps, dve.tensor_copy(tok[:, :, 2, :], cum_ps[:, :, 1, :]))
            dve.tensor_tensor(tok[:, :, 1, :], tok[:, :, 2, :], tok[:, :, 0, :], ALU.subtract).then_inc(pre_d, 1)
            dve.tensor_copy(ident_r, ident)
            dve.tensor_scalar(mask_r, tri, -1.0, 1e30, ALU.add, ALU.mult)
            dve.wait_ge(pre_a, 1)
            for k in (32, 96):
                ins = dve.tensor_tensor(cum4[k:k + 32], bank[2][k:k + 32, 0:256], cum4[k:k + 32].bitcast(F32), ALU.subtract)
            link(dve, dve_step, steps, ins)
            for c in range(2):
                R = diffR[c].rearrange("p (k l) -> p k l", k=4)
                ind = lambda n0, n1: cs[n0:n1, C_IND:C_IND + 4].unsqueeze(2).to_broadcast([n1 - n0, 4, P])
                cum_ = cum4[:, P * c:P * c + P].bitcast(F32)
                dve.tensor_tensor(R[0:64], cum_[0:64].unsqueeze(1).to_broadcast([64, 4, P]), ind(0, 64), ALU.mult)
                dve.tensor_copy(R[64:128], ind(64, 128))
                dve.tensor_copy(diffL[c][0:64], ones[0:64])
                ins = dve.tensor_scalar(diffL[c][64:128], cum_[64:128], -1.0, None, ALU.mult)
            ins.then_inc(pre_d, 1)
            z_take(1)
            dve.wait_ge(pre_a, 2)
            dve.tensor_tensor(tok[:, :, 1, :], tok[:, :, 1, :], small[:, N:N + 64].rearrange("p (c h) -> p c h", c=2), ALU.mult).then_inc(tok_ready, 1)
            dve.wait_ge(pre_p, 3)
            for b in range(2):
                hs = slice(64 * b, 64 * b + 64)
                spread = lambda ps: ps[hs, 0:256].rearrange("p (s k b) -> p b k s", s=SEQS, b=2)[:, b]
                dve.tensor_copy(da_d[hs, :, :], spread(bank[6]))
                ins = dve.tensor_copy(dt_d[hs, :, :], spread(bank[7]))
            link(dve, dve_step, steps, ins)
            dve.tensor_tensor(dtx_d[:, :, :], xact[:, 0:16, T:N], dt_d[:, :, :], ALU.mult)
            dve.tensor_copy(bc_d[:, :, :], bank[3][:, 0:64])
            dve.tensor_copy(da_bc[:, :, :], bank[6][:, 0:256]).then_inc(pre_d, 1)

            def decode_y():
                dve.wait_ge(h0_used, 8)
                dve.wait_ge(pre_a, 3)
                link(dve, dve_step, steps, dve.tensor_tensor(t1d[:, :, :], bank[2][:, 0:128].rearrange("p (k s) -> p k s", k=XT), da_d[:, :, :], ALU.mult))
                link(dve, dve_step, steps, dve.tensor_tensor(dt_d[:, :, :].rearrange("p (g t) s -> p g t s", g=G), bc_d[:, :, :].unsqueeze(2).to_broadcast([P, G, 2, SEQS]),
                                                             dtx_d[:, :, :].rearrange("p (g t) s -> p g t s", g=G), ALU.mult))
                link(dve, dve_step, steps, dve.tensor_tensor(t1d[:, :, :], t1d[:, :, :], dt_d[:, :, :], ALU.add))
                xd = xact[:, 0:XT, T:N]
                link(dve, dve_step, steps, dve.tensor_tensor(xd, xd, vs[:, V_D:V_D + XT].unsqueeze(2).to_broadcast([P, XT, SEQS]), ALU.mult))
                dve.tensor_tensor(xd, xd, t1d[:, :, :], ALU.add).then_inc(y_dec, 1)

            def by_head(a):
                return a.rearrange("p (h w) -> p h w", h=4)

            def heads(a):
                return a.unsqueeze(2).to_broadcast([P, 4, 64])

            def chunk_in(k):
                g, c = k // 2, k % 2
                dve.wait_ge(ssd_in, k + 1)
                if k == 0:
                    dve.wait_ge(tok_ready, 1)
                if k >= 2:
                    dve.wait_ge(ssd_part, k - 1)
                dve.tensor_copy(cbb[k % 2], bank[4][:, 0:256])
                dve.tensor_tensor(by_head(xdt[k % 2]), by_head(bank[4][:, 256:512]), heads(dtT[c][:, 4 * g:4 * g + 4]), ALU.mult)
                dve.tensor_tensor(by_head(xte[k % 2]), by_head(bank[4][:, 256:512]), heads(tok[:, c, 1, 4 * g:4 * g + 4]), ALU.mult).then_inc(ssd_read, 1)

            def carry(k):
                g, c = k // 2, k % 2
                dve.wait_ge(ssd_part, k + 1)
                if c == 0:
                    dve.tensor_copy(h1, bank[3][:, 0:256]).then_inc(ssd_carry, 1)
                    return
                if g > 0:
                    dve.wait_ge(ssd_tr, g)
                dve.tensor_tensor(by_head(isc), by_head(bank[3][:, 256:512]), heads(tok[:, 1, 0, 4 * g:4 * g + 4]), ALU.mult).then_inc(ssd_isc, 1)
                link(dve, dve_step, steps, dve.tensor_tensor(by_head(h1), by_head(h1), heads(tok[:, 1, 2, 4 * g:4 * g + 4]), ALU.mult))
                if g >= 2:
                    dve.wait_ge(st_out[g % 2], 16 * (g // 2))
                dve.tensor_tensor(state[:, g % 2, :], h1, bank[3][:, 0:256], ALU.add).then_inc(ssd_carry, 1)

            def decay(k):
                dve.wait_ge(ssd_exp, k + 1)
                dve.wait_ge(ssd_read, k + 1)
                dve.tensor_tensor(by_head(Dm[k % 2]), by_head(Dm[k % 2]), cbb[k % 2][:, 0:128].unsqueeze(1).to_broadcast([P, 4, P]), ALU.mult).then_inc(ssd_mm, 1)

            def finish(g):
                dve.wait_ge(ssd_tr, g + 1)
                for n_ in range(2):
                    xt_ = xact[:, 2 * g + n_, 0:T]
                    ins = dve.scalar_tensor_tensor(out=xt_, in0=xt_, scalar=vs[:, V_D + 2 * g + n_:V_D + 2 * g + n_ + 1],
                                                   in1=bank[6 + g % 2][:, 256 * n_:256 * n_ + 256], op0=ALU.mult, op1=ALU.add)
                ins.then_inc(ssd_y, 1)

            def low_z(t):
                dve.wait_ge(hh_ready, HREADY["sout"] + t + 1)
                dve.tensor_tensor(hl[:, t, :], zs[:, t, :], hh[:, t, :].bitcast(F32), ALU.subtract).then_inc(hl_ready, 1)

            for s_ in range(2, SLOTS):
                z_take(s_)
                if s_ == H0_AT + SEQS:
                    decode_y()
                if s_ in NORM_AT:
                    g = NORM_AT.index(s_)
                    dve.wait_ge(z_silu, 1 + g // 4)
                    dve.wait_ge(ssd_y, g + 1)
                    dve.tensor_tensor(zs[:, 2 * g:2 * g + 2, :], zs[:, 2 * g:2 * g + 2, :], xact[:, 2 * g:2 * g + 2, :], ALU.mult).then_inc(gated, 1)
                k = s_ - CHUNK0
                if 0 <= k < 2 * G:
                    chunk_in(k)
                if 0 <= k - 3 < 2 * G and k % 2 == 1:
                    finish((k - 3) // 2)
                if 0 <= k < 2 * G:
                    decay(k)
                if 0 <= k - 1 < 2 * G:
                    carry(k - 1)
                if s_ in NORM_AT:
                    dve.wait_ge(gated_sum, g + 1)
                    dve.tensor_scalar(xact[:, 2 * g, :], bank[2][:, 0:N], 1.0 / 256, EPS, ALU.mult, ALU.add).then_inc(gated_var, 1)
                    if g % 4 == 3:
                        dve.wait_ge(gated_std, g // 4 + 1)
                        v_ = xact[:, 2 * g - 6:2 * g + 1:2, :]
                        link(dve, dve_step, steps, dve.reciprocal(v_, v_))
                        for t in range(2 * g - 6, 2 * g + 2):
                            dve.scalar_tensor_tensor(out=zs[:, t, :], in0=zs[:, t, :], scalar=vs[:, V_NG + t:V_NG + t + 1],
                                                     in1=xact[:, t // 2 * 2, :], op0=ALU.mult, op1=ALU.mult).then_inc(gn_ready, 1)
                            if t > 2 * g - 6:
                                low_z(t - 1)
                        low_z(2 * g + 1)
                if s_ == SLOTS - 2:
                    dve.wait_ge(dtx_tr, 1)
                    for n_ in range(4):
                        ins = dve.tensor_copy(dtxt[:, 512 * n_:512 * n_ + 512], bank[3 + n_][0:SEQS, :])
                    ins.then_inc(dtx_row, 1)
            ahead_all("sout", XT)
            add_b("sout", XT, 1.0, G_F2, "f2i0")
            ffn_in("f2i0", "f2o0", 1)
            low_p(0)
            ahead_all("f2o0", FT)
            add_b("f2o0", FT, 0.5, G_PLE, "pg0")
            embed("pp0", "pg0", 0, True)
            for m in range(KT):
                low_x(m, G_F1 + 8, XREADY["f1i1"])
            ahead("kv", 0, 0)
            ahead("kv", 0, 1)
            row_factor("kv")
            take(kf[:, 0, :], "kv", 0)
            take(kf[:, 1, :], "kv", 1)
            ahead("kv", 0, 2)
            ahead("kv", 0, 3)
            take(vf[:, 0, :], "kv", 2)
            take(vf[:, 1, :], "kv", 3)
            for n_ in range(2):
                head_norm(n_, kf[:, n_, :], V_KN)
            for n_ in range(2):
                rope(n_, kf[:, n_, :])
            dve.wait_ge(v_tr, 1)
            dve.tensor_copy(vtok, bank[7][:, :].rearrange("p (c n) -> p c n", c=2)).then_inc(v_tok, 1)
            ffn_in("f1i1", "f1o1", 2)
            ahead_all("f1o1", FT)
            add_b("f1o1", FT, 0.5, G_MIX + 8, "q")
            ahead("q", 0, 0)
            ahead("q", 0, 1)
            row_factor("q")
            for t in range(KT + 2):
                if t < KT:
                    take(qf[:, t, :], "q", t)
                if 1 <= t <= KT:
                    head_norm(2 + t - 1, qf[:, t - 1, :], V_QN)
                if t >= 2:
                    rope(2 + t - 2, qf[:, t - 2, :])
                if 2 <= t < KT:
                    ahead("q", 0, t)
            dve.wait_ge(dec_p, 1)
            dve.wait_ge(roped, 10)
            dve.tensor_copy(sTd[:, 0:64], bank[4][:, 0:64])
            dve.tensor_copy(sTd[:, 64:128], bank[5][:, 0:64]).then_inc(dec_d, 1)
            dve.tensor_tensor(prod.rearrange("p (a b) -> p a b", a=2)[:, 0, :].rearrange("p (s k i) -> p s k i", s=SEQS, k=2),
                              qf[:, :, T:N].rearrange("p (k i) s -> p s k i", k=2),
                              kf[:, :, T:N].rearrange("p k s -> p s k").unsqueeze(3).to_broadcast([P, SEQS, 2, 4]), ALU.mult).then_inc(dec_d, 1)
            dve.wait_ge(dec_p, 2)
            dve.tensor_scalar(dS[:, 0:128], bank[6][:, 0:128], SCALE, None, ALU.mult)
            dve.tensor_scalar(dS[0:64, 128:129], bank[6][0:64, 128:129], SCALE, None, ALU.mult)
            link(dve, dve_step, steps, dve.tensor_scalar(dS[64:128, 128:129], bank[7][64:128, 0:1], SCALE, None, ALU.mult))
            link(dve, dve_step, steps, dve.tensor_reduce(dm[:, 0:1], dS, AX.X, ALU.max))
            link(dve, dve_step, steps, dve.tensor_scalar(dm[:, 0:1], dm[:, 0:1], vs[:, V_SINKD:V_SINKD + 1], None, ALU.max))
            dve.tensor_scalar(dm[:, 1:2], dm[:, 0:1], -1.0, None, ALU.mult).then_inc(dec_a_go, 1)
            dve.wait_ge(dec_a, 1)
            link(dve, dve_step, steps, dve.tensor_tensor(dm[:, 4:5], dm[:, 2:3], dm[:, 3:4], ALU.add))
            link(dve, dve_step, steps, dve.reciprocal(dm[:, 4:5], dm[:, 4:5]))
            link(dve, dve_step, steps, dve.tensor_scalar(dP, dP, dm[:, 4:5], None, ALU.mult))
            dve.tensor_scalar(dgP, ident, dP[:, 128:129], None, ALU.mult).then_inc(dec_d, 1)
            dve.wait_ge(dec_p, 3)
            dve.tensor_copy(pTd, bank[6][:, 0:128]).then_inc(dec_d, 1)
            dve.wait_ge(dec_p, 4)
            for b in range(2):
                hs = slice(64 * b, 64 * b + 64)
                od3 = od[hs, :].rearrange("p (s k i) -> p s k i", s=SEQS, k=2)
                link(dve, dve_step, steps, dve.tensor_tensor(od3, bank[5][hs, 64 * b:64 * b + 64].rearrange("p (s k i) -> p s k i", s=SEQS, k=2),
                                                             vf[hs, :, T:N].rearrange("p k s -> p s k").unsqueeze(3).to_broadcast([64, SEQS, 2, 4]), ALU.mult))
                ins = dve.tensor_tensor(o32[hs, :, T:N].rearrange("p (k i) s -> p s k i", k=2), od3,
                                        bank[4][hs, 0:64].rearrange("p (s k i) -> p s k i", s=SEQS, k=2), ALU.add)
            ins.then_inc(dec_d, 1)

            def maxima(e):
                b = e % 2
                dve.wait_ge(s_done, e + 1)
                link(dve, dve_step, steps, dve.scalar_tensor_tensor(out=sm[:, b, :], in0=bank[4 + b][:, 0:384], scalar=SCALE, in1=mask, op0=ALU.mult, op1=ALU.add))
                dve.tensor_reduce(mx[:, 2 * b:2 * b + 1], sm[:, b, 0:128], AX.X, ALU.max)
                link(dve, dve_step, steps, dve.tensor_reduce(mx[:, 2 * b + 1:2 * b + 2], sm[:, b, 128:384], AX.X, ALU.max))
                link(dve, dve_step, steps, dve.tensor_scalar(mx[:, 2 * b:2 * b + 2], mx[:, 2 * b:2 * b + 2], vs[:, V_SINK + e:V_SINK + e + 1], None, ALU.max))
                dve.tensor_scalar(nmx[:, 2 * b:2 * b + 2], mx[:, 2 * b:2 * b + 2], -1.0, None, ALU.mult).then_inc(s_max, 1)

            maxima(0)
            for e in range(AH):
                t, b = e // 2, e % 2
                hs = slice(64 * b, 64 * b + 64)
                if e + 1 < AH:
                    maxima(e + 1)
                dve.wait_ge(s_exp, e + 1)
                link(dve, dve_step, steps, dve.tensor_tensor(rr[:, 2 * b:2 * b + 2], rs[:, 2 * b:2 * b + 2], es[:, 2 * b:2 * b + 2], ALU.add))
                link(dve, dve_step, steps, dve.reciprocal(rr[:, 2 * b:2 * b + 2], rr[:, 2 * b:2 * b + 2]))
                dve.tensor_scalar(sm[:, b, 0:128], sm[:, b, 0:128], rr[:, 2 * b:2 * b + 1], None, ALU.mult)
                dve.tensor_scalar(sm[:, b, 128:384], sm[:, b, 128:384], rr[:, 2 * b + 1:2 * b + 2], None, ALU.mult).then_inc(s_prob, 1)
                dve.wait_ge(p_tr, e + 1)
                dve.tensor_copy(pT_[:, b, :], bank[6][:, 0:384]).then_inc(p_read, 1)
                dve.wait_ge(pv_done, e + 1)
                dve.tensor_copy(o32[hs, t, 0:T], bank[7][hs, 0:T]).then_inc(o_read, 1)
            for t in range(KT):
                dve.wait_ge(hh_ready, HREADY["o"] + t + 1)
                dve.tensor_tensor(hl[:, t, :], o32[:, t, :], hh[:, t, :].bitcast(F32), ALU.subtract).then_inc(hl_ready, 1)
            ahead_all("o", 8)
            add_b("o", 8, 1.0, G_F2 + 8, "f2i1")
            ffn_in("f2i1", "f2o1", 3)
            low_p(1)
            ahead_all("f2o1", FT)
            add_b("f2o1", FT, 0.5, G_PLE + 8, "pg1")
            embed("pp1", "pg1", 1, False)

        @block.gpsimd
        def _(pool):
            steps = [0]
            pool.dma_start(k_old, ck).then_inc(old_out, 16)
            pool.dma_start(v_old, cv).then_inc(old_out, 16)
            pool.wait_ge(sums_done, 2)
            for q in range(4):
                pool.dma_start(h0buf[q], ssm0[q]).then_inc(h0_landed[q], 16)
            pool.wait_ge(dec_sum, 1)
            pool.wait_ge(conv_sum, 3 * CT)
            pool.dma_start(conv_p, tail[:, :, :]).then_inc(conv_out, 16)
            pool.dma_start(conv_s[:, :, 0:2, :], convs[:, :, 1:3, :]).then_inc(conv_out, 16)
            pool.dma_start(conv_s[:, :, 2, :], decraw[:, :, :]).then_inc(conv_out, 16)
            for q in range(4, SEQS):
                pool.wait_ge(h0_used, q - 3)
                pool.dma_start(h0buf[q % 4], ssm0[q]).then_inc(h0_landed[q % 4], 16)
            for g in range(G):
                pool.wait_ge(ssd_carry, 2 * g + 2)
                pool.dma_start(ssm_p[:, 256 * g:256 * g + 256], state[:, g % 2, :]).then_inc(st_out[g % 2], 16)
            pool.wait_ge(dtx_row, 1)
            pool.dma_start(dtx_rows, dtxt).then_inc(dtx_out, 16)
            pool.wait_ge(dtx_out, 16)
            pool.wait_ge(pre_a, 3)
            pool.wait_ge(ssd_y, G)
            for q in range(SEQS):
                if q > 0:
                    pool.wait_ge(late_out, 16 * q)
                pool.dma_start(lateA, ssm0[q]).then_inc(late_in[0], 16)
                pool.dma_start(lateB, dtx_rows[q:q + 1, :].to_broadcast([P, XT * P])).then_inc(late_in[1], 16)
                pool.wait_ge(late_in[0], 16 * (q + 1))
                pool.tensor_tensor(lateA.rearrange("p (h w) -> p h w", h=HEADS), lateA.rearrange("p (h w) -> p h w", h=HEADS),
                                   da_bc[:, q, :].unsqueeze(2).to_broadcast([P, HEADS, 64]), ALU.mult)
                pool.wait_ge(late_in[1], 16 * (q + 1))
                link(pool, pool_step, steps, pool.tensor_tensor(lateB.rearrange("p (g w) -> p g w", g=G), lateB.rearrange("p (g w) -> p g w", g=G),
                                                                b_d[:, :, q].unsqueeze(2).to_broadcast([P, G, 256]), ALU.mult))
                link(pool, pool_step, steps, pool.tensor_tensor(lateA, lateA, lateB, ALU.add))
                pool.dma_start(ssm_s[q], lateA).then_inc(late_out, 16)
            pool.wait_ge(late_out, 16 * SEQS)
            pool.wait_ge(gn_ready, XT)
            pool.dma_start(kc, kcT).then_inc(cache_in, 16)
            pool.dma_start(vc, vc_in).then_inc(cache_in, 16)
            pool.wait_ge(roped, 2)
            pool.wait_ge(v_tok, 1)
            pool.dma_start(kv_p[0], kf[:, :, 128:256]).then_inc(kv_out, 16)
            pool.dma_start(kv_p[1], vf[:, :, 128:256]).then_inc(kv_out, 16)
            pool.dma_start(kv_new[0], kf[:, :, T:N]).then_inc(kv_out, 16)
            pool.dma_start(kv_new[1], vf[:, :, T:N]).then_inc(kv_out, 16)
            pool.wait_ge(kv_out, 64)
            pool.wait_ge(old_out, 32)
            pool.wait_ge(conv_out, 48)
            for b in range(2):
                pool.wait_ge(st_out[b], 16 * G // 2)


def in_a(w):
    m = w.shape[1] // P
    return w.reshape(KT, P, m, P).transpose(2, 1, 0, 3).reshape(m, P, UNIT)


def ffn_units(wi):
    return in_a(wi).reshape(2, FT, P, UNIT).transpose(1, 0, 2, 3).reshape(2 * FT, P, UNIT)


def in_b(w):
    return w.reshape(-1, P, UNIT)


def proj_units(w):
    return w.reshape(2, P, 2, 4, P).transpose(2, 1, 3, 0, 4).reshape(2, P, UNIT)


def columns(v):
    return v.reshape(-1, P).T


def constants():
    c = np.zeros((P, NC_), np.float32)
    k, m = np.arange(P)[:, None], np.arange(P)[None, :]
    c[:, C_ID:C_ID + P] = k == m
    c[:, C_TRI:C_TRI + P] = k <= m
    c[:, C_ONE:C_ONE + P] = 1
    c[:, C_BLK:C_BLK + P] = k // 64 == m // 64
    c[:, C_ROT:C_ROT + P] = 1.0 * ((k == m - 32) & (m % 64 >= 32)) - 1.0 * ((k == m + 32) & (m % 64 < 32))
    pos = np.concatenate([np.arange(T), np.full(SEQS, 1024)]).astype(np.float32)
    inv = np.float32(10000.0) ** (-np.arange(32, dtype=np.float32) / np.float32(32))
    ang = (pos[None, :] * inv[:, None]).astype(np.float32)[np.arange(P) % 32]
    c[:, C_COS:C_COS + N] = np.cos(ang)
    c[:, C_SIN:C_SIN + N] = np.sin(ang)
    far = np.float32(-1e30)
    c[:, C_MASK:C_MASK + 128] = np.where(m <= k, 0, far)
    c[:, C_MASK + 128:C_MASK + 256] = np.where(m >= k, 0, far)
    c[:, C_MASK + 256:C_MASK + 384] = np.where(m <= k, 0, far)
    c[:, C_IND:C_IND + 4] = k % 4 == np.arange(4)[None, :]
    c[:, C_SEL:C_SEL + G] = k % HEADS // 4 == np.arange(G)[None, :]
    return c


def kernel(**inputs):
    import concourse.bacc as bacc
    from concourse.bass_utils import run_bass_kernel_spmd

    a = {k: np.asarray(v) for k, v in inputs.items()}
    perm = [(2 * (t // 4) + b) * 4 + t % 4 for t in range(KT) for b in range(2)]
    ssm_in = a["ssm_in"][0]
    weights = np.concatenate([
        ffn_units(a["ffn1_wi"][0]), in_b(a["ffn1_wo"][0]),
        in_a(np.tile(ssm_in[:, 6144:6176], (1, 4))), in_a(ssm_in[:, 2048:6144]), in_a(ssm_in[:, 0:2048]),
        in_b(a["ssm_out"][0]),
        ffn_units(a["ffn2_wi"][0]), in_b(a["ffn2_wo"][0]), proj_units(a["ple_proj"][0]), in_a(a["ple_gate"][0]),
        in_a(a["w_kv"]),
        ffn_units(a["ffn1_wi"][1]), in_b(a["ffn1_wo"][1]),
        in_a(a["w_q"][0].reshape(D, AH, 64)[:, perm].reshape(D, D)), in_b(a["w_o"][0].reshape(AH, 64, D)[perm].reshape(D, D)),
        ffn_units(a["ffn2_wi"][1]), in_b(a["ffn2_wo"][1]), proj_units(a["ple_proj"][1]), in_a(a["ple_gate"][1]),
    ])
    assert weights.shape == (NU, P, UNIT)
    rows = lambda p, s: np.concatenate([p, s])
    fm = lambda r: r.T.reshape(-1, P, r.shape[0]).transpose(1, 0, 2)
    xT = fm(rows(a["x_prompt"][0], a["x_sample"][:, 0]))
    pT = np.stack([fm(rows(a["p_prompt"][l, 0], a["p_sample"][l, :, 0])) for l in range(2)])
    v = [columns(a[n][l]) for n in ("ffn1_norm", "mix_norm", "ffn2_norm", "ple_norm") for l in range(2)] + [columns(a["kv_norm"])]
    v += [columns(a["ssm_conv_w"][0, k]) for k in range(4)] + [columns(a["ssm_conv_b"][0])]
    v += [columns(np.repeat(a["ssm_d"][0], 64)), columns(a["ssm_norm"][0])]
    v += [np.tile(a["ssm_a_log"][0], 4)[:, None], np.tile(a["ssm_dt_bias"][0], 4)[:, None]]
    v += [np.tile(a["k_norm"], 2)[:, None], np.tile(a["q_norm"][0], 2)[:, None]]
    sinks = a["attn_sinks"][0]
    v += [sinks[[(2 * kp + b) * 4 + i for b in range(2) for _ in range(SEQS) for kp in range(2) for i in range(4)]][:, None]]
    v += [np.broadcast_to(sinks[perm][None, :], (P, AH))]
    vec = np.concatenate(v, axis=1)
    assert vec.shape == (P, NV)
    convst = a["state_conv"][0].reshape(SEQS, 3, CT, P).transpose(3, 2, 1, 0)
    ssm0 = a["state_ssm"][0].transpose(0, 3, 1, 2).reshape(SEQS, P, XT * P)
    ck = a["cache_k"].reshape(SEQS, WINDOW, 256)
    cv = a["cache_v"].reshape(SEQS, WINDOW, 256)
    kcT = a["cache_k"].reshape(SEQS, WINDOW, 2, 2, 64).transpose(3, 4, 2, 0, 1).reshape(P, 2, SEQS, WINDOW)
    vcT = cv.transpose(1, 0, 2)

    nc = bacc.Bacc("TRN2", target_bir_lowering=False, num_devices=1)
    arrays = {"weights": weights, "xT": xT, "pT": pT, "cst": constants(), "vec": vec, "convst": convst, "ssm0": ssm0,
              "kcT": kcT, "vcT": vcT, "ck": ck, "cv": cv}
    arrays = {k: np.ascontiguousarray(v_) for k, v_ in arrays.items()}
    ins = {k: nc.dram_tensor(k, v_.shape, mybir.dt.from_np(v_.dtype), kind="ExternalInput").ap() for k, v_ in arrays.items()}
    shapes = {"y": (P, KT, N), "ssm_p": (P, 2048), "conv_p": (P, CT, 3), "kv_p": (2, P, 2, 128), "ssm_s": (SEQS, P, 2048),
              "conv_s": (P, CT, 3, SEQS), "k_old": (SEQS, WINDOW - 1, 256), "v_old": (SEQS, WINDOW - 1, 256), "kv_new": (2, P, 2, SEQS)}
    outs = {k: nc.dram_tensor("out_" + k, s, F32, kind="ExternalOutput").ap() for k, s in shapes.items()}
    i = ins
    trunk_kernel(nc, i["weights"], i["xT"], i["pT"], i["cst"], i["vec"], i["convst"], i["ssm0"], i["kcT"], i["vcT"],
                 i["ck"][:, 1:, :], i["cv"][:, 1:, :], *outs.values())
    r = run_bass_kernel_spmd(nc, [arrays], core_ids=[0]).results[0]
    o = {k: np.asarray(r["out_" + k]) for k in shapes}

    y = o["y"].transpose(2, 1, 0).reshape(N, D)
    ssm_p = o["ssm_p"].reshape(P, HEADS, 64).transpose(1, 2, 0)[None, None]
    conv_p = o["conv_p"].transpose(2, 1, 0).reshape(1, 1, 3, CT * P)
    heads = lambda t: t.reshape(2, 64, 2, -1).transpose(3, 2, 0, 1).reshape(-1, 4, 64)
    k_p, v_p = heads(o["kv_p"][0])[None], heads(o["kv_p"][1])[None]
    ssm_s = o["ssm_s"].reshape(SEQS, P, HEADS, 64).transpose(0, 2, 3, 1)[None]
    conv_s = o["conv_s"].transpose(3, 2, 1, 0).reshape(1, SEQS, 3, CT * P)
    k_s, v_s = (np.concatenate([o[n].reshape(SEQS, WINDOW - 1, 4, 64), heads(o["kv_new"][j])[:, None]], axis=1)
                for j, n in enumerate(("k_old", "v_old")))
    return (y[None, :T], y[T:][:, None], ssm_p, conv_p, k_p, v_p, ssm_s, conv_s, k_s, v_s)
```

```python
from contextlib import ExitStack

import numpy as np

import concourse.bass as bass
from concourse import mybir

F32 = mybir.dt.float32
F32R = mybir.dt.float32r
ACT = mybir.ActivationFunctionType
ALU = mybir.AluOpType
AX = mybir.AxisListType

P = 128
D = 1024
KT = D // P
T = 256
SEQS = 8
N = T + SEQS
FT = 2816 // P
EPS = 1e-6
HEADS = 32
XT = 16
G = 8
CT = 32
WINDOW = 128
AH = 16
RING = 4
UNIT = KT * P
SCALE = 64 ** -0.5

STAGES = [("f1i0", 2 * FT), ("f1o0", FT), ("sin", 49), ("sout", XT), ("f2i0", 2 * FT), ("pp0", 2), ("f2o0", FT), ("pg0", 8),
          ("f1i1", 2 * FT), ("kv", 4), ("f1o1", FT), ("q", 8), ("o", 8), ("f2i1", 2 * FT), ("pp1", 2), ("f2o1", FT), ("pg1", 8)]
NU = sum(n for _, n in STAGES)
U0 = {}
for _name, _n in STAGES:
    U0[_name] = sum(n for _, n in STAGES[:len(U0)])
A0, _a = {}, 0
for _name, _n in STAGES:
    A0[_name] = _a
    if not (_name[:3] in ("f1o", "f2o") or _name in ("sout", "o")):
        _a += 4 * _n if _name[:2] == "pp" else _n
A0["end"] = _a
BSTAGE = {"f1o0": 0, "sout": 1, "f2o0": 2, "f1o1": 3, "o": 4, "f2o1": 5}
NORM = {"f1i0": 0, "sin": 1, "f2i0": 2, "pg0": 3, "f1i1": 4, "q": 5, "f2i1": 6, "pg1": 7}
POOLED = ["f1i0", "sin", "pg0", "f1i1", "q", "f2i1", "pg1"]
XREADY = {"f1i0": 0, "sin": 8, "f2i0": 16, "pg0": 24, "f1i1": 32, "q": 40, "f2i1": 48, "pg1": 56}
HREADY = {"f1o0": 0, "sout": FT, "f2o0": FT + XT, "f1o1": 2 * FT + XT, "o": 3 * FT + XT, "f2o1": 3 * FT + XT + 8}

HEAD_TILES, HEAD_BATCH = 10, 5

C_ID, C_TRI, C_ONE, C_BLK, C_ROT, C_COS, C_SIN, C_MASK = 0, 128, 256, 384, 512, 640, 640 + N, 640 + 2 * N
C_IND, C_SEL = C_MASK + 384, C_MASK + 388
C_EPS = C_SEL + G
C_WIN = C_EPS + 1
NC_ = C_WIN + 38
G_F1, G_MIX, G_F2, G_PLE, G_KV = 0, 16, 32, 48, 64
V_CW, V_CB, V_D, V_NG, V_ALOG, V_DTB, V_KN, V_QN, V_SINKD, V_SINK = 72, 200, 232, 248, 264, 265, 266, 267, 268, 269
NV = 269 + AH


DT_STEPS = 18
CHUNK0 = 3
H0_AT = 2
NORM_AT = [11, 12, 13, 14, 16, 17, 19, 21]
ROOT_AFTER = {1: (0, 2), 3: (2, 4), 5: (4, 6), 6: (6, 7), 7: (7, 8)}
APPLY_AT = [14, 15, 16, 17, 18, 19, 20, 21]
Z_AT = list(range(12)) + [15, 16, 17, 18]
SILU_AT = {9: (0, 8), 16: (8, 12), 19: (12, 16)}
SLOTS = NORM_AT[-1] + 1


def unit(base, i, j):
    return base + j + 4 * i, (base + j) // RING + i, (base + j) % RING


def trunk_kernel(nc, weights, xT, pT, cst, vec, convst, ssm0, kcT, vc_in, ck, cv,
                 y_out, ssm_p, conv_p, kv_p, ssm_s, conv_s, k_old, v_old, kv_new):
    dtx_rows = nc.dram_tensor("dtx_rows", (SEQS, XT * P), F32, kind="Internal").ap()
    with ExitStack() as ctx:
        def sb(name, shape, dt=F32):
            return ctx.enter_context(nc.sbuf_tensor(name, shape, dt))

        def sem(name):
            return ctx.enter_context(nc.semaphore(name))

        raw = sb("raw", [P, RING, UNIT])
        whi = sb("whi", [P, RING, UNIT], F32R)
        wlo = sb("wlo", [P, RING, UNIT], F32R)
        x = sb("x", [P, KT, N])
        xh = sb("xh", [P, KT, N], F32R)
        xl = sb("xl", [P, KT, N], F32R)
        sq = sb("sq", [P, KT * N])
        with nc.sbuf_tensor("h0", [P, 4, XT * P], F32) as h0buf_:
            h0buf = [h0buf_[:, b, :] for b in range(4)]
        hh = sb("hh", [P, FT, N], F32R)
        hl = sb("hl", [P, FT, N], F32R)
        xact = sb("xact", [P, CT, N])
        with nc.sbuf_tensor("xh2", [P, KT, N], F32R) as xh2, nc.sbuf_tensor("xl2", [P, KT, N], F32R) as xl2:
            pass
        zs = sb("zs", [P, XT, N])
        ph = sb("ph", [P, 2, N], F32R)
        pl = sb("pl", [P, 2, N], F32R)
        gu = sb("gu", [P, 4, N])
        rstd = sb("rstd", [P, N])
        cs = sb("cs", [P, NC_])
        vs = sb("vs", [P, NV])
        avec = sb("avec", [P, 1])
        gsq = sb("gsq", [P, 2, N])
        small = sb("small", [P, 1024])
        bank = [ctx.enter_context(nc.psum_tensor(f"bank{b}", [P, 512], F32)) for b in range(8)]

        ident, tri, ones = cs[:, C_ID:C_ID + P], cs[:, C_TRI:C_TRI + P], cs[:, C_ONE:C_ONE + P]
        eps = cs[:, C_EPS:C_EPS + 1]
        blk, rot = cs[:, C_BLK:C_BLK + P], cs[:, C_ROT:C_ROT + P]
        cosT, sinT, mask = cs[:, C_COS:C_COS + N], cs[:, C_SIN:C_SIN + N], cs[:, C_MASK:C_MASK + 384]
        sq3 = sq[:, :].rearrange("p (k n) -> p k n", k=KT)

        raw_landed = [sem(f"raw_landed{s}") for s in range(RING)]
        hi_ready = sem("hi_ready")
        lo_ready = sem("lo_ready")
        unit_used = sem("unit_used")
        a_free = sem("a_free")
        b_done = sem("b_done")
        b_free = sem("b_free")
        xh_ready = sem("xh_ready")
        xl_ready = sem("xl_ready")
        sq_ready = sem("sq_ready")
        sq_pair = sem("sq_pair")
        sums_done = sem("sums_done")
        std_ready = sem("std_ready")
        silu_done = sem("silu_done")
        h_ready = sem("h_ready")
        hh_ready = sem("hh_ready")
        hl_ready = sem("hl_ready")
        w_init = sem("w_init")
        init = sem("init")
        p_landed = sem("p_landed")
        ph_ready = sem("ph_ready")
        pl_ready = sem("pl_ready")
        pj_done = sem("pj_done")
        sig_done = sem("sig_done")
        dve_step = sem("dve_step")
        pool_step = sem("pool_step")
        stored = sem("stored")
        x_final = sem("x_final")
        conv_raw = sem("conv_raw")
        conv_first = sem("conv_first")
        conv_sum = sem("conv_sum")
        conv_act = sem("conv_act")
        dt_d_step = sem("dt_d_step")
        dt_a_step = sem("dt_a_step")
        dec_sum = sem("dec_sum")
        dec_act = sem("dec_act")
        pre_p = sem("pre_p")
        pre_d = sem("pre_d")
        pre_a = sem("pre_a")
        dtx_tr = sem("dtx_tr")
        dtx_row = sem("dtx_row")
        dtx_out = sem("dtx_out")
        h0_landed = [sem(f"h0_landed{b}") for b in range(4)]
        h0_used = sem("h0_used")
        ssd_in = sem("ssd_in")
        ssd_diff = sem("ssd_diff")
        ssd_sel = sem("ssd_sel")
        ssd_read = sem("ssd_read")
        ssd_exp = sem("ssd_exp")
        ssd_mm = sem("ssd_mm")
        ssd_part = sem("ssd_part")
        ssd_carry = sem("ssd_carry")
        ssd_isc = sem("ssd_isc")
        ssd_tr = sem("ssd_tr")
        ssd_y = sem("ssd_y")
        tok_ready = sem("tok_ready")
        z_silu = sem("z_silu")
        gated = sem("gated")
        gated_sq = sem("gated_sq")
        gated_sum = sem("gated_sum")
        gated_var = sem("gated_var")
        gated_std = sem("gated_std")
        gn_ready = sem("gn_ready")
        st_out = [sem("st_out0"), sem("st_out1")]
        conv_out = sem("conv_out")
        late_in = [sem("late_in0"), sem("late_in1")]
        late_out = sem("late_out")
        kvh_ready = sem("kvh_ready")
        kvl_ready = sem("kvl_ready")
        head_sq = sem("head_sq")
        head_sum = sem("head_sum")
        head_std = sem("head_std")
        head_inv = sem("head_inv")
        head_bc = sem("head_bc")
        head_n = sem("head_n")
        rot_done = sem("rot_done")
        roped = sem("roped")
        v_tr = sem("v_tr")
        v_tok = sem("v_tok")
        cache_in = sem("cache_in")
        old_out = sem("old_out")
        kv_out = sem("kv_out")
        dec_p = sem("dec_p")
        dec_d = sem("dec_d")
        dec_a = sem("dec_a")
        dec_a_go = sem("dec_a_go")
        s_done = sem("s_done")
        s_masked = sem("s_masked")
        s_max = sem("s_max")
        s_exp = sem("s_exp")
        s_prob = sem("s_prob")
        p_tr = sem("p_tr")
        p_read = sem("p_read")
        dec_o = sem("dec_o")
        dec_l = sem("dec_l")
        pv_done = sem("pv_done")

        block = ctx.enter_context(nc.Block())

        dd = small[0:64, 0:N]
        o_ = N
        dtT = [small[:, o_ + 32 * c:o_ + 32 * c + 32] for c in range(2)]
        o_ += 64
        da4 = [small[:, o_ + P * c:o_ + P * c + P] for c in range(2)]
        tok = sb("tok", [P, 2, 3, HEADS])
        da_bc = sb("da_bc", [P, SEQS, HEADS])
        da_d = sb("da_d", [P, XT, SEQS])
        dt_d = sb("dt_d", [P, XT, SEQS])
        dtx_d = sb("dtx_d", [P, XT, SEQS])
        bc_d = sb("bc_d", [P, G, SEQS])
        b_d = sb("b_d", [P, G, SEQS])
        c_d = sb("c_d", [P, G, SEQS])
        t1d = sb("t1d", [P, XT, SEQS])
        state = sb("state", [P, 2, 256])
        decraw = sb("decraw", [P, CT, SEQS])
        tail = sb("tail", [P, CT, 3])
        zf = zs[:, :, :].rearrange("p k n -> p (k n)")
        convs = zf[:, 8 * N:8 * N + 768].rearrange("p (k w s) -> p k w s", k=CT, w=3)
        dgl = zf[0:64, 12 * N:12 * N + 256].rearrange("p (s h) -> p s h", s=SEQS)
        cwork = zf[:, 13 * N:13 * N + 256].rearrange("p (k s) -> p k s", k=CT)
        csum = xact[:, :, T:N]
        hl_mid = hl[:, 10:16, :].rearrange("p k n -> p (k n)")
        diffR = [hl_mid[:, 512 * c:512 * c + 512] for c in range(2)]
        diffL = [hl_mid[:, 1024 + P * c:1024 + P * c + P] for c in range(2)]
        diffLg = [hl_mid[:, 1280 + P * b:1280 + P * b + P] for b in range(2)]
        ident_r, mask_r = hl[:, 16, 0:P], hl[:, 16, P:2 * P]
        cum4 = hl[:, 17, 0:2 * P]
        dtxt = sq[0:SEQS, 0:2048]
        late = xact[:, 16:32, :].rearrange("p k n -> p (k n)")
        lateA, lateB = late[:, 0:2048], late[:, 2048:4096]
        Dm = [sq[:, 512 * b:512 * b + 512] for b in range(2)]
        xdt = [sq[:, 1024 + 256 * b:1280 + 256 * b] for b in range(2)]
        xte = [sq[:, 1536 + 256 * b:1792 + 256 * b] for b in range(2)]
        guf = gu[:, :, :].rearrange("p k n -> p (k n)")
        cbb = [guf[:, 256 * b:256 * b + 256] for b in range(2)]
        isc, h1 = guf[:, 512:768], guf[:, 768:1024]
        xraw = guf[:, 0:4 * 260].rearrange("p (k n) -> p k n", k=4)
        pj = xact[:, 0:8, :]
        qf, kf, vf = xact[:, 0:8, :], xact[:, 8:10, :], xact[:, 10:12, :]
        xf = xact[:, :, :].rearrange("p k n -> p (k n)")
        vtok = xf[:, 12 * N:12 * N + 512].rearrange("p (c n) -> p c n", c=2)
        kc = xf[:, 14 * N:14 * N + 2048].rearrange("p (k s w) -> p k s w", k=2, s=SEQS)
        vc = xf[:, 22 * N:22 * N + 2048].rearrange("p (s n) -> p s n", s=SEQS)
        o32 = zs[:, 0, 0:KT * SEQS].rearrange("p (k s) -> p k s", k=KT)
        zb = zs[:, 8:16, :].rearrange("p k n -> p (k n)")
        sm = [zb[:, 384 * b:384 * b + 384] for b in range(3)]
        pT_ = [zb[:, 1152 + 384 * b:1536 + 384 * b] for b in range(2)]
        aw = gu
        mx, nmx, rs, es, rr = ([small[:, 6 * n_ + 2 * b:6 * n_ + 2 * b + 2] for b in range(3)] for n_ in range(5))
        nsink = small[:, 30:30 + AH]
        dS = small[:, 128:128 + 129]; dP = small[:, 260:260 + 129]; sTd = small[:, 400:528]
        prod = small[:, 528:656]; dgP = small[:, 656:784]; pTd = small[:, 784:912]; od = small[:, 912:976]
        dm = small[:, 976:984]

        def link(eng, step, count, ins):
            count[0] += 1
            ins.then_inc(step, 1)
            eng.wait_ge(step, count[0])

        @block.sync
        def _(sp):
            sp.dma_start(raw[:, 0, :], weights[0]).then_inc(raw_landed[0], 16)
            sp.dma_start(x[:, :, :], xT).then_inc(w_init, 16)
            sp.dma_start(vs[:, :], vec).then_inc(w_init, 16)
            for s in range(1, RING):
                sp.dma_start(raw[:, s, :], weights[s]).then_inc(raw_landed[s], 16)
            sp.dma_start(cs[:, :], cst).then_inc(init, 16)
            sp.dma_start(convs, convst).then_inc(init, 16)
            with sp.Fori(1, NU // RING) as i:
                for s in range(RING):
                    sp.wait_ge(lo_ready, i * RING + (s - RING + 1))
                    sp.dma_start(raw[:, s, :], weights[bass.ds(i * RING + s, 1)].rearrange("u p n -> p (u n)")).then_inc(raw_landed[s], 16)
            for u in range(NU // RING * RING, NU):
                sp.wait_ge(lo_ready, u - RING + 1)
                sp.dma_start(raw[:, u % RING, :], weights[u]).then_inc(raw_landed[u % RING], 16)
            for m in range(KT):
                sp.wait_ge(x_final, KT + m + 1)
                sp.dma_start(y_out[:, m, :], x[:, m, :]).then_inc(stored, 16)
            sp.wait_ge(stored, 16 * KT)

        @block.tensor
        def _(pe):
            pe.sem_inc(unit_used, RING)

            def split_products(out, w, tile, rh, rl, start, stop):
                c = slice(tile * P, tile * P + P)
                pe.matmul(out, whi[:, w, c], rh, start=start, stop=False)
                pe.matmul(out, whi[:, w, c], rl, start=False, stop=False)
                return pe.matmul(out, wlo[:, w, c], rh, start=False, stop=stop)

            def unit_a(stage, i, j, b_wait=None, x_wait=False, rh=xh, rl=xl, kv_wait=False, banks=4):
                u, _, s = unit(U0[stage], i, j)
                out = bank[(A0[stage] + j) % banks]
                pe.wait_ge(lo_ready, u + 1)
                pe.wait_ge(a_free, A0[stage] + j + 4 * i + 5 - banks)
                if b_wait is not None:
                    pe.wait_ge(b_free, 8 * b_wait + (A0[stage] + j) % 4 + 1)
                for k in range(KT):
                    if x_wait:
                        pe.wait_ge(xl_ready, XREADY[stage] + k + 1)
                    if kv_wait:
                        pe.wait_ge(kvl_ready, k + 1)
                    mm = split_products(out[:, 0:N], s, k, rh[:, k, :], rl[:, k, :], k == 0, k == KT - 1)
                mm.then_inc(unit_used, 1)

            def sums(stage, b_wait=None):
                if stage == "f1i0":
                    pe.wait_ge(init, 32)
                if stage in POOLED:
                    pe.wait_ge(sq_pair, 4 * POOLED.index(stage) + 4)
                else:
                    pe.wait_ge(sq_ready, 8 * NORM[stage] + 8)
                tiles = 1 if stage in POOLED else KT
                if b_wait is not None:
                    pe.wait_ge(b_free, 8 * b_wait + 5)
                for k in range(tiles):
                    mm = pe.matmul(bank[4][:, 0:N], ones, sq3[:, k, :], start=k == 0, stop=k == tiles - 1)
                mm.then_inc(sums_done, 1)

            def first_units(stage, n, b_wait, **ops):
                for j in range(n):
                    unit_a(stage, 0, j, b_wait if j < 4 else None, x_wait=(j == 0), **ops)
                    if j == 1:
                        sums(stage, b_wait)

            def first_units_p(stage, b_wait):
                for j in range(KT):
                    unit_a(stage, 0, j, x_wait=(j == 0))
                    if j == 1:
                        sums(stage, b_wait)

            def head_sum_(n_):
                pe.wait_ge(head_sq, n_ + 1)
                if n_ == HEAD_BATCH:
                    pe.wait_ge(head_std, 1)
                pe.matmul(bank[5][0:20, 0:N], cs[:, C_WIN + 18 - 2 * n_:C_WIN + 38 - 2 * n_], aw[:, n_ % 2, :],
                          start=n_ in (0, HEAD_BATCH), stop=n_ in (HEAD_BATCH - 1, HEAD_TILES - 1)).then_inc(head_sum, 1)

            def head_spread(n_):
                pe.wait_ge(head_inv, 1 if n_ < HEAD_BATCH else 2)
                if n_ > 0:
                    pe.wait_ge(head_n, max(n_ - 1, 1))
                if n_ == 1:
                    pe.wait_ge(v_tok, 1)
                for b in range(2):
                    mm = pe.matmul(bank[6 + n_ % 2][64 * b:64 * b + 64, 0:N], ident[0:20, 2 * n_ + b:2 * n_ + b + 1].to_broadcast([20, 64]),
                                   aw[0:20, 3, :], start=True, stop=True)
                mm.then_inc(head_bc, 1)

            def head_rot(n_, tile):
                pe.wait_ge(head_n, n_ + 1)
                if n_ > 0:
                    pe.wait_ge(roped, n_)
                pe.matmul(bank[4][:, 0:N], rot, tile, start=True, stop=True).then_inc(rot_done, 1)

            def decode_scores(q, kp):
                if q == 0 and kp == 0:
                    pe.wait_ge(cache_in, 32)
                    pe.wait_ge(a_free, A0["q"] + KT + 4)
                if q == 0:
                    pe.wait_ge(roped, 6 if kp == 0 else HEAD_TILES)
                for b in range(2):
                    hs = slice(64 * b, 64 * b + 64)
                    c_ = 8 * q + 4 * kp
                    mm = pe.matmul(bank[b][:, c_:c_ + 4], kc[hs, kp, q, :], qf[hs, 4 * kp:4 * kp + 4, T + q], start=True, stop=True)
                if q == SEQS - 1 and kp == 1:
                    mm.then_inc(dec_p, 1)

            def decode_values(q):
                if q == 0:
                    pe.wait_ge(dec_d, 4)
                for kp in range(2):
                    for b in range(2):
                        c_ = 8 * q + 4 * kp
                        mm = pe.matmul(bank[0][64 * b:64 * b + 64, c_:c_ + 4], vc[:, q, 64 * (2 * kp + b):64 * (2 * kp + b) + 64],
                                       pTd[:, 64 * b + c_:64 * b + c_ + 4], start=True, stop=True)
                if q == SEQS - 1:
                    mm.then_inc(dec_p, 1)

            def decode_step(e):
                if e < 4:
                    decode_scores(2 * e, 1)
                    decode_scores(2 * e + 1, 1)
                elif e == 5:
                    pe.wait_ge(dec_d, 2)
                    pe.transpose(bank[0][:, 128:256], sTd, ident)
                    pe.matmul(bank[0][0:64, 256:257], prod[0:64, 0:64], ones[0:64, 0:1], start=True, stop=True)
                    pe.matmul(bank[1][64:128, 256:257], prod[64:128, 0:64], ones[64:128, 0:1], start=True, stop=True).then_inc(dec_p, 1)
                elif e == 8:
                    pe.wait_ge(dec_d, 3)
                    pe.transpose(bank[0][:, 128:256], dP[:, 0:128], ident)
                    pe.matmul(bank[1][:, 128:256], ones, dgP, start=True, stop=True).then_inc(dec_p, 1)
                elif 10 <= e < 14:
                    decode_values(2 * (e - 10))
                    decode_values(2 * (e - 10) + 1)

            def ffn_in(stage, b_wait, **ops):
                first_units(stage, 4, b_wait, **ops)
                with pe.Fori(1, 2 * FT // RING) as i:
                    for j in range(RING):
                        unit_a(stage, i, j, **ops)

            def unit_b(stage, u, s, kt, where, order, first, hready):
                pe.wait_ge(lo_ready, u + 1)
                pe.wait_ge(hl_ready, hready)
                rh, rl = (hh[:, kt, :], hl[:, kt, :]) if isinstance(kt, int) else (
                    hh[:, bass.ds(kt, 1), :].rearrange("p a n -> p (a n)"), hl[:, bass.ds(kt, 1), :].rearrange("p a n -> p (a n)"))
                for m in order:
                    if first and m == 0:
                        pe.wait_ge(a_free, A0[where] + 4)
                    if first and m == 2 and stage == "o":
                        pe.wait_ge(hl_ready, HREADY[stage] + KT)
                    mm = split_products(bank[m][:, 0:N], s, m, rh, rl, first, False)
                mm.then_inc(unit_used, 1)

            def stage_b(stage, n, after):
                h0_ = HREADY[stage]
                u, _, s = unit(U0[stage], 0, 0)
                unit_b(stage, u, s, 0, after, (4, 5, 6, 7, 0, 1, 2, 3), True, h0_ + 1)
                loops = (n - 3) // RING
                with pe.Fori(0, loops) as i:
                    for j in range(1, RING + 1):
                        u, _, s = unit(U0[stage], i, j)
                        unit_b(stage, u, s, i * RING + j, after, range(8), False, i * RING + (h0_ + j + 1))
                for j in range(1 + loops * RING, n - 2):
                    u, _, s = unit(U0[stage], 0, j)
                    unit_b(stage, u, s, j, after, range(8), False, h0_ + j + 1)
                pe.wait_ge(lo_ready, U0[stage] + n)
                pe.wait_ge(hl_ready, h0_ + n)
                for m in range(KT):
                    for j in (n - 2, n - 1):
                        mm = split_products(bank[m][:, 0:N], (U0[stage] + j) % RING, m, hh[:, j, :], hl[:, j, :], False, j == n - 1)
                    if m < KT - 1:
                        mm.then_inc(b_done, 1)
                mm.then_inc(unit_used, 2)

            def embed(stage, layer):
                pe.wait_ge(pl_ready, layer + 1)
                for j in range(2):
                    u, _, s = unit(U0[stage], 0, j)
                    pe.wait_ge(lo_ready, u + 1)
                    for m in range(4):
                        a = A0[stage] + 4 * j + m
                        pe.wait_ge(a_free, a + 1)
                        for k in range(2):
                            mm = split_products(bank[a % 4][:, 0:N], s, 2 * m + k, ph[:, k, :], pl[:, k, :], k == 0, k == 1)
                        mm.then_inc(unit_used if m == 3 else pj_done, 1)

            def chunk_in(k):
                g, c = k // 2, k % 2
                r = slice(128 * c, 128 * c + 128)
                if k > 0:
                    pe.wait_ge(ssd_read, k)
                pe.matmul(bank[4][:, 0:128], xact[:, 16 + g, r], xact[:, 24 + g, r], start=True, stop=True)
                pe.transpose(bank[4][:, 128:256], xact[:, 16 + g, r], ident)
                pe.transpose(bank[4][:, 256:384], xact[:, 2 * g, r], ident)
                pe.transpose(bank[4][:, 384:512], xact[:, 2 * g + 1, r], ident).then_inc(ssd_in, 1)
                pe.wait_ge(ssd_sel, k + 1)
                if k > 0:
                    pe.wait_ge(ssd_exp, k)
                pe.matmul(bank[5][:, 0:512], diffLg[k % 2], diffR[c], start=True, stop=False)
                pe.matmul(bank[5][:, 0:512], ident_r, mask_r.unsqueeze(1).to_broadcast([P, 4, P]), start=False, stop=True).then_inc(ssd_diff, 1)

            def chunk_out(k):
                g, c = k // 2, k % 2
                yb = bank[6 + g % 2]
                pe.wait_ge(ssd_mm, k + 1)
                if k == 0:
                    pe.wait_ge(pre_d, 6)
                if g >= 2 and c == 0:
                    pe.wait_ge(ssd_y, g - 1)
                for h in range(4):
                    pe.matmul(yb[64 * (h % 2):64 * (h % 2) + 64, 256 * (h // 2) + 128 * c:256 * (h // 2) + 128 * c + 128],
                              xdt[k % 2][:, 64 * h:64 * h + 64], Dm[k % 2][:, 128 * h:128 * h + 128],
                              start=h < 2, stop=c == 0, skip_group_check=True)
                if k > 0:
                    pe.wait_ge(ssd_carry, k)
                mm = pe.matmul(bank[3][:, 0:256], cbb[k % 2][:, 128:256], xte[k % 2], start=True, stop=True)
                if c == 1:
                    mm = pe.matmul(bank[3][:, 256:512], xact[:, 24 + g, 128:256], h1, start=True, stop=True)
                mm.then_inc(ssd_part, 1)

            def add_inter(g):
                pe.wait_ge(ssd_isc, g + 1)
                for n_ in range(2):
                    mm = pe.matmul(bank[6 + g % 2][:, 256 * n_ + 128:256 * n_ + 256], isc[:, 128 * n_:128 * n_ + 128], ident,
                                   start=False, stop=True, skip_group_check=True)
                mm.then_inc(ssd_tr, 1)

            def decode_state(q):
                pe.wait_ge(h0_landed[q % 4], 16 * (q // 4 + 1))
                for j in range(XT):
                    mm = pe.matmul(bank[2][:, 8 * j + q:8 * j + q + 1], h0buf[q % 4][:, 128 * j:128 * j + 128],
                                   c_d[:, j // 2, q:q + 1], start=True, stop=True)
                mm.then_inc(h0_used, 1)

            def norm_sums(g):
                pe.wait_ge(gated_sq, g + 1)
                if g > 0:
                    pe.wait_ge(gated_var, g)
                pe.matmul(bank[2][:, 0:N], ones, gsq[:, 0, :], start=True, stop=False)
                pe.matmul(bank[2][:, 0:N], ones, gsq[:, 1, :], start=False, stop=True).then_inc(gated_sum, 1)

            ffn_in("f1i0", None)
            stage_b("f1o0", FT, "sin")
            first_units("sin", 5, 0)
            with pe.Fori(0, 7) as i:
                for j in range(5, 9):
                    unit_a("sin", i, j)
            def z_unit(s_):
                if s_ in Z_AT:
                    unit_a("sin", 0, 33 + Z_AT.index(s_), banks=2)

            pe.transpose(bank[4][:, 0:64], dd[:, 0:128], ident[0:64, 0:64])
            pe.transpose(bank[4][:, 64:128], dd[:, 128:256], ident[0:64, 0:64]).then_inc(pre_p, 1)
            z_unit(0)
            pe.wait_ge(pre_d, 1)
            for c in range(2):
                dta = da4[c][:, 0:HEADS]
                pe.matmul(bank[5][:, 64 * c:64 * c + 32], tri, dta, start=True, stop=True)
                pe.matmul(bank[5][:, 64 * c + 32:64 * c + 64], ones, dta, start=True, stop=True)
                mm = pe.matmul(bank[2][:, 128 * c:128 * c + 128], da4[c], tri, start=True, stop=True)
            mm.then_inc(pre_p, 1)
            z_unit(1)
            pe.wait_ge(pre_d, 3)
            pe.wait_ge(a_free, A0["sin"] + 33 + 4)
            pe.matmul(bank[7][:, 0:256], ones[32:64, :], dgl[32:64], start=True, stop=True)
            pe.matmul(bank[6][:, 0:256], ones[0:32, :], dgl[0:32], start=True, stop=True)
            pe.matmul(bank[3][:, 0:64], ones, bc_d[:, :, :], start=True, stop=True).then_inc(pre_p, 1)
            pe.wait_ge(pre_d, 5)
            for s_ in range(2, SLOTS):
                z_unit(s_)
                if 0 <= s_ - H0_AT < SEQS:
                    decode_state(s_ - H0_AT)
                k = s_ - CHUNK0
                if 0 <= k < 2 * G:
                    chunk_in(k)
                if 0 <= k - 3 < 2 * G and k % 2 == 1:
                    add_inter((k - 3) // 2)
                if 0 <= k - 1 < 2 * G:
                    chunk_out(k - 1)
                if s_ in NORM_AT:
                    norm_sums(NORM_AT.index(s_))
                if s_ == SLOTS - 2:
                    pe.wait_ge(ssd_y, G)
                    for j in range(XT):
                        mm = pe.transpose(bank[3 + j // 4][0:SEQS, 128 * (j % 4):128 * (j % 4) + 128], dtx_d[:, j, :], ident)
                    mm.then_inc(dtx_tr, 1)
            pe.wait_ge(gated_var, G)
            pe.wait_ge(dtx_row, 1)
            stage_b("sout", XT, "f2i0")
            ffn_in("f2i0", 1)
            embed("pp0", 0)
            stage_b("f2o0", FT, "pg0")
            first_units_p("pg0", 2)
            ffn_in("f1i1", None, rh=xh2, rl=xl2)
            for j in range(4):
                unit_a("kv", 0, j, kv_wait=(j == 0))
            stage_b("f1o1", FT, "q")
            for t in range(HEAD_TILES + 6):
                if t < KT:
                    unit_a("q", 0, t, 3 if t < 4 else None, x_wait=(t == 0))
                if t == 0:
                    pe.wait_ge(b_free, 8 * 4)
                    for c in range(2):
                        for n_ in range(2):
                            mm = pe.transpose(bank[7][:, 256 * c + 128 * n_:256 * c + 128 * n_ + 128], vf[:, n_, 128 * c:128 * c + 128], ident)
                    mm.then_inc(v_tr, 1)
                if t == 1:
                    sums("q", 3)
                if t < HEAD_TILES:
                    head_sum_(t)
                if 0 <= t - 5 < HEAD_TILES:
                    head_spread(t - 5)
                if 0 <= t - 6:
                    head_rot(t - 6, kf[:, t - 6, :] if t < 8 else qf[:, t - 8, :])
                if t in (12, 13, 14):
                    for q in range(3 * (t - 12), min(3 * (t - 11), SEQS)):
                        decode_scores(q, 0)
            def scores(e):
                t, b = e // 2, e % 2
                hs = slice(64 * b, 64 * b + 64)
                if e == 0:
                    pe.wait_ge(roped, HEAD_TILES)
                if e >= 2:
                    pe.wait_ge(s_masked, e - 1)
                k = kf[hs, t // 4, :]
                pe.matmul(bank[4 + b][:, 0:128], qf[hs, t, 0:128], k[:, 0:128], start=True, stop=True)
                pe.matmul(bank[4 + b][:, 128:384], qf[hs, t, 128:256], k[:, 0:256], start=True, stop=True).then_inc(s_done, 1)

            def transposes(e):
                pe.wait_ge(s_prob, e + 1)
                if e >= 2:
                    pe.wait_ge(p_read, e - 1)
                for n_ in range(3):
                    mm = pe.transpose(bank[6 + e % 2][:, 128 * n_:128 * n_ + 128], sm[e % 3][:, 128 * n_:128 * n_ + 128], ident)
                mm.then_inc(p_tr, 1)

            def weighted_sum(e):
                t, b = e // 2, e % 2
                pe.wait_ge(p_read, e + 1)
                if t >= 2 and b == 0:
                    pe.wait_ge(hl_ready, HREADY["o"] + t - 1)
                ob = bank[2 + t % 2][64 * b:64 * b + 64, :]
                v_ = slice(64 * (2 * (t // 4) + b), 64 * (2 * (t // 4) + b) + 64)
                pe.matmul(ob[:, 0:128], vtok[:, 0, v_], pT_[e % 2][:, 0:128], start=True, stop=True)
                pe.matmul(ob[:, 128:256], vtok[:, 0, v_], pT_[e % 2][:, 128:256], start=True, stop=False)
                pe.matmul(ob[:, 128:256], vtok[:, 1, v_], pT_[e % 2][:, 256:384], start=False, stop=True).then_inc(pv_done, 1)

            scores(0)
            scores(1)
            pe.wait_ge(v_tok, 1)
            for e in range(AH + 3):
                if 0 <= e - 2 < AH:
                    transposes(e - 2)
                if 0 <= e - 3:
                    weighted_sum(e - 3)
                if e + 2 < AH:
                    scores(e + 2)
                decode_step(e)
            pe.wait_ge(dec_l, 1)
            stage_b("o", 8, "f2i1")
            ffn_in("f2i1", 4)
            embed("pp1", 1)
            stage_b("f2o1", FT, "pg1")
            first_units_p("pg1", 5)

        @block.scalar
        def _(act):
            steps = [0]

            def round_unit(u, q, s):
                act.wait_ge(raw_landed[s], q * 16 + 16)
                act.wait_ge(unit_used, u + 1)
                act.activation(whi[:, s, :], raw[:, s, :], ACT.Copy).then_inc(hi_ready, 1)

            def ahead(stage, i, j):
                if U0[stage] + RING + j < NU:
                    round_unit(*unit(U0[stage] + RING, i, j))

            def ahead_all(stage, n):
                n -= 2
                if n >= 8:
                    with act.Fori(0, n // RING) as i:
                        for j in range(RING):
                            ahead(stage, i, j)
                for j in range(n // RING * RING if n >= 8 else 0, n):
                    ahead(stage, 0, j)

            def high_x(m, gain, xh=xh):
                act.activation(xh[:, m, :], x[:, m, :], ACT.Copy, scale=vs[:, gain + m:gain + m + 1]).then_inc(xh_ready, 1)

            def square_x(m):
                act.activation(sq3[:, m, :], x[:, m, :], ACT.Square).then_inc(sq_ready, 1)

            def split_tile(m, gain, xh=xh):
                high_x(m, gain, xh)
                square_x(m)

            def split_x(gain, b_stage, stage=None, n=0):
                for m in range(KT):
                    if b_stage is not None:
                        act.wait_ge(b_free, 8 * b_stage + m + 1)
                    split_tile(m, gain)
                for j in range(max(n - 2, 0), n):
                    ahead(stage, 0, j)

            def root(stage):
                act.wait_ge(sums_done, NORM[stage] + 1)
                act.activation(rstd[:, :], bank[4][:, 0:N], ACT.Sqrt, scale=1.0 / D, bias=eps).then_inc(std_ready, 1)

            def ffn_in(stage, out, ffn, aside=None):
                def silu(i, p):
                    act.wait_ge(a_free, A0[stage] + 4 * i + 2 * p + 1 + 4)
                    act.activation(gu[:, 2 * p, :], gu[:, 2 * p, :], ACT.Silu).then_inc(silu_done, 1)

                def round_h(i, p):
                    act.wait_ge(h_ready, FT * ffn + 2 * i + p + 1)
                    dst = hh[:, p, :] if isinstance(i, int) else hh[:, bass.ds(2 * i + p, 1), :].rearrange("p a n -> p (a n)")
                    act.activation(dst, gu[:, 2 * p + 1, :], ACT.Copy).then_inc(hh_ready, 1)

                ahead(stage, 0, 0)
                ahead(stage, 0, 1)
                if stage in NORM:
                    root(stage)
                act.preload_act_table(ACT.Silu)
                silu(0, 0)
                ahead(stage, 0, 2)
                round_h(0, 0)
                silu(0, 1)
                ahead(stage, 0, 3)
                round_h(0, 1)
                if aside:
                    aside()
                with act.Fori(1, 2 * FT // RING) as i:
                    ahead(stage, i, 0)
                    silu(i, 0)
                    ahead(stage, i, 1)
                    round_h(i, 0)
                    ahead(stage, i, 2)
                    silu(i, 1)
                    ahead(stage, i, 3)
                    round_h(i, 1)

            def gates(gate, layer, gain):
                root(gate)
                for j in range(KT + 2):
                    if j < KT:
                        ahead(gate, 0, j)
                        act.wait_ge(a_free, A0[gate] + j + 1 + 4)
                        act.activation(gu[:, j % 4, :], gu[:, j % 4, :], ACT.Sigmoid).then_inc(sig_done, 1)
                    if gain is not None and j >= 2:
                        act.wait_ge(x_final, j - 1)
                        split_tile(j - 2, gain, xh2)

            def split_p(layer):
                act.wait_ge(p_landed, 16 * (layer + 1))
                act.activation(ph[:, :, :], gsq[:, :, :], ACT.Copy).then_inc(ph_ready, 1)

            def head_square(n_, tile, a):
                act.wait_ge(a_free, a + 1 + 4)
                if n_ < 2:
                    act.wait_ge(hl_ready, HREADY["o"])
                else:
                    act.wait_ge(head_sum, n_ - 1)
                act.activation(aw[:, n_ % 2, :], tile, ACT.Square).then_inc(head_sq, 1)

            def head_root(batch):
                act.wait_ge(head_sum, HEAD_TILES if batch else HEAD_BATCH)
                if batch:
                    act.wait_ge(head_bc, HEAD_BATCH)
                act.activation(aw[0:20, 3, :], bank[5][0:20, 0:N], ACT.Sqrt, scale=1.0 / 64, bias=eps[0:20]).then_inc(head_std, 1)

            round_unit(*unit(0, 0, 0))
            act.wait_ge(w_init, 32)
            for m in range(KT):
                high_x(m, G_F1)
            for u in range(1, RING):
                round_unit(*unit(0, 0, u))
                for m in range(3 * u - 3, min(3 * u, KT)):
                    square_x(m)
            ffn_in("f1i0", "f1o0", 0)
            ahead_all("f1o0", FT)
            split_x(G_MIX, 0, "f1o0", FT)
            ahead("sin", 0, 0)
            root("sin")
            act.activation(avec[0:32, :], vs[0:32, V_ALOG:V_ALOG + 1], ACT.Exp).then_inc(dt_a_step, 1)
            act.wait_ge(dt_d_step, 2)
            act.activation(zs[0:64, 1, :], zs[0:64, 1, :], ACT.Exp).then_inc(dt_a_step, 1)
            act.preload_act_table(ACT.Silu)

            def tap_last(i, p, tile):
                act.wait_ge(conv_raw, tile + 1)
                one = (lambda a: a[:, p, :]) if isinstance(i, int) else (lambda a: a[:, bass.ds(tile, 1), :].rearrange("p a n -> p (a n)"))
                act.activation(one(xact)[:, 0:T], xraw[:, p, 3:259], ACT.Identity, scale=cw3(i, p, tile), bias=cb(i, p, tile)).then_inc(conv_first, 1)

            def cw3(i, p, tile):
                c = V_CW + 3 * CT
                return vs[:, c + p:c + p + 1] if isinstance(i, int) else vs[:, bass.ds(tile + c, 1)]

            def cb(i, p, tile):
                return vs[:, V_CB + p:V_CB + p + 1] if isinstance(i, int) else vs[:, bass.ds(tile + V_CB, 1)]

            def conv_silu(i, p, tile):
                t_ = xact[:, p, 0:T] if isinstance(i, int) else xact[:, bass.ds(tile, 1), 0:T].rearrange("p a n -> p (a n)")
                act.activation(t_, t_, ACT.Silu).then_inc(conv_act, 1)

            def conv_body(i, j0):
                for p in range(4):
                    ahead("sin", *((0, j0 + p) if isinstance(i, int) else (i - 1, j0 + p)))
                    first = isinstance(i, int) and p == 0
                    if not first:
                        act.wait_ge(conv_sum, 3 * (i * 4) + 3 * p)
                    tap_last(i, p, i * 4 + p)
                    if not first:
                        conv_silu(i, p - 1, i * 4 + (p - 1))

            conv_body(0, 1)
            with act.Fori(1, CT // 4) as i:
                conv_body(i, 5)
            act.wait_ge(conv_sum, 3 * CT)
            act.activation(xact[:, CT - 1, 0:T], xact[:, CT - 1, 0:T], ACT.Silu).then_inc(conv_act, 1)
            act.wait_ge(dec_sum, 1)
            act.activation(csum, csum, ACT.Silu).then_inc(dec_act, 1)
            ahead("sin", 0, 33)
            act.wait_ge(pre_p, 2)
            act.activation(cum4, bank[2][:, 0:256], ACT.Copy).then_inc(pre_a, 1)
            act.wait_ge(pre_d, 4)
            act.activation(tok[:, :, :, :], tok[:, :, :, :], ACT.Exp).then_inc(pre_a, 1)
            ahead("sin", 0, 34)

            def select(k):
                g, c = k // 2, k % 2
                if k >= 2:
                    act.wait_ge(ssd_diff, k - 1)
                act.activation(diffLg[k % 2], diffL[c].bitcast(F32), ACT.Copy, scale=cs[:, C_SEL + g:C_SEL + g + 1]).then_inc(ssd_sel, 1)

            act.wait_ge(pre_d, 5)
            select(0)
            act.wait_ge(pre_d, 6)
            act.activation(da_d[:, :, :], da_d[:, :, :], ACT.Exp)
            act.activation(da_bc[:, :, :], da_bc[:, :, :], ACT.Exp).then_inc(pre_a, 1)

            def zsilu(t0, t1):
                act.wait_ge(a_free, A0["sin"] + 33 + t1 + 4)
                act.activation(zs[:, t0:t1, :], zs[:, t0:t1, :], ACT.Silu).then_inc(z_silu, 1)

            for s_ in range(2, SLOTS):
                if s_ in Z_AT:
                    ahead("sin", 0, 33 + Z_AT.index(s_))
                if s_ in SILU_AT:
                    zsilu(*SILU_AT[s_])
                k = s_ - CHUNK0
                if 0 <= k < 2 * G:
                    if k + 1 < 2 * G:
                        select(k + 1)
                    act.wait_ge(ssd_diff, k + 1)
                    if k >= 2:
                        act.wait_ge(ssd_part, k - 1)
                    act.activation(Dm[k % 2], bank[5][:, 0:512], ACT.Exp).then_inc(ssd_exp, 1)
                if s_ in NORM_AT:
                    g = NORM_AT.index(s_)
                    act.wait_ge(gated, g + 1)
                    if g > 0:
                        act.wait_ge(gated_sum, g)
                    act.activation(gsq[:, :, :], zs[:, 2 * g:2 * g + 2, :], ACT.Square).then_inc(gated_sq, 1)
                    act.wait_ge(gated_sum, g + 1)
                    act.activation(xact[:, 2 * g, :], bank[2][:, 0:N], ACT.Identity, scale=1.0 / 256, bias=eps).then_inc(gated_var, 1)
                    if g in ROOT_AFTER:
                        g0, g1 = ROOT_AFTER[g]
                        act.wait_ge(gated_var, g + 1)
                        v_ = xact[:, 2 * g0:2 * g1 - 1:2, :]
                        act.activation(v_, v_, ACT.Sqrt).then_inc(gated_std, 1)
                if s_ in APPLY_AT:
                    g = APPLY_AT.index(s_)
                    for t in (2 * g, 2 * g + 1):
                        act.wait_ge(gn_ready, t + 1)
                        act.activation(hh[:, t, :], zs[:, t, :], ACT.Copy).then_inc(hh_ready, 1)
            ahead_all("sout", XT)
            act.wait_ge(dtx_out, 16)
            split_x(G_F2, 1, "sout", XT)
            act.wait_ge(gated_sum, 8)
            act.dma_start(gsq[:, :, :], pT[0]).then_inc(p_landed, 16)
            ffn_in("f2i0", "f2o0", 1, lambda: split_p(0))
            ahead("pp0", 0, 0)
            ahead("pp0", 0, 1)
            ahead_all("f2o0", FT)
            split_x(G_PLE, 2, "f2o0", FT)
            gates("pg0", 0, G_F1 + 8)
            def kv_high():
                for m in range(KT):
                    act.activation(xh[:, m, :], x[:, m, :], ACT.Copy, scale=vs[:, G_KV + m:G_KV + m + 1]).then_inc(kvh_ready, 1)

            ffn_in("f1i1", "f1o1", 2, kv_high)
            for j in range(4):
                ahead("kv", 0, j)
            ahead_all("f1o1", FT)
            split_x(G_MIX + 8, 3, "f1o1", FT)
            for t in range(HEAD_TILES):
                head_square(t, kf[:, t, :] if t < 2 else qf[:, t - 2, :], A0["kv"] + t if t < 2 else A0["q"] + t - 2)
                if t < KT:
                    ahead("q", 0, t)
                if t == 1:
                    root("q")
                if t == HEAD_BATCH - 1:
                    head_root(0)
            head_root(1)
            def decode_exp():
                act.wait_ge(dec_a_go, 1)
                act.activation(dP, dS, ACT.Exp, bias=dm[:, 1:2], accum_out=dm[:, 2:3])
                act.activation(dm[:, 3:4], dm[:, 1:2], ACT.Exp, bias=vs[:, V_SINKD:V_SINKD + 1]).then_inc(dec_a, 1)

            for e in range(AH + 4):
                if 0 <= e - 3 < AH:
                    n_ = e - 3
                    act.wait_ge(p_tr, n_ + 1)
                    if n_ >= 2:
                        act.wait_ge(pv_done, n_ - 1)
                    act.activation(pT_[n_ % 2], bank[6 + n_ % 2][:, 0:384], ACT.Copy).then_inc(p_read, 1)
                if e == 7:
                    decode_exp()
                if e < AH:
                    b = e % 3
                    act.wait_ge(s_max, e + 1)
                    act.activation(sm[b][:, 0:128], sm[b][:, 0:128], ACT.Exp, bias=nmx[b][:, 0:1], accum_out=rs[b][:, 0:1])
                    act.activation(sm[b][:, 128:384], sm[b][:, 128:384], ACT.Exp, bias=nmx[b][:, 1:2], accum_out=rs[b][:, 1:2])
                    act.activation(es[b], nmx[b], ACT.Exp, bias=vs[:, V_SINK + e:V_SINK + e + 1]).then_inc(s_exp, 1)
                if e == 15:
                    act.wait_ge(dec_d, 5)
                    act.activation(hh[:, 0:KT, T:N], o32, ACT.Copy).then_inc(dec_o, 1)
                if e >= 5 and e % 2 == 1:
                    t = (e - 5) // 2
                    act.wait_ge(pv_done, 2 * t + 2)
                    act.activation(hh[:, t, 0:T], bank[2 + t % 2][:, 0:T], ACT.Copy).then_inc(hh_ready, 1)
            ahead_all("o", 8)
            split_x(G_F2 + 8, 4, "o", 8)
            act.dma_start(gsq[:, :, :], pT[1]).then_inc(p_landed, 16)
            ffn_in("f2i1", "f2o1", 3, lambda: split_p(1))
            ahead("pp1", 0, 0)
            ahead("pp1", 0, 1)
            ahead_all("f2o1", FT)
            split_x(G_PLE + 8, 5, "f2o1", FT)
            gates("pg1", 1, None)

        @block.vector
        def _(dve):
            steps = [0]

            def low_unit(u, q, s):
                dve.wait_ge(hi_ready, u + 1)
                dve.tensor_tensor(wlo[:, s, :], raw[:, s, :], whi[:, s, :].bitcast(F32), ALU.subtract).then_inc(lo_ready, 1)

            def ahead(stage, i, j):
                if U0[stage] + RING + j < NU:
                    low_unit(*unit(U0[stage] + RING, i, j))

            def ahead_all(stage, n):
                n -= 2
                if n >= 8:
                    with dve.Fori(0, n // RING) as i:
                        for j in range(RING):
                            ahead(stage, i, j)
                for j in range(n // RING * RING if n >= 8 else 0, n):
                    ahead(stage, 0, j)

            def low_x(m, gain, n_, xh=xh, xl=xl):
                dve.wait_ge(xh_ready, n_ + m + 1)
                dve.scalar_tensor_tensor(out=xl[:, m, :], in0=x[:, m, :], scalar=vs[:, gain + m:gain + m + 1],
                                         in1=xh[:, m, :].bitcast(F32), op0=ALU.mult, op1=ALU.subtract).then_inc(xl_ready, 1)

            def add_b(stage, n, scale, gain, after):
                b = BSTAGE[stage]
                for m in range(KT):
                    if m < 7:
                        dve.wait_ge(b_done, 7 * b + m + 1)
                    else:
                        dve.wait_ge(unit_used, U0[stage] + n + RING)
                    dve.scalar_tensor_tensor(out=x[:, m, :], in0=bank[m][:, 0:N], scalar=scale, in1=x[:, m, :],
                                             op0=ALU.mult, op1=ALU.add).then_inc(b_free, 1)
                    if m > 0:
                        low_x(m - 1, gain, XREADY[after])
                low_x(7, gain, XREADY[after])
                for j in range(n - 2, n):
                    ahead(stage, 0, j)

            def row_factor(stage):
                dve.wait_ge(std_ready, NORM[stage] + 1)
                link(dve, dve_step, steps, dve.reciprocal(rstd[:, :], rstd[:, :]))

            def take(dst, stage, j, i=0, cols=slice(0, N), signal=True, banks=4):
                dve.wait_ge(unit_used, U0[stage] + j + 4 * i + 1 + RING)
                ins = dve.tensor_tensor(dst, bank[(A0[stage] + j) % banks][:, cols], rstd[:, cols], ALU.mult)
                return ins.then_inc(a_free, 1) if signal else ins

            def ffn_in(stage, out, ffn, aside=None):
                def gate(i, p):
                    take(gu[:, 2 * p, :], stage, 2 * p, i)

                def up(i, p):
                    take(gu[:, 2 * p + 1, :], stage, 2 * p + 1, i)

                def hidden(i, p):
                    dve.wait_ge(silu_done, FT * ffn + 2 * i + p + 1)
                    dve.wait_ge(a_free, A0[stage] + 4 * i + 2 * p + 2 + 4)
                    dve.tensor_tensor(gu[:, 2 * p + 1, :], gu[:, 2 * p, :], gu[:, 2 * p + 1, :], ALU.mult).then_inc(h_ready, 1)

                def low_h(i, p):
                    dve.wait_ge(hh_ready, HREADY[out] + 2 * i + p + 1)
                    one = (lambda a: a[:, p, :]) if isinstance(i, int) else (lambda a: a[:, bass.ds(2 * i + p, 1), :].rearrange("p a n -> p (a n)"))
                    dve.tensor_tensor(one(hl), gu[:, 2 * p + 1, :], one(hh).bitcast(F32), ALU.subtract).then_inc(hl_ready, 1)

                ahead(stage, 0, 0)
                ahead(stage, 0, 1)
                if stage in NORM:
                    row_factor(stage)
                gate(0, 0)
                up(0, 0)
                hidden(0, 0)
                gate(0, 1)
                ahead(stage, 0, 2)
                low_h(0, 0)
                up(0, 1)
                ahead(stage, 0, 3)
                hidden(0, 1)
                low_h(0, 1)
                if aside:
                    aside()
                with dve.Fori(1, 2 * FT // RING) as i:
                    gate(i, 0)
                    ahead(stage, i, 0)
                    up(i, 0)
                    ahead(stage, i, 1)
                    hidden(i, 0)
                    gate(i, 1)
                    ahead(stage, i, 2)
                    low_h(i, 0)
                    up(i, 1)
                    ahead(stage, i, 3)
                    hidden(i, 1)
                    low_h(i, 1)

            def embed(stage, layer):
                for j in range(2):
                    for m in range(4):
                        if m < 3:
                            dve.wait_ge(pj_done, 3 * (2 * layer + j) + m + 1)
                        else:
                            dve.wait_ge(unit_used, U0[stage] + j + 1 + RING)
                        dve.tensor_copy(pj[:, 4 * j + m, :], bank[(A0[stage] + 4 * j + m) % 4][:, 0:N]).then_inc(a_free, 1)
                    ahead(stage, 0, j)

            def gates(gate, layer, gain):
                def gated_add(j):
                    t_ = gu[:, j % 4, :]
                    dve.wait_ge(sig_done, KT * layer + j + 1)
                    link(dve, dve_step, steps, dve.tensor_tensor(t_, t_, pj[:, j, :], ALU.mult))
                    dve.tensor_tensor(x[:, j, :], x[:, j, :], t_, ALU.add).then_inc(x_final, 1)

                row_factor(gate)
                for j in range(KT + 3):
                    if j < KT:
                        take(gu[:, j % 4, :], gate, j)
                    if 1 <= j <= KT:
                        gated_add(j - 1)
                    if j < KT:
                        ahead(gate, 0, j)
                    if gain is not None and j >= 3:
                        low_x(j - 3, gain, XREADY["f1i1"], xh2, xl2)

            def low_kv(m):
                dve.wait_ge(kvh_ready, m + 1)
                dve.scalar_tensor_tensor(out=xl[:, m, :], in0=x[:, m, :], scalar=vs[:, G_KV + m:G_KV + m + 1],
                                         in1=xh[:, m, :].bitcast(F32), op0=ALU.mult, op1=ALU.subtract).then_inc(kvl_ready, 1)

            def low_p(layer):
                dve.wait_ge(ph_ready, layer + 1)
                dve.tensor_tensor(pl[:, :, :], gsq[:, :, :], ph[:, :, :].bitcast(F32), ALU.subtract).then_inc(pl_ready, 1)

            def head_inverse(batch):
                dve.wait_ge(head_std, batch + 1)
                dve.reciprocal(aw[0:20, 3, :], aw[0:20, 3, :]).then_inc(head_inv, 1)

            def head_norm(n_, tile, gain):
                dve.wait_ge(head_bc, n_ + 1)
                dve.scalar_tensor_tensor(out=tile, in0=tile, scalar=vs[:, gain:gain + 1], in1=bank[6 + n_ % 2][:, 0:N],
                                         op0=ALU.mult, op1=ALU.mult).then_inc(head_n, 1)

            def rope(n_, tile):
                dve.wait_ge(rot_done, n_ + 1)
                dve.tensor_tensor(aw[:, 2, :], bank[4][:, 0:N], sinT, ALU.mult)
                link(dve, dve_step, steps, dve.tensor_tensor(tile, tile, cosT, ALU.mult))
                dve.tensor_tensor(tile, tile, aw[:, 2, :], ALU.add).then_inc(roped, 1)

            dve.sem_inc(a_free, 4)
            low_unit(*unit(0, 0, 0))
            dve.wait_ge(w_init, 32)
            for m in range(KT):
                low_x(m, G_F1, 0)
            for u in range(1, RING):
                low_unit(*unit(0, 0, u))
            ffn_in("f1i0", "f1o0", 0)
            ahead_all("f1o0", FT)
            add_b("f1o0", FT, 0.5, G_MIX, "sin")
            dve.memset(xraw[:, :, 0:3], 0.0)
            dve.memset(avec[32:64, :], 1.0)
            ahead("sin", 0, 0)
            row_factor("sin")
            t_, e_, m_, r_, s_, s2_, a_ = (zs[0:64, k, :] for k in range(7))
            n_dt = [0]

            def dt_step(ins):
                link(dve, dt_d_step, n_dt, ins)

            dve.wait_ge(unit_used, U0["sin"] + 1 + RING)
            dve.tensor_tensor(t_, bank[A0["sin"] % 4][0:64, 0:N], rstd[0:64, :], ALU.mult).then_inc(a_free, 1)
            dve.wait_ge(a_free, A0["sin"] + 1 + 4)
            dt_step(dve.tensor_scalar(t_, t_, vs[0:64, V_DTB:V_DTB + 1], None, ALU.add))
            dt_step(dve.scalar_tensor_tensor(out=e_, in0=t_, scalar=-1.0, in1=t_, op0=ALU.mult, op1=ALU.min))
            dt_step(dve.tensor_scalar(m_, t_, 0.0, None, ALU.max))
            dve.wait_ge(dt_a_step, 2)
            dt_step(dve.tensor_scalar(r_, e_, 2.0, None, ALU.add))
            dt_step(dve.reciprocal(r_, r_))
            dt_step(dve.tensor_tensor(s_, e_, r_, ALU.mult))
            dt_step(dve.tensor_tensor(s2_, s_, s_, ALU.mult))
            dt_step(dve.tensor_scalar(a_, s2_, 1.0 / 17, None, ALU.mult))
            for k in (15, 13, 11, 9, 7, 5, 3):
                dt_step(dve.scalar_tensor_tensor(out=a_, in0=a_, scalar=1.0 / k, in1=s2_, op0=ALU.add, op1=ALU.mult))
            dt_step(dve.scalar_tensor_tensor(out=a_, in0=a_, scalar=1.0, in1=s_, op0=ALU.add, op1=ALU.mult))
            dt_step(dve.scalar_tensor_tensor(out=a_, in0=a_, scalar=2.0, in1=m_, op0=ALU.mult, op1=ALU.add))
            link(dve, dve_step, steps, dve.tensor_scalar(avec[0:32, :], avec[0:32, :], -1.0, None, ALU.mult))
            dt_step(dve.tensor_scalar(dd, a_, avec[0:64, :], None, ALU.mult))
            assert n_dt[0] == DT_STEPS

            def conv_in(i, p, j):
                tile = i * 4 + p
                if not isinstance(i, int):
                    i_ = i - 1
                    dst = decraw[:, bass.ds(tile, 1), :].rearrange("p a n -> p (a n)")
                else:
                    i_ = 0
                    dst = decraw[:, tile, :]
                take(xraw[:, p, 3:259], "sin", j, i_, slice(0, T), signal=False).then_inc(conv_raw, 1)
                take(dst, "sin", j, i_, slice(T, N))

            def conv_taps(i, p):
                tile = p if i is None else i * 4 + p
                fixed = i is None or isinstance(i, int)
                xr = xraw[:, p % 4, :]
                out = xact[:, tile, 0:T] if fixed else xact[:, bass.ds(tile, 1), 0:T].rearrange("p a n -> p (a n)")
                tl = tail[:, tile, :] if fixed else tail[:, bass.ds(tile, 1), :].rearrange("p a n -> p (a n)")
                dve.wait_ge(conv_first, tile + 1)
                dve.tensor_copy(tl, xr[:, T:T + 3])
                for k in range(3):
                    w = vs[:, V_CW + CT * k + tile:V_CW + CT * k + tile + 1] if fixed else vs[:, bass.ds(tile + (V_CW + CT * k), 1)]
                    if k > 0:
                        dve.wait_ge(conv_sum, tile * 3 + k)
                    dve.scalar_tensor_tensor(out=out, in0=xr[:, k:k + T], scalar=w, in1=out, op0=ALU.mult, op1=ALU.add).then_inc(conv_sum, 1)

            def conv_body(i, j0):
                for p in range(4):
                    conv_in(i, p, j0 + p)
                    if p > 0 or not isinstance(i, int):
                        conv_taps(i, p - 1)
                    ahead("sin", *((0, j0 + p) if isinstance(i, int) else (i - 1, j0 + p)))

            conv_body(0, 1)
            with dve.Fori(1, CT // 4) as i:
                conv_body(i, 5)
            conv_taps(None, CT - 1)
            dve.wait_ge(pre_p, 1)
            for c in range(2):
                dve.tensor_copy(dtT[c], bank[4][:, 64 * c + 32:64 * c + 64])
                ins = dve.tensor_copy(da4[c].rearrange("p (k h) -> p k h", k=4), bank[4][:, 64 * c:64 * c + 32].unsqueeze(1).to_broadcast([P, 4, HEADS]))
            ins.then_inc(pre_d, 1)
            for k in (0, 32):
                ins = dve.tensor_tensor(dgl[k:k + 32], ident[k:k + 32, k:k + 32].unsqueeze(1).to_broadcast([32, SEQS, HEADS]),
                                        dd[k:k + 32, T:N].unsqueeze(2).to_broadcast([32, SEQS, HEADS]), ALU.mult)
            ins.then_inc(pre_d, 1)
            cw_ = lambda k: vs[:, V_CW + CT * k:V_CW + CT * k + CT].unsqueeze(2).to_broadcast([P, CT, SEQS])
            link(dve, dve_step, steps, dve.tensor_tensor(csum, decraw[:, :, :], cw_(3), ALU.mult))
            link(dve, dve_step, steps, dve.tensor_tensor(csum, csum, vs[:, V_CB:V_CB + CT].unsqueeze(2).to_broadcast([P, CT, SEQS]), ALU.add))
            for k in range(3):
                link(dve, dve_step, steps, dve.tensor_tensor(cwork, convs[:, :, k, :], cw_(k), ALU.mult))
                ins = dve.tensor_tensor(csum, csum, cwork, ALU.add)
                if k < 2:
                    link(dve, dve_step, steps, ins)
            ins.then_inc(dec_sum, 1)
            def z_take(s_):
                if s_ == 8:
                    dve.wait_ge(conv_out, 48)
                if s_ in Z_AT:
                    t = Z_AT.index(s_)
                    take(zs[:, t, :], "sin", 33 + t, banks=2)

            z_take(0)
            ahead("sin", 0, 33)
            dve.wait_ge(dec_act, 1)
            dve.tensor_copy(b_d[:, :, :], xact[:, 16:24, T:N])
            link(dve, dve_step, steps, dve.tensor_copy(c_d[:, :, :], xact[:, 24:32, T:N]))
            dve.tensor_tensor(bc_d[:, :, :], b_d[:, :, :], c_d[:, :, :], ALU.mult).then_inc(pre_d, 1)
            dve.wait_ge(pre_p, 2)
            cum_ps = bank[5][:, 0:128].rearrange("p (c k h) -> p c k h", c=2, k=2)
            dve.tensor_copy(tok[:, :, 0, :], cum_ps[:, :, 0, :])
            link(dve, dve_step, steps, dve.tensor_copy(tok[:, :, 2, :], cum_ps[:, :, 1, :]))
            dve.tensor_tensor(tok[:, :, 1, :], tok[:, :, 2, :], tok[:, :, 0, :], ALU.subtract).then_inc(pre_d, 1)
            dve.tensor_copy(ident_r, ident)
            dve.tensor_scalar(mask_r, tri, -1.0, 1e30, ALU.add, ALU.mult)
            dve.wait_ge(pre_a, 1)
            for k in (32, 96):
                ins = dve.tensor_tensor(cum4[k:k + 32], bank[2][k:k + 32, 0:256], cum4[k:k + 32].bitcast(F32), ALU.subtract)
            link(dve, dve_step, steps, ins)
            for c in range(2):
                R = diffR[c].rearrange("p (k l) -> p k l", k=4)
                ind = lambda n0, n1: cs[n0:n1, C_IND:C_IND + 4].unsqueeze(2).to_broadcast([n1 - n0, 4, P])
                cum_ = cum4[:, P * c:P * c + P].bitcast(F32)
                dve.tensor_tensor(R[0:64], cum_[0:64].unsqueeze(1).to_broadcast([64, 4, P]), ind(0, 64), ALU.mult)
                dve.tensor_copy(R[64:128], ind(64, 128))
                dve.tensor_copy(diffL[c][0:64], ones[0:64])
                ins = dve.tensor_scalar(diffL[c][64:128], cum_[64:128], -1.0, None, ALU.mult)
            ins.then_inc(pre_d, 1)
            z_take(1)
            ahead("sin", 0, 34)
            dve.wait_ge(pre_a, 2)
            dve.tensor_tensor(tok[:, :, 1, :], tok[:, :, 1, :], small[:, N:N + 64].rearrange("p (c h) -> p c h", c=2), ALU.mult).then_inc(tok_ready, 1)
            dve.wait_ge(pre_p, 3)
            for b in range(2):
                hs = slice(64 * b, 64 * b + 64)
                spread = lambda ps: ps[hs, 0:256].rearrange("p (s k b) -> p b k s", s=SEQS, b=2)[:, b]
                dve.tensor_copy(da_d[hs, :, :], spread(bank[6]))
                ins = dve.tensor_copy(dt_d[hs, :, :], spread(bank[7]))
            link(dve, dve_step, steps, ins)
            dve.tensor_tensor(dtx_d[:, :, :], xact[:, 0:16, T:N], dt_d[:, :, :], ALU.mult)
            dve.tensor_copy(bc_d[:, :, :], bank[3][:, 0:64])
            dve.tensor_copy(da_bc[:, :, :], bank[6][:, 0:256]).then_inc(pre_d, 1)

            def decode_y():
                dve.wait_ge(h0_used, 8)
                dve.wait_ge(pre_a, 3)
                link(dve, dve_step, steps, dve.tensor_tensor(t1d[:, :, :], bank[2][:, 0:128].rearrange("p (k s) -> p k s", k=XT), da_d[:, :, :], ALU.mult))
                link(dve, dve_step, steps, dve.tensor_tensor(dt_d[:, :, :].rearrange("p (g t) s -> p g t s", g=G), bc_d[:, :, :].unsqueeze(2).to_broadcast([P, G, 2, SEQS]),
                                                             dtx_d[:, :, :].rearrange("p (g t) s -> p g t s", g=G), ALU.mult))
                link(dve, dve_step, steps, dve.tensor_tensor(t1d[:, :, :], t1d[:, :, :], dt_d[:, :, :], ALU.add))
                xd = xact[:, 0:XT, T:N]
                link(dve, dve_step, steps, dve.tensor_tensor(xd, xd, vs[:, V_D:V_D + XT].unsqueeze(2).to_broadcast([P, XT, SEQS]), ALU.mult))
                dve.tensor_tensor(xd, xd, t1d[:, :, :], ALU.add)

            def by_head(a):
                return a.rearrange("p (h w) -> p h w", h=4)

            def heads(a):
                return a.unsqueeze(2).to_broadcast([P, 4, 64])

            def chunk_in(k):
                g, c = k // 2, k % 2
                dve.wait_ge(ssd_in, k + 1)
                if k == 0:
                    dve.wait_ge(tok_ready, 1)
                if k >= 2:
                    dve.wait_ge(ssd_part, k - 1)
                dve.tensor_copy(cbb[k % 2], bank[4][:, 0:256])
                dve.tensor_tensor(by_head(xdt[k % 2]), by_head(bank[4][:, 256:512]), heads(dtT[c][:, 4 * g:4 * g + 4]), ALU.mult)
                dve.tensor_tensor(by_head(xte[k % 2]), by_head(bank[4][:, 256:512]), heads(tok[:, c, 1, 4 * g:4 * g + 4]), ALU.mult).then_inc(ssd_read, 1)

            def carry(k):
                g, c = k // 2, k % 2
                dve.wait_ge(ssd_part, k + 1)
                if c == 0:
                    dve.tensor_copy(h1, bank[3][:, 0:256]).then_inc(ssd_carry, 1)
                    return
                if g > 0:
                    dve.wait_ge(ssd_tr, g)
                dve.tensor_tensor(by_head(isc), by_head(bank[3][:, 256:512]), heads(tok[:, 1, 0, 4 * g:4 * g + 4]), ALU.mult).then_inc(ssd_isc, 1)
                link(dve, dve_step, steps, dve.tensor_tensor(by_head(h1), by_head(h1), heads(tok[:, 1, 2, 4 * g:4 * g + 4]), ALU.mult))
                if g >= 2:
                    dve.wait_ge(st_out[g % 2], 16 * (g // 2))
                dve.tensor_tensor(state[:, g % 2, :], h1, bank[3][:, 0:256], ALU.add).then_inc(ssd_carry, 1)

            def decay(k):
                dve.wait_ge(ssd_exp, k + 1)
                dve.wait_ge(ssd_read, k + 1)
                dve.tensor_tensor(by_head(Dm[k % 2]), by_head(Dm[k % 2]), cbb[k % 2][:, 0:128].unsqueeze(1).to_broadcast([P, 4, P]), ALU.mult).then_inc(ssd_mm, 1)

            def finish(g):
                dve.wait_ge(ssd_tr, g + 1)
                for n_ in range(2):
                    xt_ = xact[:, 2 * g + n_, 0:T]
                    ins = dve.scalar_tensor_tensor(out=xt_, in0=xt_, scalar=vs[:, V_D + 2 * g + n_:V_D + 2 * g + n_ + 1],
                                                   in1=bank[6 + g % 2][:, 256 * n_:256 * n_ + 256], op0=ALU.mult, op1=ALU.add)
                ins.then_inc(ssd_y, 1)

            def low_z(t):
                dve.wait_ge(hh_ready, HREADY["sout"] + t + 1)
                dve.tensor_tensor(hl[:, t, :], zs[:, t, :], hh[:, t, :].bitcast(F32), ALU.subtract).then_inc(hl_ready, 1)

            for s_ in range(2, SLOTS):
                z_take(s_)
                if s_ == H0_AT + SEQS:
                    decode_y()
                if s_ in NORM_AT:
                    g = NORM_AT.index(s_)
                    dve.wait_ge(z_silu, 1 + (g > 3) + (g > 5))
                    dve.wait_ge(ssd_y, g + 1)
                    dve.tensor_tensor(zs[:, 2 * g:2 * g + 2, :], zs[:, 2 * g:2 * g + 2, :], xact[:, 2 * g:2 * g + 2, :], ALU.mult).then_inc(gated, 1)
                k = s_ - CHUNK0
                if 0 <= k < 2 * G:
                    chunk_in(k)
                if 0 <= k - 3 < 2 * G and k % 2 == 1:
                    finish((k - 3) // 2)
                if 0 <= k < 2 * G:
                    decay(k)
                if 0 <= k - 1 < 2 * G:
                    carry(k - 1)
                if s_ in Z_AT:
                    ahead("sin", 0, 33 + Z_AT.index(s_))
                if s_ in APPLY_AT:
                    g = APPLY_AT.index(s_)
                    dve.wait_ge(gated_std, [g >= g0 for g0, _ in ROOT_AFTER.values()].count(True))
                    link(dve, dve_step, steps, dve.reciprocal(xact[:, 2 * g, :], xact[:, 2 * g, :]))
                    for t in (2 * g, 2 * g + 1):
                        dve.scalar_tensor_tensor(out=zs[:, t, :], in0=zs[:, t, :], scalar=vs[:, V_NG + t:V_NG + t + 1],
                                                 in1=xact[:, 2 * g, :], op0=ALU.mult, op1=ALU.mult).then_inc(gn_ready, 1)
                    low_z(2 * g)
                    low_z(2 * g + 1)
                if s_ == SLOTS - 2:
                    dve.wait_ge(dtx_tr, 1)
                    for n_ in range(4):
                        ins = dve.tensor_copy(dtxt[:, 512 * n_:512 * n_ + 512], bank[3 + n_][0:SEQS, :])
                    ins.then_inc(dtx_row, 1)
            ahead_all("sout", XT)
            add_b("sout", XT, 1.0, G_F2, "f2i0")
            ffn_in("f2i0", "f2o0", 1, lambda: low_p(0))
            embed("pp0", 0)
            ahead_all("f2o0", FT)
            add_b("f2o0", FT, 0.5, G_PLE, "pg0")
            gates("pg0", 0, G_F1 + 8)
            ffn_in("f1i1", "f1o1", 2, lambda: [low_kv(m) for m in range(KT)])
            for j in range(4):
                take((kf if j < 2 else vf)[:, j % 2, :], "kv", j)
                ahead("kv", 0, j)
            ahead_all("f1o1", FT)
            add_b("f1o1", FT, 0.5, G_MIX + 8, "q")
            for t in range(HEAD_TILES + 6):
                if t == 1:
                    row_factor("q")
                    take(qf[:, 0, :], "q", 0)
                    take(qf[:, 1, :], "q", 1)
                    dve.wait_ge(v_tr, 1)
                    dve.tensor_copy(vtok, bank[7][:, :].rearrange("p (c n) -> p c n", c=2)).then_inc(v_tok, 1)
                if 2 <= t < KT:
                    take(qf[:, t, :], "q", t)
                if 0 <= t - 5 < HEAD_TILES:
                    head_norm(t - 5, kf[:, t - 5, :] if t < 7 else qf[:, t - 7, :], V_KN if t < 7 else V_QN)
                if 0 <= t - 6:
                    rope(t - 6, kf[:, t - 6, :] if t < 8 else qf[:, t - 8, :])
                if t < KT:
                    ahead("q", 0, t)
                if t == HEAD_BATCH - 1:
                    head_inverse(0)
                if t == HEAD_TILES - 1:
                    head_inverse(1)
            def decode_step(n_):
                dve.wait_ge(dec_p, n_)
                if n_ == 1:
                    dve.tensor_copy(sTd[:, 0:64], bank[0][:, 0:64])
                    dve.tensor_copy(sTd[:, 64:128], bank[1][:, 0:64]).then_inc(dec_d, 1)
                    dve.tensor_tensor(prod.rearrange("p (a b) -> p a b", a=2)[:, 0, :].rearrange("p (s k i) -> p s k i", s=SEQS, k=2),
                                      qf[:, :, T:N].rearrange("p (k i) s -> p s k i", k=2),
                                      kf[:, :, T:N].rearrange("p k s -> p s k").unsqueeze(3).to_broadcast([P, SEQS, 2, 4]), ALU.mult).then_inc(dec_d, 1)
                elif n_ == 2:
                    dve.tensor_scalar(dS[:, 0:128], bank[0][:, 128:256], SCALE, None, ALU.mult)
                    dve.tensor_scalar(dS[0:64, 128:129], bank[0][0:64, 256:257], SCALE, None, ALU.mult)
                    link(dve, dve_step, steps, dve.tensor_scalar(dS[64:128, 128:129], bank[1][64:128, 256:257], SCALE, None, ALU.mult))
                    link(dve, dve_step, steps, dve.tensor_reduce(dm[:, 0:1], dS, AX.X, ALU.max))
                    link(dve, dve_step, steps, dve.tensor_scalar(dm[:, 0:1], dm[:, 0:1], vs[:, V_SINKD:V_SINKD + 1], None, ALU.max))
                    dve.tensor_scalar(dm[:, 1:2], dm[:, 0:1], -1.0, None, ALU.mult).then_inc(dec_a_go, 1)
                elif n_ == 3:
                    dve.tensor_copy(pTd, bank[0][:, 128:256]).then_inc(dec_d, 1)
                else:
                    for b in range(2):
                        hs = slice(64 * b, 64 * b + 64)
                        od3 = od[hs, :].rearrange("p (s k i) -> p s k i", s=SEQS, k=2)
                        link(dve, dve_step, steps, dve.tensor_tensor(od3, bank[1][hs, 128 + 64 * b:192 + 64 * b].rearrange("p (s k i) -> p s k i", s=SEQS, k=2),
                                                                     vf[hs, :, T:N].rearrange("p k s -> p s k").unsqueeze(3).to_broadcast([64, SEQS, 2, 4]), ALU.mult))
                        ins = dve.tensor_tensor(o32[hs].rearrange("p (k i) s -> p s k i", k=2), od3,
                                                bank[0][hs, 0:64].rearrange("p (s k i) -> p s k i", s=SEQS, k=2), ALU.add)
                    ins.then_inc(dec_d, 1)

            def decode_prob():
                dve.wait_ge(dec_a, 1)
                link(dve, dve_step, steps, dve.tensor_tensor(dm[:, 4:5], dm[:, 2:3], dm[:, 3:4], ALU.add))
                link(dve, dve_step, steps, dve.reciprocal(dm[:, 4:5], dm[:, 4:5]))
                link(dve, dve_step, steps, dve.tensor_scalar(dP, dP, dm[:, 4:5], None, ALU.mult))
                dve.tensor_scalar(dgP, ident, dP[:, 128:129], None, ALU.mult).then_inc(dec_d, 1)

            def maxima(e):
                b = e % 3
                dve.wait_ge(s_done, e + 1)
                if e >= 3:
                    dve.wait_ge(p_tr, e - 2)
                dve.scalar_tensor_tensor(out=sm[b], in0=bank[4 + e % 2][:, 0:384], scalar=SCALE, in1=mask, op0=ALU.mult, op1=ALU.add).then_inc(s_masked, 1)
                dve.wait_ge(s_masked, e + 1)
                dve.tensor_reduce(mx[b][:, 0:1], sm[b][:, 0:128], AX.X, ALU.max)
                link(dve, dve_step, steps, dve.tensor_reduce(mx[b][:, 1:2], sm[b][:, 128:384], AX.X, ALU.max))
                dve.tensor_scalar(nmx[b], mx[b], -1.0, nsink[:, e:e + 1], ALU.mult, ALU.min).then_inc(s_max, 1)

            def probabilities(e):
                b = e % 3
                dve.wait_ge(s_exp, e + 1)
                link(dve, dve_step, steps, dve.tensor_tensor(rr[b], rs[b], es[b], ALU.add))
                link(dve, dve_step, steps, dve.reciprocal(rr[b], rr[b]))
                dve.tensor_scalar(sm[b][:, 0:128], sm[b][:, 0:128], rr[b][:, 0:1], None, ALU.mult)
                dve.tensor_scalar(sm[b][:, 128:384], sm[b][:, 128:384], rr[b][:, 1:2], None, ALU.mult).then_inc(s_prob, 1)

            link(dve, dve_step, steps, dve.tensor_scalar(nsink, vs[:, V_SINK:V_SINK + AH], -1.0, None, ALU.mult))
            for e in range(AH + 5):
                if e < AH:
                    maxima(e)
                if 0 <= e - 1 < AH:
                    probabilities(e - 1)
                if e == 4:
                    decode_step(1)
                if e == 6:
                    decode_step(2)
                if e == 8:
                    decode_prob()
                if e == 9:
                    decode_step(3)
                if e == 14:
                    decode_step(4)
                if e == 16:
                    dve.wait_ge(dec_o, 1)
                    dve.tensor_tensor(hl[:, 0:KT, T:N], o32, hh[:, 0:KT, T:N].bitcast(F32), ALU.subtract).then_inc(dec_l, 1)
                if e >= 6 and e % 2 == 0:
                    t = (e - 6) // 2
                    dve.wait_ge(hh_ready, HREADY["o"] + t + 1)
                    dve.tensor_tensor(hl[:, t, 0:T], bank[2 + t % 2][:, 0:T], hh[:, t, 0:T].bitcast(F32), ALU.subtract).then_inc(hl_ready, 1)
            ahead_all("o", 8)
            add_b("o", 8, 1.0, G_F2 + 8, "f2i1")
            ffn_in("f2i1", "f2o1", 3, lambda: low_p(1))
            embed("pp1", 1)
            ahead_all("f2o1", FT)
            add_b("f2o1", FT, 0.5, G_PLE + 8, "pg1")
            gates("pg1", 1, None)

        @block.gpsimd
        def _(pool):
            steps = [0]
            def add_squares(stage):
                n = 4 * POOLED.index(stage)
                first = 8 * NORM[stage]
                two = lambda t: sq[:, N * t:N * t + 2 * N]
                pool.wait_ge(sq_ready, first + 4)
                pool.tensor_tensor(two(0), two(0), two(2), ALU.add).then_inc(sq_pair, 1)
                pool.wait_ge(sq_ready, first + 8)
                pool.tensor_tensor(two(4), two(4), two(6), ALU.add).then_inc(sq_pair, 1)
                pool.wait_ge(sq_pair, n + 2)
                pool.tensor_tensor(two(0), two(0), two(4), ALU.add).then_inc(sq_pair, 1)
                pool.wait_ge(sq_pair, n + 3)
                pool.tensor_tensor(sq3[:, 0, :], sq3[:, 0, :], sq3[:, 1, :], ALU.add).then_inc(sq_pair, 1)

            add_squares("f1i0")
            pool.dma_start(k_old, ck).then_inc(old_out, 16)
            pool.dma_start(v_old, cv).then_inc(old_out, 16)
            add_squares("sin")
            pool.wait_ge(sums_done, 2)
            for q in range(4):
                pool.dma_start(h0buf[q], ssm0[q]).then_inc(h0_landed[q], 16)
            pool.wait_ge(dec_sum, 1)
            pool.wait_ge(conv_sum, 3 * CT)
            pool.dma_start(conv_p, tail[:, :, :]).then_inc(conv_out, 16)
            pool.dma_start(conv_s[:, :, 0:2, :], convs[:, :, 1:3, :]).then_inc(conv_out, 16)
            pool.dma_start(conv_s[:, :, 2, :], decraw[:, :, :]).then_inc(conv_out, 16)
            for q in range(4, SEQS):
                pool.wait_ge(h0_used, q - 3)
                pool.dma_start(h0buf[q % 4], ssm0[q]).then_inc(h0_landed[q % 4], 16)
            for g in range(G):
                pool.wait_ge(ssd_carry, 2 * g + 2)
                pool.dma_start(ssm_p[:, 256 * g:256 * g + 256], state[:, g % 2, :]).then_inc(st_out[g % 2], 16)
            pool.wait_ge(dtx_row, 1)
            pool.dma_start(dtx_rows, dtxt).then_inc(dtx_out, 16)
            pool.wait_ge(dtx_out, 16)
            pool.wait_ge(pre_a, 3)
            pool.wait_ge(ssd_y, G)
            for q in range(SEQS):
                if q > 0:
                    pool.wait_ge(late_out, 16 * q)
                pool.dma_start(lateA, ssm0[q]).then_inc(late_in[0], 16)
                pool.dma_start(lateB, dtx_rows[q:q + 1, :].to_broadcast([P, XT * P])).then_inc(late_in[1], 16)
                pool.wait_ge(late_in[0], 16 * (q + 1))
                pool.tensor_tensor(lateA.rearrange("p (h w) -> p h w", h=HEADS), lateA.rearrange("p (h w) -> p h w", h=HEADS),
                                   da_bc[:, q, :].unsqueeze(2).to_broadcast([P, HEADS, 64]), ALU.mult)
                pool.wait_ge(late_in[1], 16 * (q + 1))
                link(pool, pool_step, steps, pool.tensor_tensor(lateB.rearrange("p (g w) -> p g w", g=G), lateB.rearrange("p (g w) -> p g w", g=G),
                                                                b_d[:, :, q].unsqueeze(2).to_broadcast([P, G, 256]), ALU.mult))
                link(pool, pool_step, steps, pool.tensor_tensor(lateA, lateA, lateB, ALU.add))
                pool.dma_start(ssm_s[q], lateA).then_inc(late_out, 16)
            pool.wait_ge(late_out, 16 * SEQS)
            pool.wait_ge(gn_ready, XT)
            pool.dma_start(kc, kcT).then_inc(cache_in, 16)
            pool.dma_start(vc, vc_in).then_inc(cache_in, 16)
            add_squares("pg0")
            add_squares("f1i1")
            add_squares("q")
            pool.wait_ge(roped, 2)
            pool.wait_ge(v_tok, 1)
            pool.dma_start(kv_p[0], kf[:, :, 128:256]).then_inc(kv_out, 16)
            pool.dma_start(kv_p[1], vf[:, :, 128:256]).then_inc(kv_out, 16)
            pool.dma_start(kv_new[0], kf[:, :, T:N]).then_inc(kv_out, 16)
            pool.dma_start(kv_new[1], vf[:, :, T:N]).then_inc(kv_out, 16)
            add_squares("f2i1")
            add_squares("pg1")
            pool.wait_ge(kv_out, 64)
            pool.wait_ge(old_out, 32)
            pool.wait_ge(conv_out, 48)
            for b in range(2):
                pool.wait_ge(st_out[b], 16 * G // 2)


def in_a(w):
    m = w.shape[1] // P
    return w.reshape(KT, P, m, P).transpose(2, 1, 0, 3).reshape(m, P, UNIT)


def ffn_units(wi):
    return in_a(wi).reshape(2, FT, P, UNIT).transpose(1, 0, 2, 3).reshape(2 * FT, P, UNIT)


def in_b(w):
    return w.reshape(-1, P, UNIT)


def proj_units(w):
    return w.reshape(2, P, 2, 4, P).transpose(2, 1, 3, 0, 4).reshape(2, P, UNIT)


def columns(v):
    return v.reshape(-1, P).T


def constants():
    c = np.zeros((P, NC_), np.float32)
    k, m = np.arange(P)[:, None], np.arange(P)[None, :]
    c[:, C_ID:C_ID + P] = k == m
    c[:, C_TRI:C_TRI + P] = k <= m
    c[:, C_ONE:C_ONE + P] = 1
    c[:, C_BLK:C_BLK + P] = k // 64 == m // 64
    c[:, C_ROT:C_ROT + P] = 1.0 * ((k == m - 32) & (m % 64 >= 32)) - 1.0 * ((k == m + 32) & (m % 64 < 32))
    pos = np.concatenate([np.arange(T), np.full(SEQS, 1024)]).astype(np.float32)
    inv = np.float32(10000.0) ** (-np.arange(32, dtype=np.float32) / np.float32(32))
    ang = (pos[None, :] * inv[:, None]).astype(np.float32)[np.arange(P) % 32]
    c[:, C_COS:C_COS + N] = np.cos(ang)
    c[:, C_SIN:C_SIN + N] = np.sin(ang)
    far = np.float32(-1e30)
    c[:, C_MASK:C_MASK + 128] = np.where(m <= k, 0, far)
    c[:, C_MASK + 128:C_MASK + 256] = np.where(m >= k, 0, far)
    c[:, C_MASK + 256:C_MASK + 384] = np.where(m <= k, 0, far)
    c[:, C_IND:C_IND + 4] = k % 4 == np.arange(4)[None, :]
    c[:, C_SEL:C_SEL + G] = k % HEADS // 4 == np.arange(G)[None, :]
    c[:, C_EPS] = EPS
    c[:, C_WIN:C_WIN + 38] = np.arange(38)[None, :] == 18 + k // 64
    return c


def kernel(**inputs):
    import concourse.bacc as bacc
    from concourse.bass_utils import run_bass_kernel_spmd

    a = {k: np.asarray(v) for k, v in inputs.items()}
    perm = [(2 * (t // 4) + b) * 4 + t % 4 for t in range(KT) for b in range(2)]
    ssm_in = a["ssm_in"][0]
    weights = np.concatenate([
        ffn_units(a["ffn1_wi"][0]), in_b(a["ffn1_wo"][0]),
        in_a(np.tile(ssm_in[:, 6144:6176], (1, 4))), in_a(ssm_in[:, 2048:6144]), in_a(ssm_in[:, 0:2048]),
        in_b(a["ssm_out"][0]),
        ffn_units(a["ffn2_wi"][0]), proj_units(a["ple_proj"][0]), in_b(a["ffn2_wo"][0]), in_a(a["ple_gate"][0]),
        ffn_units(a["ffn1_wi"][1]), in_a(a["w_kv"]), in_b(a["ffn1_wo"][1]),
        in_a(a["w_q"][0].reshape(D, AH, 64)[:, perm].reshape(D, D)), in_b(a["w_o"][0].reshape(AH, 64, D)[perm].reshape(D, D)),
        ffn_units(a["ffn2_wi"][1]), proj_units(a["ple_proj"][1]), in_b(a["ffn2_wo"][1]), in_a(a["ple_gate"][1]),
    ])
    assert weights.shape == (NU, P, UNIT)
    rows = lambda p, s: np.concatenate([p, s])
    fm = lambda r: r.T.reshape(-1, P, r.shape[0]).transpose(1, 0, 2)
    xT = fm(rows(a["x_prompt"][0], a["x_sample"][:, 0]))
    pT = np.stack([fm(rows(a["p_prompt"][l, 0], a["p_sample"][l, :, 0])) for l in range(2)])
    v = [columns(a[n][l]) for n in ("ffn1_norm", "mix_norm", "ffn2_norm", "ple_norm") for l in range(2)] + [columns(a["kv_norm"])]
    v += [columns(a["ssm_conv_w"][0, k]) for k in range(4)] + [columns(a["ssm_conv_b"][0])]
    v += [columns(np.repeat(a["ssm_d"][0], 64)), columns(a["ssm_norm"][0])]
    v += [np.tile(a["ssm_a_log"][0], 4)[:, None], np.tile(a["ssm_dt_bias"][0], 4)[:, None]]
    v += [np.tile(a["k_norm"], 2)[:, None], np.tile(a["q_norm"][0], 2)[:, None]]
    sinks = a["attn_sinks"][0]
    v += [sinks[[(2 * kp + b) * 4 + i for b in range(2) for _ in range(SEQS) for kp in range(2) for i in range(4)]][:, None]]
    v += [np.broadcast_to(sinks[perm][None, :], (P, AH))]
    vec = np.concatenate(v, axis=1)
    assert vec.shape == (P, NV)
    convst = a["state_conv"][0].reshape(SEQS, 3, CT, P).transpose(3, 2, 1, 0)
    ssm0 = a["state_ssm"][0].transpose(0, 3, 1, 2).reshape(SEQS, P, XT * P)
    ck = a["cache_k"].reshape(SEQS, WINDOW, 256)
    cv = a["cache_v"].reshape(SEQS, WINDOW, 256)
    kcT = a["cache_k"].reshape(SEQS, WINDOW, 2, 2, 64).transpose(3, 4, 2, 0, 1).reshape(P, 2, SEQS, WINDOW)
    vcT = cv.transpose(1, 0, 2)

    nc = bacc.Bacc("TRN2", target_bir_lowering=False, num_devices=1)
    arrays = {"weights": weights, "xT": xT, "pT": pT, "cst": constants(), "vec": vec, "convst": convst, "ssm0": ssm0,
              "kcT": kcT, "vcT": vcT, "ck": ck, "cv": cv}
    arrays = {k: np.ascontiguousarray(v_) for k, v_ in arrays.items()}
    ins = {k: nc.dram_tensor(k, v_.shape, mybir.dt.from_np(v_.dtype), kind="ExternalInput").ap() for k, v_ in arrays.items()}
    shapes = {"y": (P, KT, N), "ssm_p": (P, 2048), "conv_p": (P, CT, 3), "kv_p": (2, P, 2, 128), "ssm_s": (SEQS, P, 2048),
              "conv_s": (P, CT, 3, SEQS), "k_old": (SEQS, WINDOW - 1, 256), "v_old": (SEQS, WINDOW - 1, 256), "kv_new": (2, P, 2, SEQS)}
    outs = {k: nc.dram_tensor("out_" + k, s, F32, kind="ExternalOutput").ap() for k, s in shapes.items()}
    i = ins
    trunk_kernel(nc, i["weights"], i["xT"], i["pT"], i["cst"], i["vec"], i["convst"], i["ssm0"], i["kcT"], i["vcT"],
                 i["ck"][:, 1:, :], i["cv"][:, 1:, :], *outs.values())
    r = run_bass_kernel_spmd(nc, [arrays], core_ids=[0]).results[0]
    o = {k: np.asarray(r["out_" + k]) for k in shapes}

    y = o["y"].transpose(2, 1, 0).reshape(N, D)
    ssm_p = o["ssm_p"].reshape(P, HEADS, 64).transpose(1, 2, 0)[None, None]
    conv_p = o["conv_p"].transpose(2, 1, 0).reshape(1, 1, 3, CT * P)
    heads = lambda t: t.reshape(2, 64, 2, -1).transpose(3, 2, 0, 1).reshape(-1, 4, 64)
    k_p, v_p = heads(o["kv_p"][0])[None], heads(o["kv_p"][1])[None]
    ssm_s = o["ssm_s"].reshape(SEQS, P, HEADS, 64).transpose(0, 2, 3, 1)[None]
    conv_s = o["conv_s"].transpose(3, 2, 1, 0).reshape(1, SEQS, 3, CT * P)
    k_s, v_s = (np.concatenate([o[n].reshape(SEQS, WINDOW - 1, 4, 64), heads(o["kv_new"][j])[:, None]], axis=1)
                for j, n in enumerate(("k_old", "v_old")))
    return (y[None, :T], y[T:][:, None], ssm_p, conv_p, k_p, v_p, ssm_s, conv_s, k_s, v_s)
```
